# Optimizing a Trainium2 kernel written in Bass

```python
import jax, jax.numpy as jnp
from jax import lax
import numpy as np
import math

D_MODEL = 1024
BATCH = 1
SEQ = 256
DEPTH = 2

N_EVEN = (DEPTH + 1) // 2
N_ODD = DEPTH // 2
BLOCK = 128
D_FF = 2816
EPS = 1e-6
SB_HEADS = 8
SB_HEAD_DIM = 64
SB_WIDTH = SB_HEADS * SB_HEAD_DIM
SG_GROUPS = 8
SG_GROUP_DIM = 64
SG_WIDTH = SG_GROUPS * SG_GROUP_DIM
SG_CHUNK = 128
EVEN_IN = 3 * SB_WIDTH + 2 * SG_WIDTH
EVEN_MIX = SB_WIDTH + SG_WIDTH
MLA_HEADS = 16
MLA_NOPE = 64
MLA_ROPE = 32
MLA_QK = MLA_NOPE + MLA_ROPE
MLA_V = 64
MLA_Q_LORA = 512
MLA_KV_LORA = 256
MLA_IN = MLA_Q_LORA + MLA_KV_LORA + MLA_ROPE
MLA_MIX = MLA_HEADS * MLA_V
ROPE_THETA = 10000.0
MEM_TOKENS = 256
MEM_HEADS = 4
MEM_HEAD_DIM = D_MODEL // MEM_HEADS


def _rmsnorm(x, g):
    xf = x.astype(jnp.float32)
    y = xf * lax.rsqrt(jnp.mean(xf * xf, axis=-1, keepdims=True) + EPS)
    return (y * g.astype(jnp.float32)).astype(x.dtype)

def _layernorm(x, g, b):
    xf = x.astype(jnp.float32)
    mu = jnp.mean(xf, axis=-1, keepdims=True)
    var = jnp.mean(jnp.square(xf - mu), axis=-1, keepdims=True)
    y = (xf - mu) * lax.rsqrt(var + EPS)
    return (y * g.astype(jnp.float32) + b.astype(jnp.float32)).astype(x.dtype)

def _swiglu(h, w_gu, w_down):
    gate, up = jnp.split(h @ w_gu, 2, axis=-1)
    return (jax.nn.silu(gate) * up) @ w_down

def _to_blocks(t):
    b, s, h, d = t.shape
    return t.reshape(b, s // BLOCK, BLOCK, h, d).transpose(1, 0, 2, 3, 4)

def _from_blocks(t):
    nb, b, l, h, d = t.shape
    return t.transpose(1, 0, 2, 3, 4).reshape(b, nb * l, h, d)

def _rope(t, positions):
    half = t.shape[-1] // 2
    inv_freq = ROPE_THETA ** (-jnp.arange(half, dtype=jnp.float32) / half)
    ang = positions.astype(jnp.float32)[:, :, None, None] * inv_freq
    cos, sin = jnp.cos(ang), jnp.sin(ang)
    tf = t.astype(jnp.float32)
    t1, t2 = tf[..., :half], tf[..., half:]
    return jnp.concatenate([t1 * cos - t2 * sin, t1 * sin + t2 * cos], axis=-1).astype(t.dtype)

def _stick_breaking_attention(q, k, v):
    s_len = q.shape[1]
    scale = SB_HEAD_DIM ** -0.5
    k_pos = jnp.arange(s_len)

    def block(args):
        q_blk, i = args
        z = jnp.einsum('bqhd,bkhd->bhqk', q_blk, k).astype(jnp.float32) * scale
        q_pos = i * BLOCK + jnp.arange(BLOCK)
        strict = (k_pos[None, :] < q_pos[:, None])[None, None]
        log_stay = jnp.where(strict, jax.nn.log_sigmoid(-z), 0.0)
        log_rest = lax.cumsum(log_stay, axis=3, reverse=True) - log_stay
        w = jnp.where(strict, jnp.exp(jax.nn.log_sigmoid(z) + log_rest), 0.0)
        return jnp.einsum('bhqk,bkhd->bqhd', w.astype(v.dtype), v)

    out = lax.map(block, (_to_blocks(q), jnp.arange(s_len // BLOCK)))
    return _from_blocks(out)

def _causal_softmax_attention(q, k, v):
    s_len = q.shape[1]
    scale = q.shape[-1] ** -0.5
    k_pos = jnp.arange(s_len)

    def block(args):
        q_blk, i = args
        sc = jnp.einsum('bqhd,bkhd->bhqk', q_blk, k).astype(jnp.float32) * scale
        q_pos = i * BLOCK + jnp.arange(BLOCK)
        causal = (k_pos[None, :] <= q_pos[:, None])[None, None]
        p = jax.nn.softmax(jnp.where(causal, sc, -jnp.inf), axis=-1)
        return jnp.einsum('bhqk,bkhd->bqhd', p.astype(v.dtype), v)

    out = lax.map(block, (_to_blocks(q), jnp.arange(s_len // BLOCK)))
    return _from_blocks(out)

def _even_mixer(h, w_in, ln_g, ln_b, sgu_w, sgu_b, w_out):
    b, s, _ = h.shape
    q, k, v, z = jnp.split(h @ w_in, [SB_WIDTH, 2 * SB_WIDTH, 3 * SB_WIDTH], axis=-1)
    heads = lambda t: t.reshape(b, s, SB_HEADS, SB_HEAD_DIM)
    o_sb = _stick_breaking_attention(heads(q), heads(k), heads(v)).reshape(b, s, SB_WIDTH)
    u, g = jnp.split(jax.nn.gelu(z), 2, axis=-1)
    g = _layernorm(g, ln_g, ln_b).reshape(b, s // SG_CHUNK, SG_CHUNK, SG_GROUPS, SG_GROUP_DIM)
    tri = jnp.tril(jnp.ones((SG_CHUNK, SG_CHUNK), dtype=sgu_w.dtype))
    mixed = jnp.einsum('gts,bcsgd->bctgd', sgu_w * tri, g) + sgu_b.T[None, None, :, :, None]
    o_sg = u * mixed.reshape(b, s, SG_WIDTH)
    return jnp.concatenate([o_sb, o_sg], axis=-1) @ w_out

def _mla_mixer(h, positions, w_in, q_lora_g, kv_lora_g, w_uq, w_ukv, q_g, k_g, w_out):
    b, s, _ = h.shape
    c_q, c_kv, k_r = jnp.split(h @ w_in, [MLA_Q_LORA, MLA_Q_LORA + MLA_KV_LORA], axis=-1)
    q = (_rmsnorm(c_q, q_lora_g) @ w_uq).reshape(b, s, MLA_HEADS, MLA_QK)
    kv = (_rmsnorm(c_kv, kv_lora_g) @ w_ukv).reshape(b, s, MLA_HEADS, MLA_NOPE + MLA_V)
    k_nope, v = kv[..., :MLA_NOPE], kv[..., MLA_NOPE:]
    k_r = jnp.broadcast_to(k_r[:, :, None, :], (b, s, MLA_HEADS, MLA_ROPE))
    k = jnp.concatenate([k_nope, k_r], axis=-1)
    q = _rmsnorm(q, q_g)
    k = _rmsnorm(k, k_g)
    q = jnp.concatenate([q[..., :MLA_NOPE], _rope(q[..., MLA_NOPE:], positions)], axis=-1)
    k = jnp.concatenate([k[..., :MLA_NOPE], _rope(k[..., MLA_NOPE:], positions)], axis=-1)
    o = _causal_softmax_attention(q, k, v).reshape(b, s, MLA_MIX)
    return o @ w_out

def _memory_cross_attention(hq, hm, wq, wkv, q_g, k_g, wo):
    b, s, _ = hq.shape
    m = hm.shape[1]
    q = _rmsnorm((hq @ wq).reshape(b, s, MEM_HEADS, MEM_HEAD_DIM), q_g)
    k, v = jnp.split((hm @ wkv).reshape(b, m, MEM_HEADS, 2 * MEM_HEAD_DIM), 2, axis=-1)
    k = _rmsnorm(k, k_g)
    sc = jnp.einsum('bqhd,bmhd->bhqm', q, k).astype(jnp.float32) * (MEM_HEAD_DIM ** -0.5)
    p = jax.nn.softmax(sc, axis=-1)
    o = jnp.einsum('bhqm,bmhd->bqhd', p.astype(v.dtype), v).reshape(b, s, D_MODEL)
    return o @ wo

def _w(k, shape, fan_in):
    return jax.random.normal(k, shape, jnp.float32) * (fan_in ** -0.5)

def _gain(k, shape):
    return 1.0 + 0.02 * jax.random.normal(k, shape, jnp.float32)

def first_inputs(seed: int = 0) -> dict:
    key = jax.random.key(seed)
    ks = list(jax.random.split(key, 32))
    nk = ks.pop
    inp = {}
    inp['x'] = jax.random.normal(nk(), (BATCH, SEQ, D_MODEL), jnp.float32)
    inp['mem'] = jax.random.normal(nk(), (BATCH, MEM_TOKENS, D_MODEL), jnp.float32)
    inp['positions'] = jnp.broadcast_to(jnp.arange(SEQ, dtype=jnp.int32)[None, :], (BATCH, SEQ))
    inp['ffn_pre_norm'] = _gain(nk(), (DEPTH, D_MODEL))
    inp['ffn_pre_w_gu'] = _w(nk(), (DEPTH, D_MODEL, 2 * D_FF), D_MODEL)
    inp['ffn_pre_w_down'] = _w(nk(), (DEPTH, D_FF, D_MODEL), D_FF)
    inp['mix_norm'] = _gain(nk(), (DEPTH, D_MODEL))
    inp['sbg_w_in'] = _w(nk(), (N_EVEN, D_MODEL, EVEN_IN), D_MODEL)
    inp['sgu_ln_gain'] = _gain(nk(), (N_EVEN, SG_WIDTH))
    inp['sgu_ln_bias'] = 0.02 * jax.random.normal(nk(), (N_EVEN, SG_WIDTH), jnp.float32)
    inp['sgu_w'] = _w(nk(), (N_EVEN, SG_GROUPS, SG_CHUNK, SG_CHUNK), SG_CHUNK)
    inp['sgu_b'] = 1.0 + 0.1 * jax.random.normal(nk(), (N_EVEN, SG_GROUPS, SG_CHUNK), jnp.float32)
    inp['sbg_w_out'] = _w(nk(), (N_EVEN, EVEN_MIX, D_MODEL), EVEN_MIX)
    inp['mla_w_in'] = _w(nk(), (N_ODD, D_MODEL, MLA_IN), D_MODEL)
    inp['mla_q_lora_gain'] = _gain(nk(), (N_ODD, MLA_Q_LORA))
    inp['mla_kv_lora_gain'] = _gain(nk(), (N_ODD, MLA_KV_LORA))
    inp['mla_w_uq'] = _w(nk(), (N_ODD, MLA_Q_LORA, MLA_HEADS * MLA_QK), MLA_Q_LORA)
    inp['mla_w_ukv'] = _w(nk(), (N_ODD, MLA_KV_LORA, MLA_HEADS * (MLA_NOPE + MLA_V)), MLA_KV_LORA)
    inp['mla_q_gain'] = _gain(nk(), (N_ODD, MLA_QK))
    inp['mla_k_gain'] = _gain(nk(), (N_ODD, MLA_QK))
    inp['mla_w_out'] = _w(nk(), (N_ODD, MLA_MIX, D_MODEL), MLA_MIX)
    inp['xmem_norm'] = _gain(nk(), (DEPTH, D_MODEL))
    inp['xmem_mem_norm'] = _gain(nk(), (DEPTH, D_MODEL))
    inp['xmem_wq'] = _w(nk(), (DEPTH, D_MODEL, D_MODEL), D_MODEL)
    inp['xmem_wkv'] = _w(nk(), (DEPTH, D_MODEL, 2 * D_MODEL), D_MODEL)
    inp['xmem_q_gain'] = _gain(nk(), (DEPTH, MEM_HEAD_DIM))
    inp['xmem_k_gain'] = _gain(nk(), (DEPTH, MEM_HEAD_DIM))
    inp['xmem_wo'] = _w(nk(), (DEPTH, D_MODEL, D_MODEL), D_MODEL)
    inp['ffn_post_norm'] = _gain(nk(), (DEPTH, D_MODEL))
    inp['ffn_post_w_gu'] = _w(nk(), (DEPTH, D_MODEL, 2 * D_FF), D_MODEL)
    inp['ffn_post_w_down'] = _w(nk(), (DEPTH, D_FF, D_MODEL), D_FF)
    return inp

def first_block(x, mem, positions,
              ffn_pre_norm, ffn_pre_w_gu, ffn_pre_w_down,
              mix_norm,
              sbg_w_in, sgu_ln_gain, sgu_ln_bias, sgu_w, sgu_b, sbg_w_out,
              mla_w_in, mla_q_lora_gain, mla_kv_lora_gain, mla_w_uq, mla_w_ukv,
              mla_q_gain, mla_k_gain, mla_w_out,
              xmem_norm, xmem_mem_norm, xmem_wq, xmem_wkv, xmem_q_gain, xmem_k_gain, xmem_wo,
              ffn_post_norm, ffn_post_w_gu, ffn_post_w_down):
    for layer in range(DEPTH):
        x = x + 0.5 * _swiglu(_rmsnorm(x, ffn_pre_norm[layer]),
                              ffn_pre_w_gu[layer], ffn_pre_w_down[layer])
        h = _rmsnorm(x, mix_norm[layer])
        if layer % 2 == 0:
            e = layer // 2
            x = x + _even_mixer(h, sbg_w_in[e], sgu_ln_gain[e], sgu_ln_bias[e],
                                sgu_w[e], sgu_b[e], sbg_w_out[e])
        else:
            o = layer // 2
            x = x + _mla_mixer(h, positions, mla_w_in[o], mla_q_lora_gain[o],
                               mla_kv_lora_gain[o], mla_w_uq[o], mla_w_ukv[o],
                               mla_q_gain[o], mla_k_gain[o], mla_w_out[o])
        x = x + _memory_cross_attention(_rmsnorm(x, xmem_norm[layer]),
                                        _rmsnorm(mem, xmem_mem_norm[layer]),
                                        xmem_wq[layer], xmem_wkv[layer],
                                        xmem_q_gain[layer], xmem_k_gain[layer], xmem_wo[layer])
        x = x + 0.5 * _swiglu(_rmsnorm(x, ffn_post_norm[layer]),
                              ffn_post_w_gu[layer], ffn_post_w_down[layer])
    return x


PLE_DIM = 256
CONV_WIDTH = 3
CONV_CH = 512
S5_CH = 512
S5_GROUP = 16
S5_GROUPS = S5_CH // S5_GROUP
S5_STATE = 64
AB_IN = 3 * CONV_CH + S5_CH
N_HEADS = 8
HEAD_DIM = 128
N_KV_HEADS = 2
IDX_HEADS = 8
IDX_DIM = 64
TOPK_MAX = 256
Q_BLOCK = 128
C_SIZES = (N_HEADS * HEAD_DIM, N_KV_HEADS * HEAD_DIM, N_KV_HEADS * HEAD_DIM,
           IDX_HEADS * IDX_DIM, IDX_DIM, IDX_HEADS)
C_SPLITS = tuple(int(v) for v in np.cumsum(C_SIZES)[:-1])
C_IN = int(sum(C_SIZES))
ROPE_THETA_2 = 500000.0
ROT_FRAC = 4
LN_EPS = 1e-5
DN_ALPHA = (2 * DEPTH) ** 0.25
DN_BETA = (8 * DEPTH) ** -0.25
N_EVEN_2 = (DEPTH + 1) // 2
N_ODD_2 = DEPTH // 2


def layer_norm(x, g, b):
    xf = x.astype(jnp.float32)
    mu = jnp.mean(xf, axis=-1, keepdims=True)
    var = jnp.mean(jnp.square(xf - mu), axis=-1, keepdims=True)
    return ((xf - mu) * lax.rsqrt(var + LN_EPS) * g.astype(jnp.float32) + b.astype(jnp.float32)).astype(x.dtype)

def swiglu(x, w1, w3, w2):
    return (jax.nn.silu(x @ w1) * (x @ w3)) @ w2

def rope_tables(positions, rot_dim):
    inv = ROPE_THETA_2 ** (-jnp.arange(0, rot_dim, 2, dtype=jnp.float32) / rot_dim)
    ang = positions.astype(jnp.float32)[..., None] * inv
    return jnp.cos(ang), jnp.sin(ang)

def partial_rope(t, cos, sin):
    half = cos.shape[-1]
    r = 2 * half
    tr = t[..., :r].astype(jnp.float32)
    t1, t2 = tr[..., :half], tr[..., half:]
    rot = jnp.concatenate([t1 * cos - t2 * sin, t2 * cos + t1 * sin], axis=-1).astype(t.dtype)
    return jnp.concatenate([rot, t[..., r:]], axis=-1)

def short_conv_mixer(h, gb, gc, conv_w):
    u = gc * h
    L = u.shape[1]
    up = jnp.pad(u, ((0, 0), (CONV_WIDTH - 1, 0), (0, 0)))
    v = sum(conv_w[j] * up[:, j:j + L] for j in range(CONV_WIDTH))
    return gb * v

def s5_mixer(u, lam_re, lam_im, log_dt, b_re, b_im, c_re, c_im, d_skip, w_glu, b_glu):
    f32 = jnp.float32
    Bt, L, _ = u.shape
    uf = u.astype(f32)
    ug = uf.reshape(Bt, L, S5_GROUPS, S5_GROUP)
    lr = jnp.minimum(lam_re.astype(f32), -1e-4)
    li = lam_im.astype(f32)
    dt = jnp.exp(log_dt.astype(f32))[:, None]
    mag = jnp.exp(lr * dt)
    ab_re = mag * jnp.cos(li * dt)
    ab_im = mag * jnp.sin(li * dt)
    nr, ni = ab_re - 1.0, ab_im
    den = lr * lr + li * li
    f_re = (nr * lr + ni * li) / den
    f_im = (ni * lr - nr * li) / den
    br, bi = b_re.astype(f32), b_im.astype(f32)
    bb_re = f_re[..., None] * br - f_im[..., None] * bi
    bb_im = f_re[..., None] * bi + f_im[..., None] * br
    bu_re = jnp.einsum('blgc,gpc->blgp', ug, bb_re)
    bu_im = jnp.einsum('blgc,gpc->blgp', ug, bb_im)
    a_re = jnp.broadcast_to(ab_re, bu_re.shape)
    a_im = jnp.broadcast_to(ab_im, bu_im.shape)

    def combine(e1, e2):
        a1r, a1i, b1r, b1i = e1
        a2r, a2i, b2r, b2i = e2
        return (a2r * a1r - a2i * a1i, a2r * a1i + a2i * a1r,
                a2r * b1r - a2i * b1i + b2r, a2r * b1i + a2i * b1r + b2i)

    _, _, s_re, s_im = lax.associative_scan(combine, (a_re, a_im, bu_re, bu_im), axis=1)
    y = (jnp.einsum('blgp,gcp->blgc', s_re, c_re.astype(f32))
         - jnp.einsum('blgp,gcp->blgc', s_im, c_im.astype(f32)))
    y = y.reshape(Bt, L, S5_CH) + d_skip.astype(f32) * uf
    z = jax.nn.gelu(y)
    out = z * jax.nn.sigmoid(z @ w_glu.astype(f32) + b_glu.astype(f32))
    return out.astype(u.dtype)

def dsa_mixer(proj, cos_a, sin_a, cos_i, sin_i):
    f32 = jnp.float32
    Bt, L, _ = proj.shape
    q, k, v, qi, ki, wi = jnp.split(proj, C_SPLITS, axis=-1)
    q = partial_rope(q.reshape(Bt, L, N_HEADS, HEAD_DIM), cos_a[:, :, None], sin_a[:, :, None])
    k = partial_rope(k.reshape(Bt, L, N_KV_HEADS, HEAD_DIM), cos_a[:, :, None], sin_a[:, :, None])
    v = v.reshape(Bt, L, N_KV_HEADS, HEAD_DIM)
    qi = partial_rope(qi.reshape(Bt, L, IDX_HEADS, IDX_DIM), cos_i[:, :, None], sin_i[:, :, None])
    ki = partial_rope(ki, cos_i, sin_i).astype(f32)
    wi = wi.astype(f32) * (IDX_HEADS ** -0.5 * IDX_DIM ** -0.5)
    topk = min(TOPK_MAX, L // 4)
    nb = L // Q_BLOCK

    def to_blocks(t):
        return jnp.moveaxis(t.reshape(Bt, nb, Q_BLOCK, *t.shape[2:]), 1, 0)

    t_pos = jnp.arange(L, dtype=jnp.int32).reshape(nb, Q_BLOCK)
    key_pos = jnp.arange(L, dtype=jnp.int32)
    bidx = jnp.arange(Bt)[:, None, None]
    rep = N_HEADS // N_KV_HEADS

    def block(args):
        qb, qib, wb, tb = args
        logits = jax.nn.relu(jnp.einsum('bthd,bsd->bths', qib.astype(f32), ki))
        score = jnp.einsum('bths,bth->bts', logits, wb)
        causal = key_pos[None, :] <= tb[:, None]
        score = jnp.where(causal[None], score, -jnp.inf)
        _, idx = lax.top_k(score, topk)
        valid = idx <= tb[None, :, None]
        k_sel = k[bidx, idx]
        v_sel = v[bidx, idx]
        qg = qb.reshape(Bt, Q_BLOCK, N_KV_HEADS, rep, HEAD_DIM)
        s = jnp.einsum('btgrd,btjgd->btgrj', qg, k_sel).astype(f32) * (HEAD_DIM ** -0.5)
        s = jnp.where(valid[:, :, None, None, :], s, -jnp.inf)
        pr = jax.nn.softmax(s, axis=-1)
        o = jnp.einsum('btgrj,btjgd->btgrd', pr.astype(v.dtype), v_sel)
        return o.reshape(Bt, Q_BLOCK, N_HEADS * HEAD_DIM)

    out = lax.map(block, (to_blocks(q), to_blocks(qi), to_blocks(wi), t_pos))
    return jnp.moveaxis(out, 0, 1).reshape(Bt, L, N_HEADS * HEAD_DIM)

def second_inputs(seed: int = 0) -> dict:
    key = jax.random.key(seed)
    ks = jax.random.split(key, 32)
    f32 = jnp.float32

    def nrm(i, shape, scale):
        return jax.random.normal(ks[i], shape, f32) * scale

    x = nrm(0, (BATCH, SEQ, D_MODEL), 1.0)
    p = nrm(1, (DEPTH, BATCH, SEQ, PLE_DIM), 1.0)
    offs = jax.random.randint(ks[2], (BATCH, 1), 0, 1024, dtype=jnp.int32)
    positions = offs + jnp.arange(SEQ, dtype=jnp.int32)[None, :]
    ln_g = 1.0 + nrm(3, (DEPTH, 3, D_MODEL), 0.02)
    ln_b = nrm(4, (DEPTH, 3, D_MODEL), 0.02)
    ffn_w1 = nrm(5, (DEPTH, 2, D_MODEL, D_FF), D_MODEL ** -0.5)
    ffn_w3 = nrm(6, (DEPTH, 2, D_MODEL, D_FF), D_MODEL ** -0.5)
    ffn_w2 = nrm(7, (DEPTH, 2, D_FF, D_MODEL), D_FF ** -0.5 * DN_BETA)
    ple_w_proj = nrm(8, (DEPTH, PLE_DIM, D_MODEL), PLE_DIM ** -0.5)
    ple_w_gate = nrm(9, (DEPTH, D_MODEL, D_MODEL), D_MODEL ** -0.5)
    ab_w_in = nrm(10, (N_EVEN_2, D_MODEL, AB_IN), D_MODEL ** -0.5)
    ab_w_out = nrm(11, (N_EVEN_2, CONV_CH + S5_CH, D_MODEL), (CONV_CH + S5_CH) ** -0.5 * DN_BETA)
    conv_w = nrm(12, (N_EVEN_2, CONV_WIDTH, CONV_CH), CONV_WIDTH ** -0.5)
    s5_lam_re = -0.5 + nrm(13, (N_EVEN_2, S5_GROUPS, S5_STATE), 0.01)
    s5_lam_im = (math.pi * jnp.arange(S5_STATE, dtype=f32))[None, None, :] + nrm(14, (N_EVEN_2, S5_GROUPS, S5_STATE), 0.01)
    s5_log_dt = jax.random.uniform(ks[15], (N_EVEN_2, S5_GROUPS), f32, math.log(1e-3), math.log(1e-1))
    s5_b_re = nrm(16, (N_EVEN_2, S5_GROUPS, S5_STATE, S5_GROUP), (2 * S5_GROUP) ** -0.5)
    s5_b_im = nrm(17, (N_EVEN_2, S5_GROUPS, S5_STATE, S5_GROUP), (2 * S5_GROUP) ** -0.5)
    s5_c_re = nrm(18, (N_EVEN_2, S5_GROUPS, S5_GROUP, S5_STATE), S5_STATE ** -0.5)
    s5_c_im = nrm(19, (N_EVEN_2, S5_GROUPS, S5_GROUP, S5_STATE), S5_STATE ** -0.5)
    s5_d = nrm(20, (N_EVEN_2, S5_CH), 1.0)
    s5_w_glu = nrm(21, (N_EVEN_2, S5_CH, S5_CH), S5_CH ** -0.5)
    s5_b_glu = nrm(22, (N_EVEN_2, S5_CH), 0.02)
    c_w_in = nrm(23, (N_ODD_2, D_MODEL, C_IN), D_MODEL ** -0.5)
    c_w_out = nrm(24, (N_ODD_2, N_HEADS * HEAD_DIM, D_MODEL), (N_HEADS * HEAD_DIM) ** -0.5 * DN_BETA)
    return {'x': x, 'p': p, 'positions': positions, 'ln_g': ln_g, 'ln_b': ln_b,
            'ffn_w1': ffn_w1, 'ffn_w3': ffn_w3, 'ffn_w2': ffn_w2,
            'ple_w_proj': ple_w_proj, 'ple_w_gate': ple_w_gate,
            'ab_w_in': ab_w_in, 'ab_w_out': ab_w_out, 'conv_w': conv_w,
            's5_lam_re': s5_lam_re, 's5_lam_im': s5_lam_im, 's5_log_dt': s5_log_dt,
            's5_b_re': s5_b_re, 's5_b_im': s5_b_im, 's5_c_re': s5_c_re, 's5_c_im': s5_c_im,
            's5_d': s5_d, 's5_w_glu': s5_w_glu, 's5_b_glu': s5_b_glu,
            'c_w_in': c_w_in, 'c_w_out': c_w_out}

def second_block(x, p, positions, ln_g, ln_b, ffn_w1, ffn_w3, ffn_w2, ple_w_proj, ple_w_gate,
              ab_w_in, ab_w_out, conv_w, s5_lam_re, s5_lam_im, s5_log_dt, s5_b_re, s5_b_im,
              s5_c_re, s5_c_im, s5_d, s5_w_glu, s5_b_glu, c_w_in, c_w_out):
    cos_a, sin_a = rope_tables(positions, HEAD_DIM // ROT_FRAC)
    cos_i, sin_i = rope_tables(positions, IDX_DIM // ROT_FRAC)
    h = x
    for i in range(DEPTH):
        h = layer_norm(DN_ALPHA * h + 0.5 * swiglu(h, ffn_w1[i, 0], ffn_w3[i, 0], ffn_w2[i, 0]),
                       ln_g[i, 0], ln_b[i, 0])
        j = i // 2
        if i % 2 == 0:
            proj = h @ ab_w_in[j]
            hc, gb, gc, u = jnp.split(proj, [CONV_CH, 2 * CONV_CH, 3 * CONV_CH], axis=-1)
            ya = short_conv_mixer(hc, gb, gc, conv_w[j])
            yb = s5_mixer(u, s5_lam_re[j], s5_lam_im[j], s5_log_dt[j], s5_b_re[j], s5_b_im[j],
                          s5_c_re[j], s5_c_im[j], s5_d[j], s5_w_glu[j], s5_b_glu[j])
            mix = jnp.concatenate([ya, yb], axis=-1) @ ab_w_out[j]
        else:
            proj = h @ c_w_in[j]
            mix = dsa_mixer(proj, cos_a, sin_a, cos_i, sin_i) @ c_w_out[j]
        h = layer_norm(DN_ALPHA * h + mix, ln_g[i, 1], ln_b[i, 1])
        h = layer_norm(DN_ALPHA * h + 0.5 * swiglu(h, ffn_w1[i, 1], ffn_w3[i, 1], ffn_w2[i, 1]),
                       ln_g[i, 2], ln_b[i, 2])
        h = h + (p[i] @ ple_w_proj[i]) * jax.nn.sigmoid(h @ ple_w_gate[i])
    return h


def setup_inputs(seed=0):
    out = dict(first_inputs(seed))
    for name, value in second_inputs(seed + 1).items():
        if name != "x":
            out[name + "_2"] = value
    return out


def reference(
    x, mem, positions, ffn_pre_norm, ffn_pre_w_gu, ffn_pre_w_down, mix_norm, sbg_w_in,
    sgu_ln_gain, sgu_ln_bias, sgu_w, sgu_b, sbg_w_out, mla_w_in, mla_q_lora_gain,
    mla_kv_lora_gain, mla_w_uq, mla_w_ukv, mla_q_gain, mla_k_gain, mla_w_out, xmem_norm,
    xmem_mem_norm, xmem_wq, xmem_wkv, xmem_q_gain, xmem_k_gain, xmem_wo, ffn_post_norm,
    ffn_post_w_gu, ffn_post_w_down, p_2, positions_2, ln_g_2, ln_b_2, ffn_w1_2, ffn_w3_2,
    ffn_w2_2, ple_w_proj_2, ple_w_gate_2, ab_w_in_2, ab_w_out_2, conv_w_2, s5_lam_re_2,
    s5_lam_im_2, s5_log_dt_2, s5_b_re_2, s5_b_im_2, s5_c_re_2, s5_c_im_2, s5_d_2, s5_w_glu_2,
    s5_b_glu_2, c_w_in_2, c_w_out_2,
):
    x = first_block(
        x, mem, positions, ffn_pre_norm, ffn_pre_w_gu, ffn_pre_w_down, mix_norm, sbg_w_in,
        sgu_ln_gain, sgu_ln_bias, sgu_w, sgu_b, sbg_w_out, mla_w_in, mla_q_lora_gain,
        mla_kv_lora_gain, mla_w_uq, mla_w_ukv, mla_q_gain, mla_k_gain, mla_w_out, xmem_norm,
        xmem_mem_norm, xmem_wq, xmem_wkv, xmem_q_gain, xmem_k_gain, xmem_wo, ffn_post_norm,
        ffn_post_w_gu, ffn_post_w_down,
    )
    return second_block(
        x, p_2, positions_2, ln_g_2, ln_b_2, ffn_w1_2, ffn_w3_2, ffn_w2_2, ple_w_proj_2,
        ple_w_gate_2, ab_w_in_2, ab_w_out_2, conv_w_2, s5_lam_re_2, s5_lam_im_2, s5_log_dt_2,
        s5_b_re_2, s5_b_im_2, s5_c_re_2, s5_c_im_2, s5_d_2, s5_w_glu_2, s5_b_glu_2, c_w_in_2,
        c_w_out_2,
    )


_drawn_inputs = setup_inputs


def setup_inputs(seed=0):
    import zlib

    import numpy as np

    out = dict(_drawn_inputs(seed))
    spreads = {}
    factors = {'ffn_pre_norm': 4.637,
     'mix_norm': 3.65,
     'sgu_ln_gain': 8.0,
     'sgu_ln_bias': 8.0,
     'mla_q_lora_gain': 8.0,
     'mla_kv_lora_gain': 8.0,
     'mla_q_gain': 8.0,
     'mla_k_gain': 8.0,
     'xmem_norm': 8.0,
     'xmem_mem_norm': 8.0,
     'xmem_q_gain': 8.0,
     'xmem_k_gain': 8.0,
     'ffn_post_norm': 5.691,
     's5_lam_re_2': 64.0,
     's5_lam_im_2': 62.664,
     's5_log_dt_2': 64.0,
     's5_b_re_2': 64.0,
     's5_b_im_2': 64.0,
     's5_c_re_2': 64.0,
     's5_c_im_2': 64.0,
     's5_b_glu_2': 64.0,
     's5_w_glu_2': 2.87}
    for name, (base, spread) in spreads.items():
        noise = np.random.default_rng([zlib.crc32(name.encode()), seed]).standard_normal(out[name].shape)
        drawn = base * np.exp(spread * noise) if base else spread * noise
        out[name] = __import__('jax').numpy.asarray(drawn.astype(out[name].dtype))
    for name, factor in factors.items():
        out[name] = (out[name] * factor).astype(out[name].dtype)
    return out
```

```python
from contextlib import ExitStack

import numpy as np

import concourse.bass as bass
from concourse import mybir

F32 = mybir.dt.float32
F32R = mybir.dt.float32r
I32 = mybir.dt.int32
ALU = mybir.AluOpType
ACT = mybir.ActivationFunctionType
AX = mybir.AxisListType

D = 1024
FF = 2816
UNIT = 1024
RAW = 6
SPLIT = 6
AHEAD = 3
NEG = -1.0e30
GONE = -3.0e38
ALPHA = 4.0 ** 0.25
MAGIC = 12582912.0
TWO_PI = (6.28125, 2029.0 / 2 ** 20, 2 * np.pi - 6.28125 - 2029.0 / 2 ** 20)

FFN_GU = [512] * 11
HALVES = [512, 512]


def layers():
    out = []
    for l in range(2):
        out += [(f"gu_pre{l}", 8, FFN_GU), (f"dn_pre{l}", 22, HALVES)]
        if l == 0:
            out += [("sbg_in", 8, [512] * 5), ("sbg_out", 8, HALVES)]
        else:
            out += [("mla_in", 8, [512, 288]), ("mla_uq", 4, [512] * 3), ("mla_ukv", 2, [512] * 4),
                    ("mla_out", 8, HALVES)]
        out += [(f"x_kv{l}", 8, [512] * 4), (f"x_q{l}", 8, HALVES), (f"x_o{l}", 8, HALVES)]
        out += [(f"gu_post{l}", 8, FFN_GU), (f"dn_post{l}", 22, HALVES)]
    for l in range(2):
        out += [(f"w13_{l}_0", 8, FFN_GU), (f"w2_{l}_0", 22, HALVES)]
        if l == 0:
            out += [("ab_in", 8, [512] * 4), ("glu", 4, [512]), ("ab_out", 8, HALVES)]
        else:
            out += [("c_in", 8, [512] * 4 + [72]), ("c_out", 8, HALVES)]
        out += [(f"w13_{l}_1", 8, FFN_GU), (f"w2_{l}_1", 22, HALVES)]
        out += [(f"ple_p{l}", 2, HALVES), (f"ple_g{l}", 8, HALVES)]
    return out


def units_of(kts, widths):
    out, col = [], 0
    for c, w in enumerate(widths):
        n = max(1, UNIT // w)
        for k in range(0, kts, n):
            out.append((c, k, min(n, kts - k), w, col))
        col += w
    return out


CONSTS = ["ident", "incl", "ones", "tril", "sbmask", "causal", "inv1", "inva", "invi"]


def consts():
    i = np.arange(128)
    k, q = i[:, None], np.arange(256)[None, :]
    ident = np.eye(128)
    incl = (i[:, None] >= i[None, :]) * 1.0
    tril = (i[:, None] <= i[None, :]) * 1.0
    sbmask = np.concatenate([np.where(k < q, 0.0, NEG), np.where(k < i[None, :], 0.0, NEG)], 1)
    causal = np.concatenate([np.where(i[None, :] <= k, 0.0, NEG), np.where(q <= k + 128, 0.0, NEG)], 1)

    def inv(theta, half):
        e = -np.arange(half, dtype=np.float32) / np.float32(half)
        return np.broadcast_to(np.float32(theta) ** e, (128, half))

    parts = [ident, incl, np.ones((128, 128)), tril, sbmask, causal,
             inv(10000.0, 16), inv(500000.0, 16), inv(500000.0, 8)]
    at, o = {}, 0
    for name, p in zip(CONSTS, parts):
        at[name] = (o, o + p.shape[1])
        o += p.shape[1]
    return np.concatenate([p.astype(np.float32) for p in parts], 1), at


SMALL = [("sguw", 1024), ("sgub", 8), ("convw", 12), ("dskip", 4), ("bglu", 4),
         ("lre", 16), ("lim", 16), ("ldt", 16), ("bre", 512), ("bim", 512), ("cre", 512), ("cim", 512),
         ("pt0", 512), ("pt1", 512)]


def small_at():
    at, o = {}, 0
    for name, w in SMALL:
        at[name] = (o, o + w)
        o += w
    return at, o


class Program:

    def __init__(self, nc, ctx):
        self.nc = nc
        self.ctx = ctx
        self.queue = {e: [] for e in ("pe", "act", "dve", "pool", "sp")}
        self.sem = {e: ctx.enter_context(nc.semaphore("s_" + e)) for e in ("pe", "act", "dve", "pool")}
        self.count = {}
        self.seen = {e: {} for e in self.queue}
        self.last = {e: None for e in ("pe", "act", "dve", "pool")}

    def wait(self, e, waits):
        need = {}

        def gather(x):
            if x is None:
                return
            if isinstance(x, tuple) and len(x) == 2 and isinstance(x[0], str):
                need[x[0]] = max(need.get(x[0], 0), x[1])
            else:
                for y in x:
                    gather(y)

        gather(waits)
        for s, v in need.items():
            if self.seen[e].get(s, 0) < v:
                self.seen[e][s] = v
                self.queue[e].append(lambda eng, s=s, v=v: eng.wait_ge(self.sem[s], v))

    def emit(self, e, fn, waits=(), inc=True):
        self.wait(e, waits)
        if not inc:
            self.queue[e].append(lambda eng: fn(eng))
            return None
        self.count[e] = self.count.get(e, 0) + 1
        self.queue[e].append(lambda eng: fn(eng).then_inc(self.sem[e], 1))
        self.last[e] = (e, self.count[e])
        return self.last[e]

    def dma(self, e, s, out, in_, waits=()):
        if s not in self.sem:
            self.sem[s] = self.ctx.enter_context(self.nc.semaphore(s))
        self.wait(e, waits)
        self.count[s] = self.count.get(s, 0) + 16
        self.queue[e].append(lambda eng: eng.dma_start(out, in_).then_inc(self.sem[s], 16))
        return (s, self.count[s])

    def fence(self):
        done = [t for t in self.last.values() if t]
        for e in ("act", "dve", "pool"):
            self.wait(e, done)

    def act(self, out, in_, func=ACT.Copy, waits=(), bias=0.0, scale=1.0, accum=None):
        if func == ACT.Copy:
            return self.emit("act", lambda e: e.activation(out, in_, func, scale=scale), waits)
        if accum is None:
            return self.emit("act", lambda e: e.activation(out, in_, func, bias=bias, scale=scale), waits)
        return self.emit("act", lambda e: e.activation(out, in_, func, bias=bias, scale=scale, accum_out=accum), waits)

    def tt(self, out, a, b, op, waits=(), e="dve"):
        return self.emit(e, lambda g: g.tensor_tensor(out, a, b, op), waits)

    def ts(self, out, a, s1, op0, s2=None, op1=ALU.bypass, waits=(), e="dve"):
        if s2 is None:
            return self.emit(e, lambda g: g.tensor_scalar(out, a, s1, None, op0), waits)
        return self.emit(e, lambda g: g.tensor_scalar(out, a, s1, s2, op0, op1), waits)

    def stt(self, out, a, s, b, op0, op1, waits=()):
        return self.emit("dve", lambda g: g.scalar_tensor_tensor(out=out, in0=a, scalar=s, in1=b, op0=op0, op1=op1), waits)

    def copy(self, out, a, waits=(), e="dve"):
        return self.emit(e, lambda g: g.tensor_copy(out, a), waits)

    def recip(self, out, a, waits=()):
        return self.emit("dve", lambda g: g.reciprocal(out, a), waits)

    def reduce(self, out, a, op, waits=(), negate=False):
        return self.emit("dve", lambda g: g.tensor_reduce(out, a, AX.X, op, negate=negate), waits)

    def memset(self, out, v, waits=(), e="dve"):
        return self.emit(e, lambda g: g.memset(out, v), waits)

    def mm(self, out, l, r, start, stop, waits=(), inc=False):
        return self.emit("pe", lambda e: e.matmul(out, l, r, start=start, stop=stop), waits, inc)

    def tr(self, out, in_, ident, waits=(), inc=False):
        return self.emit("pe", lambda e: e.transpose(out, in_, ident), waits, inc)


class Bank:
    def __init__(self, t):
        self.t = t
        self.free = []


def build(nc, d, out):
    plan = layers()
    ctx = ExitStack()
    with ctx:
        p = Program(nc, ctx)

        def sb(name, shape, dt=F32, where=None):
            return (where or ctx).enter_context(nc.sbuf_tensor(name, shape, dt))

        X = sb("X", [128, 2, D])
        XN = sb("XN", [128, 2, D])
        XH = sb("XH", [128, 8, 256], F32R)
        XL = sb("XL", [128, 8, 256], F32R)
        raw = [sb(f"raw{i}", [128, UNIT]) for i in range(RAW)]
        whi = [sb(f"whi{i}", [128, UNIT], F32R) for i in range(SPLIT)]
        wlo = [sb(f"wlo{i}", [128, UNIT], F32R) for i in range(SPLIT)]
        gain_sb = [sb(f"gain{i}", [128, D]) for i in range(4)]
        cat, cn = consts()[1], consts()[0].shape[1]
        C = sb("C", [128, cn])
        st = sb("st", [128, 64])
        banks = [Bank(ctx.enter_context(nc.psum_tensor(f"bank{i}", [128, 512], F32))) for i in range(8)]
        turn = [0, 0]

        def const(name):
            a, b = cat[name]
            return C[:, a:b]

        t_const = p.dma("sp", "d_const", C[:, :], d["consts"])
        ident = const("ident")

        def scratch():
            turn[0] += 1
            return banks[4 + turn[0] % 4]

        def pair():
            turn[1] += 1
            return banks[2 * (turn[1] % 2)], banks[2 * (turn[1] % 2) + 1]

        stream = []
        for name, kts, widths in plan:
            off = 0
            for u in units_of(kts, widths):
                n = u[2] * u[3]
                stream.append((name, off, n))
                off += 128 * n
        t_load, t_split, t_used = {}, {}, {}

        def load(u):
            if u >= len(stream):
                return
            name, off, n = stream[u]
            t_load[u] = p.dma("sp", f"d_raw{u % RAW}", raw[u % RAW][:, 0:n],
                              d["w_" + name][off:off + 128 * n].rearrange("(p w) -> p w", p=128),
                              [t_split[u - RAW]] if u >= RAW else [])

        split_next = [0]

        def split_to(u):
            while split_next[0] <= min(u, len(stream) - 1):
                v = split_next[0]
                n = stream[v][2]
                src, hi, lo = raw[v % RAW][:, 0:n], whi[v % SPLIT][:, 0:n], wlo[v % SPLIT][:, 0:n]
                free = t_used[v - SPLIT] if v >= SPLIT else None
                th = p.act(hi, src, waits=[t_load[v], free])
                t_split[v] = p.tt(lo, src, hi.bitcast(F32), ALU.subtract, [th, t_load[v], free])
                load(v + RAW)
                split_next[0] += 1

        for u in range(RAW):
            load(u)
        unit_now = [0]
        layer_now = [0]
        pending = []

        def flush():
            todo, pending[:] = list(pending), []
            for f in todo:
                f()

        def weights(k0, nk, w):
            u = unit_now[0]
            unit_now[0] += 1
            split_to(u + AHEAD)
            hi = whi[u % SPLIT][:, 0:nk * w].rearrange("p (k w) -> p k w", k=nk)
            lo = wlo[u % SPLIT][:, 0:nk * w].rearrange("p (k w) -> p k w", k=nk)
            return u, hi, lo

        def linear(name, lhs, evac):
            assert plan[layer_now[0]][0] == name, (plan[layer_now[0]][0], name)
            _, kts, widths = plan[layer_now[0]]
            layer_now[0] += 1
            us = units_of(kts, widths)
            last = None
            for c, w in enumerate(widths):
                bs = pair()
                toks = [None, None]
                mine = [x for x in us if x[0] == c]
                for i, (_, k0, nk, _, _) in enumerate(mine):
                    u, hi, lo = weights(k0, nk, w)
                    for k in range(nk):
                        kt = k0 + k
                        for t in range(2):
                            xh, xl, dep = lhs(kt, t)
                            o = bs[t].t[:, 0:w]
                            p.mm(o, xh, hi[:, k, :], kt == 0, False, [dep, t_split[u], bs[t].free])
                            p.mm(o, xh, lo[:, k, :], False, False)
                            toks[t] = p.mm(o, xl, hi[:, k, :], False, kt == kts - 1,
                                           inc=kt == kts - 1 or k == nk - 1)
                    t_used[u] = toks[1]
                    if i == min(1, len(mine) - 1):
                        flush()
                last = toks[1]
                later = evac(c, w, [(bs[t], toks[t]) for t in range(2)])
                if later:
                    pending.append(later)
            return last

        x_used = [None]

        def to_halves(src, kts, hi, lo, dep, war=None, first=0):
            got = {}
            for t in range(2):
                for g in range(0, kts, 4):
                    n = min(4, kts - g)
                    b = scratch()
                    for k in range(n):
                        tok = p.tr(b.t[:, k * 128:(k + 1) * 128], src(t, g + k), ident,
                                   [dep[t], b.free, t_const], k == n - 1)
                    v = b.t[:, 0:n * 128].rearrange("p (k n) -> p k n", k=n)
                    h = hi[:, first + g:first + g + n, t * 128:(t + 1) * 128]
                    th = p.act(h, v, waits=[tok, war])
                    tl = p.tt(lo[:, first + g:first + g + n, t * 128:(t + 1) * 128], v, h.bitcast(F32),
                              ALU.subtract, [th, war])
                    b.free = [tl]
                    for k in range(n):
                        got[g + k, t] = tl
            return got

        def lhs_of(hi, lo, got, first=0):
            return lambda kt, t: (hi[:, first + kt, t * 128:(t + 1) * 128],
                                  lo[:, first + kt, t * 128:(t + 1) * 128], got[kt, t])

        gains = []
        for l in range(2):
            gains += [d["ffn_pre_norm"][l], d["mix_norm"][l]]
            if l == 0:
                gains += [d["sgu_ln_gain"][0], d["sgu_ln_bias"][0]]
            else:
                gains += [d["mla_q_lora_gain"][0], d["mla_kv_lora_gain"][0], d["mla_q_gain"][0], d["mla_k_gain"][0]]
            gains += [d["xmem_mem_norm"][l], d["xmem_k_gain"][l], d["xmem_norm"][l], d["xmem_q_gain"][l],
                      d["ffn_post_norm"][l]]
        for l in range(2):
            for j in range(3):
                gains += [d["ln_g_2"][l, j], d["ln_b_2"][l, j]]
        gain_tok, gain_now = {}, [0]

        def gain_load(i, waits=()):
            if i < len(gains):
                n = gains[i].shape[0]
                gain_tok[i] = p.dma("sp", f"d_gain{i % 4}", gain_sb[i % 4][:, 0:n], gains[i].partition_broadcast(128), waits)

        for i in range(4):
            gain_load(i)

        def gain():
            i = gain_now[0]
            gain_now[0] += 1
            return i, gain_sb[i % 4][:, 0:gains[i].shape[0]], gain_tok[i]

        def gain_done(i, tok):
            gain_load(i + 4, [tok])

        def rstd_of(ss, n, inv_n, eps, waits):
            a = p.ts(ss, ss, inv_n, ALU.mult, eps, ALU.add, waits)
            b = p.act(ss, ss, ACT.Sqrt, [a])
            return p.recip(ss, ss, [b])

        def rms(src, dst, g, gt, col, n, waits, junk, eps=1e-6):
            a = rms_sum(src, col, waits, junk)
            return rms_scale(src, dst, g, gt, col, n, [a], eps)

        def rms_sum(src, col, waits, junk):
            return p.act(junk, src, ACT.Square, waits, accum=st[:, col:col + 1])

        def rms_scale(src, dst, g, gt, col, n, a, eps=1e-6):
            s = st[:, col:col + 1]
            r = rstd_of(s, 1, 1.0 / n, eps, [a])
            return p.stt(dst, src, s, g, ALU.mult, ALU.mult, [r, gt, a])

        xt = [None, None]

        def x_norm_halves():
            gi, g, gt = gain()
            dep = []
            for t in range(2):
                dep.append(rms(X[:, t, :], XN[:, t, :], g, gt, t, D, [xt[t], xn_used[0]], XN[:, t, :]))
            gain_done(gi, dep[1])
            got = to_halves(lambda t, k: XN[:, t, k * 128:(k + 1) * 128], 8, XH, XL, dep, x_used[0])
            xn_used[0] = p.last["pe"]
            return got

        xn_used = [None]

        def xn_halves(dep):
            got = to_halves(lambda t, k: XN[:, t, k * 128:(k + 1) * 128], 8, XH, XL, dep, x_used[0])
            xn_used[0] = p.last["pe"]
            return got

        def x_halves():
            return to_halves(lambda t, k: X[:, t, k * 128:(k + 1) * 128], 8, XH, XL, xt, x_used[0])

        def add_x(c, w, bs):
            for t, (b, tok) in enumerate(bs):
                xs = X[:, t, c * 512:c * 512 + w]
                xt[t] = p.tt(xs, b.t[:, 0:w], xs, ALU.add, [tok, xt[t]])
                b.free = [xt[t]]

        phase = [0]

        def ffn(gu, dn, got, post):
            phase[0] += 1
            n = phase[0]
            p.fence()
            with ExitStack() as s:
                HH = sb(f"HH{n}", [128, 22, 256], F32R, s)
                HL = sb(f"HL{n}", [128, 22, 256], F32R, s)
                sg = sb(f"sg{n}", [128, 2, 2, 256], F32, s)
                hb = sb(f"hb{n}", [128, 2, 2, 256], F32, s)
                ready, turned = {}, {}

                def evac(c, w, bs):
                    toks = []
                    for t, (b, tok) in enumerate(bs):
                        a = p.act(sg[:, c % 2, t, :], b.t[:, 0:256], ACT.Silu, [tok, turned.get(c - 2)])
                        h = p.tt(hb[:, c % 2, t, :], sg[:, c % 2, t, :], b.t[:, 256:512], ALU.mult,
                                 [a, tok, turned.get(c - 2)])
                        b.free = [h]
                        toks.append(h)

                    def later():
                        b = scratch()
                        for k in range(2):
                            for t in range(2):
                                tok = p.tr(b.t[:, (2 * k + t) * 128:(2 * k + t + 1) * 128],
                                           hb[:, c % 2, t, k * 128:(k + 1) * 128], ident,
                                           [toks[t], b.free], k == 1 and t == 1)
                        turned[c] = tok
                        v = b.t[:, :].rearrange("p (k n) -> p k n", k=2)
                        hh = HH[:, 2 * c:2 * c + 2, :]
                        th = p.act(hh, v, waits=[tok])
                        tl = p.tt(HL[:, 2 * c:2 * c + 2, :], v, hh.bitcast(F32), ALU.subtract, [th])
                        b.free = [tl]
                        ready[2 * c] = ready[2 * c + 1] = tl

                    return later

                x_used[0] = linear(gu, lhs_of(XH, XL, got), evac)

                def lhs(kt, t):
                    return HH[:, kt, t * 128:(t + 1) * 128], HL[:, kt, t * 128:(t + 1) * 128], ready[kt]

                linear(dn, lhs, post)

        def half_add(c, w, bs):
            for t, (b, tok) in enumerate(bs):
                xs = X[:, t, c * 512:c * 512 + w]
                xt[t] = p.stt(xs, b.t[:, 0:w], 0.5, xs, ALU.mult, ALU.add, [tok, xt[t]])
                b.free = [xt[t]]

        def half_mix(c, w, bs, half=0.5):
            for t, (b, tok) in enumerate(bs):
                xs, tmp = X[:, t, c * 512:c * 512 + w], XN[:, t, c * 512:c * 512 + w]
                a = p.act(tmp, b.t[:, 0:w], waits=[tok, xn_used[0]], scale=half)
                b.free = [a]
                xt[t] = p.stt(xs, xs, ALPHA, tmp, ALU.mult, ALU.add, [a, xt[t], x_used[0]])

        def full_mix(c, w, bs):
            half_mix(c, w, bs, 1.0)

        bn = sb("bn", [128, 2, 2, 6])
        mv = sb("mv", [128, 2, 2])

        def layer_norm():
            gi, g, gt = gain()
            bi, bb, bt = gain()
            for t in range(2):
                toks = []
                for c in range(2):
                    toks.append(p.emit("dve", lambda e, t=t, c=c: e.bn_stats(bn[:, t, c, :], X[:, t, c * 512:(c + 1) * 512]),
                                       [xt[t]]))
                a = p.emit("dve", lambda e, t=t: e.bn_aggr(mv[:, t, :], bn[:, t, :, :].rearrange("p c n -> p (c n)")), toks)
                r = rstd_of(mv[:, t, 1:2], 1, 1.0, 1e-5, [a])
                m = p.stt(XN[:, t, :], X[:, t, :], mv[:, t, 0:1], g, ALU.subtract, ALU.mult, [a, gt])
                xt[t] = p.stt(X[:, t, :], XN[:, t, :], mv[:, t, 1:2], bb, ALU.mult, ALU.add, [r, m, bt])
            xn_used[0] = xt[1]
            gain_done(gi, xt[1])
            gain_done(bi, xt[1])

        def sincos(sn, cs, ang, tmp, waits):
            a = p.ts(tmp, ang, float(1 / (2 * np.pi)), ALU.mult, MAGIC, ALU.add, waits)
            a = p.ts(tmp, tmp, MAGIC, ALU.subtract, waits=[a])
            for part in TWO_PI:
                a = p.stt(ang, tmp, -float(part), ang, ALU.mult, ALU.add, [a])
            a = p.ts(ang, ang, 3.1415925, ALU.min, -3.1415925, ALU.max, [a])
            b = p.act(sn, ang, ACT.Sin, [a])
            c = p.act(cs, ang, ACT.Sin, [a], scale=0.5)
            c = p.tt(cs, cs, cs, ALU.mult, [c])
            c = p.ts(cs, cs, -2.0, ALU.mult, 1.0, ALU.add, [c])
            return [b, c]

        def attend(name, heads, dv, segs, scores, values, scale, bias, bt, dst, dep, vdep):
            nb = 4
            width = sum(s[2] for s in segs)
            hpb = 512 // dv
            blocks = [(t, o + 128 * j, j, n // 128) for t, o, n in segs for j in range(n // 128)]
            with ExitStack() as s:
                S = sb(name + "S", [128, nb, width], F32, s)
                PT = sb(name + "PT", [128, nb, width], F32, s)
                nm = sb(name + "nm", [128, heads, 2], F32, s)
                rs = sb(name + "rs", [128, 2, heads], F32, s)
                t_exp, t_turn, t_pt, t_pv, obanks, outs = {}, {}, {}, {}, {}, {}

                def score(h):
                    b = scratch()
                    for i, (t, o, n) in enumerate(segs):
                        parts = scores(h, i)
                        for j, (l, r) in enumerate(parts):
                            tok = p.mm(b.t[:, o:o + n], l, r, j == 0, j == len(parts) - 1,
                                       [dep, b.free], j == len(parts) - 1 and i == len(segs) - 1)
                    src = b.t[:, 0:width]
                    war = t_turn.get(h - nb)
                    if bias is not None:
                        a = p.stt(S[:, h % nb, :], src, scale, bias, ALU.mult, ALU.add, [tok, bt, war])
                        b.free = [a]
                        src = S[:, h % nb, :]
                    else:
                        a = tok
                    es, ms = [], []
                    for i, (t, o, n) in enumerate(segs):
                        m = p.reduce(nm[:, h, t:t + 1], src[:, o:o + n], ALU.max, [a], negate=True)
                        if bias is None:
                            m = p.ts(nm[:, h, t:t + 1], nm[:, h, t:t + 1], scale, ALU.mult, waits=[m])
                        ms.append(m)
                    for i, (t, o, n) in enumerate(segs):
                        es.append(p.act(S[:, h % nb, o:o + n], src[:, o:o + n], ACT.Exp, [ms, war],
                                        bias=nm[:, h, t:t + 1], scale=1.0 if bias is not None else scale,
                                        accum=rs[:, t, h:h + 1]))
                    if bias is None:
                        b.free = es
                    t_exp[h] = es

                def turn_p(h):
                    b = scratch()
                    for i, (t, o, j, n) in enumerate(blocks):
                        tok = p.tr(b.t[:, i * 128:(i + 1) * 128], S[:, h % nb, o:o + 128], ident,
                                   [t_exp[h], b.free], i == len(blocks) - 1)
                    t_turn[h] = tok
                    t_pt[h] = p.act(PT[:, h % nb, :], b.t[:, 0:width], waits=[tok, t_pv.get(h - nb)])
                    b.free = [t_pt[h]]

                def pv(h):
                    if h % hpb == 0:
                        obanks[h // hpb] = pair()
                    ob = obanks[h // hpb]
                    for i, (t, o, j, n) in enumerate(blocks):
                        v = values(h, j)
                        tok = p.mm(ob[t].t[:, (h % hpb) * dv:(h % hpb + 1) * dv], PT[:, h % nb, i * 128:(i + 1) * 128], v,
                                   j == 0, j == n - 1, [t_pt[h], vdep, ob[t].free], i == len(blocks) - 1)
                    t_pv[h] = tok
                    if h % hpb == hpb - 1:
                        h0 = h - hpb + 1
                        for t in range(2):
                            r = p.recip(rs[:, t, h0:h + 1], rs[:, t, h0:h + 1], [t_exp[x] for x in range(h0, h + 1)])
                            outs[t] = p.tt(dst(t, h0, hpb).rearrange("p (h d) -> p h d", h=hpb),
                                           ob[t].t[:, 0:hpb * dv].rearrange("p (h d) -> p h d", h=hpb),
                                           rs[:, t, h0:h + 1].unsqueeze(2).broadcast_to([128, hpb, dv]),
                                           ALU.mult, [r, tok, xn_used[0]])
                            ob[t].free = [outs[t]]

                for i in range(heads + 2):
                    if i < heads:
                        score(i)
                    if 1 <= i <= heads:
                        turn_p(i - 1)
                    if i >= 2:
                        pv(i - 2)
            return [outs[0], outs[1]]

        tx = [p.dma("sp", f"d_x{t}", X[:, t, :], d["x"][t * 128:(t + 1) * 128, :]) for t in range(2)]
        xt[0], xt[1] = tx

        def even_mixer():
            got = x_norm_halves()
            p.fence()
            with ExitStack() as s:
                sat, _ = small_at()
                W = sb("sguw", [128, 8, 128], F32, s)
                sbias = sb("sgub", [128, 8], F32, s)
                Q = sb("ev_qk", [128, 2, 512], F32, s)
                qT = sb("ev_qT", [128, 4, 256], F32, s)
                kT = sb("ev_kT", [128, 4, 256], F32, s)
                V = sb("ev_v", [128, 2, 512], F32, s)
                U = sb("ev_u", [128, 2, 512], F32, s)
                G = sb("ev_g", [128, 2, 512], F32, s)
                tw = p.dma("pool", "d_sguw", W[:, :, :], d["small"][:, sat["sguw"][0]:sat["sguw"][1]].rearrange("p (g n) -> p g n", g=8))
                tb = p.dma("pool", "d_sgub", sbias[:, :], d["small"][:, sat["sgub"][0]:sat["sgub"][1]])
                twm = p.tt(W[:, :, :], W[:, :, :], const("tril").unsqueeze(1).broadcast_to([128, 8, 128]), ALU.mult,
                           [tw, t_const], "pool")
                turned = [None]
                ready = {}

                def evac(c, w, bs):
                    if c < 2:
                        toks = []
                        for t, (b, tok) in enumerate(bs):
                            a = p.act(Q[:, t, :], b.t[:, :], waits=[tok, turned[0]])
                            b.free = [a]
                            toks.append(a)

                        def later():
                            dst = (qT, kT)[c]
                            for t in range(2):
                                b = scratch()
                                for k in range(4):
                                    tok = p.tr(b.t[:, k * 128:(k + 1) * 128], Q[:, t, k * 128:(k + 1) * 128], ident,
                                               [toks[t], b.free], k == 3)
                                turned[0] = tok
                                ready[c, t] = p.copy(dst[:, :, t * 128:(t + 1) * 128],
                                                     b.t[:, :].rearrange("p (k n) -> p k n", k=4), [tok])
                                b.free = [ready[c, t]]

                        return later
                    for t, (b, tok) in enumerate(bs):
                        if c == 2:
                            ready["v", t] = p.act(V[:, t, :], b.t[:, :], waits=[tok])
                        else:
                            ready["ug"[c - 3], t] = p.act((U, G)[c - 3][:, t, :], b.t[:, :], ACT.Gelu_apprx_tanh, [tok])
                        b.free = [p.last["act"]]
                    return None

                x_used[0] = linear("sbg_in", lhs_of(XH, XL, got), evac)
                flush()
                gi, g, gt = gain()
                bi, bb, bt = gain()
                sgu = []
                for t in range(2):
                    a = p.emit("dve", lambda e, t=t: e.bn_stats(bn[:, t, 0, :], G[:, t, :]), [ready["g", t]])
                    a = p.emit("dve", lambda e, t=t: e.bn_aggr(mv[:, t, :], bn[:, t, 0, :]), [a])
                    r = rstd_of(mv[:, t, 1:2], 1, 1.0, 1e-6, [a])
                    m = p.stt(G[:, t, :], G[:, t, :], mv[:, t, 0:1], g, ALU.subtract, ALU.mult, [a, gt])
                    m = p.stt(G[:, t, :], G[:, t, :], mv[:, t, 1:2], bb, ALU.mult, ALU.add, [r, m, bt])
                    sgu.append(m)
                gain_done(gi, sgu[1])
                gain_done(bi, sgu[1])
                osg = [None, None]

                def spatial(t):
                    b = scratch()
                    for j in range(8):
                        tok = p.mm(b.t[:, j * 64:(j + 1) * 64], W[:, j, :], G[:, t, j * 64:(j + 1) * 64], True, True,
                                   [sgu[t], twm, b.free], j == 7)
                    for j in range(8):
                        osg[t] = p.stt(XN[:, t, 512 + j * 64:512 + (j + 1) * 64], b.t[:, j * 64:(j + 1) * 64], sbias[:, j:j + 1],
                                       U[:, t, j * 64:(j + 1) * 64], ALU.add, ALU.mult, [tok, tb, ready["u", t], xn_used[0]])
                    b.free = [osg[t]]

                spatial(0)
                spatial(1)
                Z = sb("ev_z", [128, 8, 384], F32, s)
                E = sb("ev_e", [128, 4, 384], F32, s)
                SP = sb("ev_sp", [128, 4, 384], F32, s)
                dep = [ready[c, t] for c in range(2) for t in range(2)]
                tz, tsp, tw_, tcum, tpv = {}, {}, {}, {}, {}
                ob = pair()

                def logits(h):
                    b = scratch()
                    r = slice(64 * (h % 2), 64 * (h % 2) + 64)
                    p.mm(b.t[:, 0:256], kT[r, h // 2, 0:128], qT[r, h // 2, :], True, True, [dep, b.free])
                    tok = p.mm(b.t[:, 256:384], kT[r, h // 2, 128:256], qT[r, h // 2, 128:256], True, True, inc=True)
                    a = p.stt(Z[:, h, :], b.t[:, 0:384], 0.125, const("sbmask"), ALU.mult, ALU.add, [tok, t_const])
                    b.free = [a]
                    x = p.act(E[:, h % 4, :], Z[:, h, :], ACT.Abs, [a, tsp.get(h - 4)])
                    x = p.act(E[:, h % 4, :], E[:, h % 4, :], ACT.Exp, [x], scale=-1.0)
                    x = p.act(E[:, h % 4, :], E[:, h % 4, :], ACT.Ln, [x], bias=1.0)
                    tsp[h] = p.stt(SP[:, h % 4, :], Z[:, h, :], 0.0, E[:, h % 4, :], ALU.max, ALU.add, [x, tcum.get(h - 4)])
                    tz[h] = a

                def rest(h):
                    b = scratch()
                    p.mm(b.t[:, 0:384], const("incl"), SP[:, h % 4, :], True, False, [tsp[h], b.free, t_const])
                    tcum[h] = p.mm(b.t[:, 128:256], const("ones"), SP[:, h % 4, 256:384], False, True, inc=True)
                    a = p.tt(Z[:, h, :], Z[:, h, :], b.t[:, 0:384], ALU.subtract, [tcum[h]])
                    b.free = [a]
                    tw_[h] = p.act(Z[:, h, :], Z[:, h, :], ACT.Exp, [a])

                def weigh(h):
                    c = slice(h * 64, h * 64 + 64)
                    p.mm(ob[0].t[:, c], Z[:, h, 0:128], V[:, 0, c], True, True,
                         [tw_[h], ready["v", 0], ready["v", 1], ob[0].free, ob[1].free])
                    p.mm(ob[1].t[:, c], Z[:, h, 128:256], V[:, 0, c], True, False)
                    tpv[h] = p.mm(ob[1].t[:, c], Z[:, h, 256:384], V[:, 1, c], False, True, inc=True)

                for i in range(8 + 4):
                    if i < 8:
                        logits(i)
                    if 2 <= i < 10:
                        rest(i - 2)
                    if i >= 4:
                        weigh(i - 4)
                dep2 = []
                for t in range(2):
                    a = p.copy(XN[:, t, 0:512], ob[t].t[:, :], [tpv[7], xn_used[0]])
                    ob[t].free = [a]
                    dep2.append([a, osg[t]])
                got = xn_halves(dep2)
                x_used[0] = linear("sbg_out", lhs_of(XH, XL, got), add_x)

        def mem_attention(l):
            p.fence()
            with ExitStack() as s:
                kT = sb(f"xm_kT{l}", [128, 8, 256], F32, s)
                V = sb(f"xm_v{l}", [128, 2, D], F32, s)
                qT = sb(f"xm_qT{l}", [128, 8, 256], F32, s)
                q = sb(f"xm_q{l}", [128, 2, 2, 256], F32, s)

                def qk_turn(dst, src, k0, toks, got, key):
                    b = scratch()
                    for k in range(2):
                        for t in range(2):
                            tok = p.tr(b.t[:, (2 * k + t) * 128:(2 * k + t + 1) * 128], src[:, t, k * 128:(k + 1) * 128],
                                       ident, [toks[t], b.free], k == 1 and t == 1)
                    got[key] = p.copy(dst[:, k0:k0 + 2, :], b.t[:, :].rearrange("p (k n) -> p k n", k=2), [tok])
                    b.free = [got[key]]
                    return tok

                with ExitStack() as s2:
                    MH = sb(f"xm_mh{l}", [128, 8, 256], F32R, s2)
                    ML = sb(f"xm_ml{l}", [128, 8, 256], F32R, s2)
                    M = sb(f"xm_m{l}", [128, 2, D], F32, s2)
                    gi, g, gt = gain()
                    dep = []
                    for t in range(2):
                        tm = p.dma("sp", f"d_m{l}{t}", M[:, t, :], d["mem"][t * 128:(t + 1) * 128, :],
                                   [p.last[e] for e in p.last if p.last[e]])
                        dep.append(rms(M[:, t, :], M[:, t, :], g, gt, 2 + t, D, [tm, xn_used[0]], XN[:, t, :]))
                    gain_done(gi, dep[1])
                    got = to_halves(lambda t, k: M[:, t, k * 128:(k + 1) * 128], 8, MH, ML, dep)
                    kgi, kg, kgt = gain()
                    t_k, turned, vt = {}, {}, {}

                    def evac(c, w, bs):
                        toks = []
                        for t, (b, tok) in enumerate(bs):
                            vt[c, t] = p.act(V[:, t, c * 256:(c + 1) * 256], b.t[:, 256:512], waits=[tok])
                            toks.append(rms(b.t[:, 0:256], q[:, c % 2, t, :], kg, kgt, 4 + t, 256,
                                            [tok, vt[c, t], turned.get(c - 2)], q[:, c % 2, t, :]))
                            b.free = [toks[t], vt[c, t]]

                        def later():
                            turned[c] = qk_turn(kT, q[:, c % 2, :, :], 2 * c, toks, t_k, c)

                        return later

                    linear(f"x_kv{l}", lhs_of(MH, ML, got), evac)
                got = x_norm_halves()
                flush()
                gain_done(kgi, t_k[3])
                qgi, qg, qgt = gain()
                t_q = {}

                def evac(c, w, bs):
                    toks = {}
                    for t, (b, tok) in enumerate(bs):
                        sums = [rms_sum(b.t[:, j * 256:(j + 1) * 256], 4 + 2 * t + j,
                                        [tok, turned.get(2), turned.get(3), turned.get(("q", c - 1, j))], q[:, j, t, :])
                                for j in range(2)]
                        for j in range(2):
                            toks[j, t] = rms_scale(b.t[:, j * 256:(j + 1) * 256], q[:, j, t, :], qg, qgt, 4 + 2 * t + j, 256, sums)
                        b.free = [toks[0, t], toks[1, t]]

                    def later():
                        for j in range(2):
                            turned["q", c, j] = qk_turn(qT, q[:, j, :, :], 4 * c + 2 * j, [toks[j, 0], toks[j, 1]], t_q, 2 * c + j)

                    return later

                x_used[0] = linear(f"x_q{l}", lhs_of(XH, XL, got), evac)
                flush()
                gain_done(qgi, t_q[3])

                def scores(h, i):
                    return [(qT[:, 2 * h + k, i * 128:(i + 1) * 128], kT[:, 2 * h + k, :]) for k in range(2)]

                dep = attend(f"xm{l}", 4, 256, [(0, 0, 256), (1, 256, 256)], scores,
                             lambda h, j: V[:, j, h * 256:(h + 1) * 256], 0.0625, None, None,
                             lambda t, h, n: XN[:, t, h * 256:(h + n) * 256],
                             [list(t_k.values()), list(t_q.values())], list(vt.values()))
                got = xn_halves(dep)
                x_used[0] = linear(f"x_o{l}", lhs_of(XH, XL, got), add_x)

        def angles(pos, inv, half, sn, cs, s, name):
            pi = sb(name + "pi", [128, 2], I32, s)
            pf = sb(name + "pf", [128, 2], F32, s)
            ang = sb(name + "an", [128, 2, half], F32, s)
            tmp = sb(name + "at", [128, 2, half], F32, s)
            a = p.dma("sp", "d_" + name, pi[:, :], pos, [x for x in p.last.values() if x])
            a = p.copy(pf[:, :], pi[:, :], [a])
            toks = [p.ts(ang[:, t, :], inv, pf[:, t:t + 1], ALU.mult, waits=[a, t_const]) for t in range(2)]
            return sincos(sn[:, :, :], cs[:, :, :], ang[:, :, :], tmp[:, :, :], toks)

        def rope(o1, o2, x1, x2, cs, sn, a, b, waits, e="dve"):
            t1 = p.tt(a, x1, cs, ALU.mult, waits, e)
            t2 = p.tt(b, x2, sn, ALU.mult, waits, e)
            t3 = p.tt(o1, a, b, ALU.subtract, [t1, t2, waits], e)
            t1 = p.tt(a, x1, sn, ALU.mult, [t3, waits], e)
            t2 = p.tt(b, x2, cs, ALU.mult, [t3, waits], e)
            return p.tt(o2, a, b, ALU.add, [t1, t2], e)

        def mla_mixer():
            got = x_norm_halves()
            p.fence()
            with ExitStack() as s:
                qT = sb("ml_qT", [96, 16, 256], F32, s)
                kT = sb("ml_kT", [96, 16, 256], F32, s)
                V = sb("ml_v", [128, 2, D], F32, s)
                with ExitStack() as s2:
                    Q = sb("ml_q", [128, 2, 1536], F32, s2)
                    K = sb("ml_k", [128, 2, D], F32, s2)
                    F = sb("ml_f", [128, 16, 96], F32, s2)
                    KR = sb("ml_kr", [128, 2, 32], F32, s2)
                    KE = sb("ml_ke", [128, 2, 32], F32, s2)
                    sn = sb("ml_sn", [128, 2, 16], F32, s2)
                    cs = sb("ml_cs", [128, 2, 16], F32, s2)
                    ra = sb("ml_ra", [128, 16, 16], F32, s2)
                    rb = sb("ml_rb", [128, 16, 16], F32, s2)
                    rr = sb("ml_rr", [128, 2, 2, 16], F32, s2)
                    r2 = sb("ml_r2", [128, 2, 16], F32, s2)
                    t_ang = angles(d["positions"], const("inv1"), 16, sn, cs, s2, "pos1")
                    qi, qg, qgt = gain()
                    ki, kg, kgt = gain()
                    tc = {}

                    def evac(c, w, bs):
                        for t, (b, tok) in enumerate(bs):
                            if c == 0:
                                tc["q", t] = rms(b.t[:, 0:512], XN[:, t, 0:512], qg, qgt, 8 + t, 512, [tok, xn_used[0]], XN[:, t, 0:512])
                                b.free = [tc["q", t]]
                            else:
                                tc["r", t] = p.copy(KR[:, t, :], b.t[:, 256:288], [tok])
                                tc["k", t] = rms(b.t[:, 0:256], XN[:, t, 512:768], kg, kgt, 10 + t, 256,
                                                 [tok, tc["r", t], xn_used[0]], XN[:, t, 512:768])
                                b.free = [tc["k", t], tc["r", t]]

                    x_used[0] = linear("mla_in", lhs_of(XH, XL, got), evac)
                    gain_done(qi, tc["q", 1])
                    gain_done(ki, tc["k", 1])
                    got = to_halves(lambda t, k: XN[:, t, k * 128:(k + 1) * 128], 6, XH, XL,
                                    [[tc["q", t], tc["k", t]] for t in range(2)], x_used[0])
                    xn_used[0] = p.last["pe"]
                    tq, tk, tv = {}, {}, {}

                    def evac_q(c, w, bs):
                        for t, (b, tok) in enumerate(bs):
                            tq[c, t] = p.act(Q[:, t, c * 512:(c + 1) * 512], b.t[:, :], waits=[tok])
                            b.free = [tq[c, t]]

                    def evac_kv(c, w, bs):
                        for t, (b, tok) in enumerate(bs):
                            dst, o, toks = (K, c, tk) if c < 2 else (V, c - 2, tv)
                            toks[c, t] = p.act(dst[:, t, o * 512:(o + 1) * 512], b.t[:, :], waits=[tok])
                            b.free = [toks[c, t]]

                    linear("mla_uq", lhs_of(XH, XL, got), evac_q)
                    x_used[0] = linear("mla_ukv", lhs_of(XH, XL, {(k, t): got[k + 4, t] for k in range(2) for t in range(2)}, 4), evac_kv)
                    gqi, gq, gqt = gain()
                    gki, gk, gkt = gain()
                    f_free = [None]
                    done = {}

                    def spread(m, t, lo, hi):
                        return m[:, t, lo:hi].unsqueeze(1).broadcast_to([128, 16, hi - lo])

                    def heads(m):
                        return m.unsqueeze(2)

                    def turn_f(dst, key, t, tok):
                        for g in range(4):
                            b = scratch()
                            for j in range(4):
                                x = p.tr(b.t[0:96, j * 128:(j + 1) * 128], F[:, 4 * g + j, :], ident, [tok, b.free], j == 3)
                            done[key, t, g] = p.copy(dst[:, 4 * g:4 * g + 4, t * 128:(t + 1) * 128],
                                                     b.t[0:96, :].rearrange("p (h n) -> p h n", h=4), [x])
                            b.free = [done[key, t, g]]
                        f_free[0] = x

                    g16 = lambda g, lo, hi: g[:, lo:hi].unsqueeze(1).broadcast_to([128, 16, hi - lo])
                    for t in range(2):
                        qn = Q[:, t, 0:1024].rearrange("p (h n) -> p h n", h=16)
                        qr = Q[:, t, 1024:1536].rearrange("p (h n) -> p h n", h=16)
                        dep = [tq[c, t] for c in range(3)]
                        a = p.act(F[:, :, 0:64], qn, ACT.Square, [dep, f_free[0]])
                        b = p.act(F[:, :, 64:96], qr, ACT.Square, [dep, f_free[0]])
                        r = rr[:, 0, t, :]
                        a = p.reduce(r, F[:, :, :], ALU.add, [a, b])
                        sq = a
                        a = rstd_of(r, 16, 1.0 / 96, 1e-6, [a])
                        n1 = p.tt(qn, qn, heads(r).broadcast_to([128, 16, 64]), ALU.mult, [a, sq], "pool")
                        n2 = p.tt(qr, qr, heads(r).broadcast_to([128, 16, 32]), ALU.mult, [a])
                        n1 = p.tt(F[:, :, 0:64], qn, g16(gq, 0, 64), ALU.mult, [n1, gqt])
                        n2 = p.tt(qr, qr, g16(gq, 64, 96), ALU.mult, [n2, gqt])
                        n2 = rope(F[:, :, 64:80], F[:, :, 80:96], qr[:, :, 0:16], qr[:, :, 16:32], spread(cs, t, 0, 16),
                                  spread(sn, t, 0, 16), ra[:, :, :], rb[:, :, :], [n2, t_ang])
                        turn_f(qT, "q", t, [n1, n2])
                    gain_done(gqi, p.last["dve"])
                    for t in range(2):
                        kn = K[:, t, :].rearrange("p (h n) -> p h n", h=16)
                        r, rk = rr[:, 1, t, :], st[:, 12 + t:13 + t]
                        kd = [tk[0, t], tk[1, t]]
                        a = p.act(F[:, :, 0:64], kn, ACT.Square, [kd, f_free[0]])
                        b = p.act(KE[:, t, :], KR[:, t, :], ACT.Square, [tc["r", t]], accum=rk)
                        a = p.reduce(r, F[:, :, 0:64], ALU.add, [a])
                        sq = a
                        a = p.ts(r, r, rk, ALU.add, waits=[a, b])
                        a = rstd_of(r, 16, 1.0 / 96, 1e-6, [a])
                        n1 = p.tt(kn, kn, heads(r).broadcast_to([128, 16, 64]), ALU.mult, [a, sq], "pool")
                        n1 = p.tt(F[:, :, 0:64], kn, g16(gk, 0, 64), ALU.mult, [n1, gkt])
                        n2 = p.tt(KR[:, t, :], KR[:, t, :], gk[:, 64:96], ALU.mult, [b, gkt])
                        n2 = rope(KE[:, t, 0:16], KE[:, t, 16:32], KR[:, t, 0:16], KR[:, t, 16:32], cs[:, t, :], sn[:, t, :],
                                  r2[:, 0, :], r2[:, 1, :], [n2, t_ang])
                        n2 = p.tt(F[:, :, 64:96], spread(KE, t, 0, 32), heads(r).broadcast_to([128, 16, 32]), ALU.mult, [n2, a])
                        turn_f(kT, "k", t, [n1, n2])
                    gain_done(gki, p.last["dve"])
                p.fence()

                def scores(h, i):
                    return [(qT[:, h, i * 128:(i + 1) * 128], kT[:, h, 0:128 * (i + 1)])]

                dep = attend("ml", 16, 64, [(0, 0, 128), (1, 128, 256)], scores,
                             lambda h, j: V[:, j, h * 64:(h + 1) * 64], 96.0 ** -0.5, const("causal"), t_const,
                             lambda t, h, n: XN[:, t, h * 64:(h + n) * 64], list(done.values()), list(tv.values()))
                got = xn_halves(dep)
                x_used[0] = linear("mla_out", lhs_of(XH, XL, got), add_x)

        def s5_params(s, early, small, ts_):
            lre, lim, ldt = small["lre"], small["lim"], small["ldt"]
            names = ["dt", "mag", "th", "tm", "sn", "cs", "abr", "abi", "den", "fre", "fim", "t1"]
            v = {n: sb("s5_" + n, [128, 16], F32, s)[:, :] for n in names}
            a = p.act(v["dt"], ldt, ACT.Exp, [ts_])
            l = p.ts(lre, lre, -1e-4, ALU.min, waits=[ts_])
            m = p.tt(v["mag"], lre, v["dt"], ALU.mult, [a, l])
            m = p.act(v["mag"], v["mag"], ACT.Exp, [m])
            t = p.tt(v["th"], lim, v["dt"], ALU.mult, [a])
            sc = sincos(v["sn"], v["cs"], v["th"], v["tm"], [t])
            r = p.tt(v["abr"], v["mag"], v["cs"], ALU.mult, [m, sc])
            r = p.ts(v["abr"], v["abr"], 1.0, ALU.subtract, waits=[r])
            i = p.tt(v["abi"], v["mag"], v["sn"], ALU.mult, [m, sc])
            e = p.tt(v["den"], lre, lre, ALU.mult, [l])
            f = p.tt(v["t1"], lim, lim, ALU.mult, [ts_])
            e = p.tt(v["den"], v["den"], v["t1"], ALU.add, [e, f])
            e = p.recip(v["den"], v["den"], [e])
            a1 = p.tt(v["fre"], v["abr"], lre, ALU.mult, [r, l])
            a2 = p.tt(v["t1"], v["abi"], lim, ALU.mult, [i, e])
            a1 = p.tt(v["fre"], v["fre"], v["t1"], ALU.add, [a1, a2])
            a1 = p.tt(v["fre"], v["fre"], v["den"], ALU.mult, [a1, e])
            a2 = p.tt(v["fim"], v["abi"], lre, ALU.mult, [i, l])
            a3 = p.tt(v["t1"], v["abr"], lim, ALU.mult, [r, a1])
            a2 = p.tt(v["fim"], v["fim"], v["t1"], ALU.subtract, [a2, a3])
            a2 = p.tt(v["fim"], v["fim"], v["den"], ALU.mult, [a2, e])
            cr, ci = small["cre"], small["cim"]
            ncr = sb("s5_ncr", [128, 512], F32, s)
            nci = sb("s5_nci", [128, 512], F32, s)
            tmp = sb("s5_ct", [128, 512], F32, early)
            g = lambda m: m.rearrange("p (i c) -> p i c", i=16)
            fr = v["fre"].unsqueeze(2).broadcast_to([128, 16, 32])
            fi = v["fim"].unsqueeze(2).broadcast_to([128, 16, 32])
            w = [a1, a2, ts_]
            x1 = p.tt(g(nci[:, :]), g(cr), fi, ALU.mult, w)
            x2 = p.tt(g(tmp[:, :]), g(ci), fr, ALU.mult, w)
            x1 = p.stt(nci[:, :], nci[:, :], -1.0, tmp[:, :], ALU.mult, ALU.subtract, [x1, x2])
            x3 = p.tt(g(cr), g(cr), fr, ALU.mult, [x1])
            x4 = p.tt(g(tmp[:, :]), g(ci), fi, ALU.mult, [x1, w])
            x3 = p.tt(cr, cr, tmp[:, :], ALU.subtract, [x3, x4])
            x4 = p.ts(ncr[:, :], cr, -1.0, ALU.mult, waits=[x3])
            return v["mag"], v["cs"], v["sn"], cr, ncr[:, :], nci[:, :], [x1, x3, x4], [m, sc]

        def ab_mixer():
            got = x_halves()
            p.fence()
            with ExitStack() as s:
                sat, _ = small_at()
                lo, hi = sat["convw"][0], sat["cim"][1]
                SM = sb("ab_sm", [128, hi - lo], F32, s)
                small = {n: SM[:, a - lo:b - lo] for n, (a, b) in sat.items() if lo <= a < hi}
                ts_ = p.dma("sp", "d_s5", SM[:, :], d["small"][:, lo:hi], [x for x in p.last.values() if x])
                uT = sb("ab_uT", [128, 4, 256], F32, s)
                gT = sb("ab_gT", [128, 4, 256], F32, s)
                cT = sb("ab_cT", [128, 4, 258], F32, s)
                T = sb("ab_T", [128, 2, 16, 256], F32, s)
                early = s.enter_context(ExitStack())
                mag, c1, s1, cre, ncre, ncim, t_c, t_ph = s5_params(s, early, small, ts_)
                H = sb("ab_h", [128, 2, 512], F32, early)
                B = sb("ab_b", [128, 2, 512], F32, early)
                z0 = p.memset(cT[:, :, 0:2], 0.0)
                a = p.copy(T[:, 0, :, 0], c1, [t_ph], "pool")
                b = p.copy(T[:, 1, :, 0], s1, [t_ph], "pool")
                t_T = {}
                tmp = sb("ab_tt", [128, 8, 128], F32, early)
                if True:
                    for half in range(2):
                        r = slice(8 * half, 8 * half + 8)
                        x = [a, b, p.last["pool"]]
                        for k in range(8):
                            m = 1 << k
                            R, I = T[:, 0, r, 0:m], T[:, 1, r, 0:m]
                            Br = T[:, 0, r, m - 1:m].broadcast_to([128, 8, m])
                            Bi = T[:, 1, r, m - 1:m].broadcast_to([128, 8, m])
                            oR, oI, tm = T[:, 0, r, m:2 * m], T[:, 1, r, m:2 * m], tmp[:, :, 0:m]
                            y1 = p.tt(oR, R, Br, ALU.mult, x, "pool")
                            y2 = p.tt(tm, I, Bi, ALU.mult, x, "pool")
                            y1 = p.tt(oR, oR, tm, ALU.subtract, [y1, y2], "pool")
                            y2 = p.tt(oI, R, Bi, ALU.mult, x, "pool")
                            y3 = p.tt(tm, I, Br, ALU.mult, [x, y1], "pool")
                            y2 = p.tt(oI, oI, tm, ALU.add, [y2, y3], "pool")
                            x = [y1, y2]
                        t_T[half] = x
                ready, turned = {}, {}

                def turn(src, dst, key, toks, off=0):
                    for t in range(2):
                        b = scratch()
                        for k in range(4):
                            tok = p.tr(b.t[:, k * 128:(k + 1) * 128], src[:, t, k * 128:(k + 1) * 128], ident,
                                       [toks[t], b.free], k == 3)
                        ready[key, t] = p.act(dst[:, :, off + t * 128:off + (t + 1) * 128],
                                              b.t[:, :].rearrange("p (k n) -> p k n", k=4), waits=[tok, z0])
                        b.free = [ready[key, t]]
                    turned[key] = tok

                hold = {}

                def evac(c, w, bs):
                    toks = []
                    for t, (b, tok) in enumerate(bs):
                        if c in (0, 3):
                            toks.append(p.act(B[:, t, :], b.t[:, :], waits=[tok, turned.get("u")]))
                        elif c == 1:
                            toks.append(p.act(H[:, t, :], b.t[:, :], waits=[tok]))
                        else:
                            toks.append(p.tt(H[:, t, :], b.t[:, :], H[:, t, :], ALU.mult, [tok, hold[t]]))
                        hold[t] = toks[t]
                        b.free = [toks[t]]
                    if c == 0:
                        return lambda: turn(B, uT, "u", toks)
                    if c == 2:
                        return lambda: turn(H, cT, "c", toks, 2)
                    if c == 3:
                        return lambda: turn(B, gT, "g", toks)

                x_used[0] = linear("ab_in", lhs_of(XH, XL, got), evac)
                flush()
                early.close()
                p.fence()
                dep = [ready["u", 0], ready["u", 1]]
                nb = 2
                A_ = sb("ab_A", [128, nb, 2, 256], F32, s)
                B_ = sb("ab_B", [128, nb, 2, 256], F32, s)
                W_ = B_
                C_ = sb("ab_C", [128, nb, 2, 256], F32, s)
                D_ = sb("ab_D", [128, nb, 2, 256], F32, s)
                ZH = sb("ab_zh", [128, 4, 256], F32R, s)
                ZL = sb("ab_zl", [128, 4, 256], F32R, s)
                Z = gT
                t_w, t_y, t_cd, zt = {}, {}, {}, {}
                ybanks = {}

                def state(i):
                    r = slice(32 * (i % 4), 32 * (i % 4) + 32)
                    b = scratch()
                    for j, nm in enumerate(("bre", "bim")):
                        l = small[nm].rearrange("p (k n) -> p k n", k=4)[r, i // 4, :]
                        tok = p.mm(b.t[:, j * 256:(j + 1) * 256], l, uT[r, i // 4, :], True, True, [dep, ts_, b.free], j == 1)
                    Tr = T[:, 0, i, :].unsqueeze(1).broadcast_to([128, 2, 256])
                    v = b.t[:, :].rearrange("p (j n) -> p j n", j=2)
                    n = i % nb
                    x = p.tt(A_[:, n, :, :], v, Tr, ALU.mult, [tok, t_T[i // 8], t_w.get(i - nb)])
                    y1 = p.tt(B_[:, n, 0, :], b.t[:, 256:512], T[:, 1, i, :], ALU.mult, [tok, t_cd.get(i - nb)])
                    y2 = p.tt(B_[:, n, 1, :], b.t[:, 0:256], T[:, 1, i, :], ALU.mult, [tok, t_cd.get(i - nb)])
                    b.free = [x, y1, y2]
                    x1 = p.tt(A_[:, n, 0, :], A_[:, n, 0, :], B_[:, n, 0, :], ALU.add, [x, y1])
                    x2 = p.tt(A_[:, n, 1, :], A_[:, n, 1, :], B_[:, n, 1, :], ALU.subtract, [x, y2])
                    for j, x in ((0, x1), (1, x2)):
                        t_w[i] = p.emit("dve", lambda e, j=j: e.tensor_tensor_scan(
                            W_[:, n, j, :], mag[:, i:i + 1].broadcast_to([128, 256]), A_[:, n, j, :], 0.0, ALU.mult, ALU.add),
                            [x, t_cd.get(i - nb)])
                    Ti = T[:, 1, i, :].unsqueeze(1).broadcast_to([128, 2, 256])
                    c = p.tt(C_[:, n, :, :], W_[:, n, :, :], Tr, ALU.mult, [t_w[i], t_y.get(i - nb)], "pool")
                    t_cd[i] = p.tt(D_[:, n, :, :], W_[:, n, :, :], Ti, ALU.mult, [t_w[i], t_y.get(i - nb)], "pool")

                def outputs(i):
                    if i % 4 == 0:
                        ybanks[i // 4] = banks[i // 4]
                    yb = ybanks[i // 4]
                    n, cc = i % nb, slice(32 * i, 32 * i + 32)
                    o = yb.t[32 * (i % 4):32 * (i % 4) + 32, 0:256]
                    p.mm(o, cre[:, cc], C_[:, n, 0, :], True, False, [t_cd[i], t_c, yb.free])
                    p.mm(o, ncim[:, cc], C_[:, n, 1, :], False, False)
                    p.mm(o, ncim[:, cc], D_[:, n, 0, :], False, False)
                    t_y[i] = p.mm(o, ncre[:, cc], D_[:, n, 1, :], False, True, inc=True)
                    if i % 4 == 3:
                        k = i // 4
                        a = p.stt(Z[:, k, :], uT[:, k, :], small["dskip"][:, k:k + 1], yb.t[:, 0:256], ALU.mult, ALU.add,
                                  [t_y[i], ya[k]])
                        yb.free = [a]
                        zt["z", k] = p.act(Z[:, k, :], Z[:, k, :], ACT.Gelu_apprx_tanh, [a])
                        h = p.copy(ZH[:, k, :], Z[:, k, :], [zt["z", k]])
                        l = p.tt(ZL[:, k, :], Z[:, k, :], ZH[:, k, :].bitcast(F32), ALU.subtract, [h])
                        zt[k] = l

                ya = {}
                got = {}
                cw = small["convw"].rearrange("p (k j) -> p k j", k=4)
                Y = [A_[:, 0, 0, :], A_[:, 0, 1, :]]
                cd = [ready["c", 0], ready["c", 1], ts_]
                for k in range(4):
                    y = Y[k % 2]
                    a = p.ts(y, cT[:, k, 0:256], cw[:, k, 0:1], ALU.mult, waits=[cd, ya.get(k - 2)])
                    a = p.stt(y, cT[:, k, 1:257], cw[:, k, 1:2], y, ALU.mult, ALU.add, [a])
                    a = p.stt(y, cT[:, k, 2:258], cw[:, k, 2:3], y, ALU.mult, ALU.add, [a])
                    a = p.tt(y, y, gT[:, k, :], ALU.mult, [a, ready["g", 0], ready["g", 1]])
                    h = p.act(XH[:, k, :], y, waits=[a, x_used[0]])
                    ya[k] = p.tt(XL[:, k, :], y, XH[:, k, :].bitcast(F32), ALU.subtract, [h, x_used[0]])
                    got[k, 0] = got[k, 1] = ya[k]
                t_w[-1] = t_w[-2] = ya[3]
                for i in range(16 + 1):
                    if i < 16:
                        state(i)
                    if i >= 1:
                        outputs(i - 1)
                assert plan[layer_now[0]][0] == "glu"
                layer_now[0] += 1
                gb = [banks[i] for i in range(4)]
                for c, k0, nk, w, _ in units_of(4, [512]):
                    u, wh, wl = weights(k0, nk, w)
                    for k in range(nk):
                        kt = k0 + k
                        for m in range(4):
                            ms = slice(m * 128, (m + 1) * 128)
                            o = gb[m].t[:, 0:256]
                            p.mm(o, wh[:, k, ms], ZH[:, kt, :], kt == 0, False, [zt[kt], t_split[u], gb[m].free])
                            p.mm(o, wh[:, k, ms], ZL[:, kt, :], False, False)
                            tok = p.mm(o, wl[:, k, ms], ZH[:, kt, :], False, kt == 3, inc=kt == 3 or k == nk - 1)
                            if kt == 3:
                                t_y["g", m] = tok
                    t_used[u] = tok
                for m in range(4):
                    sgm = W_[:, m % 2, m // 2, :]
                    a = p.act(sgm, gb[m].t[:, 0:256], ACT.Sigmoid, [t_y["g", m], t_cd[15]], bias=small["bglu"][:, m:m + 1])
                    gb[m].free = [a]
                    a = p.tt(sgm, sgm, Z[:, m, :], ALU.mult, [a, zt["z", m]])
                    h = p.act(XH[:, 4 + m, :], sgm, waits=[a, x_used[0]])
                    got[4 + m, 0] = got[4 + m, 1] = p.tt(XL[:, 4 + m, :], sgm, XH[:, 4 + m, :].bitcast(F32), ALU.subtract,
                                                         [h, x_used[0]])
                x_used[0] = linear("ab_out", lhs_of(XH, XL, got), full_mix)

        def dsa_mixer():
            got = x_halves()
            p.fence()
            with ExitStack() as s:
                qT = sb("ds_qT", [128, 10, 256], F32, s)
                iT = sb("ds_iT", [128, 5, 256], F32, s)
                V = sb("ds_v", [128, 2, 256], F32, s)
                acc = sb("ds_acc", [128, 384], F32, s)
                work = sb("ds_work", [128, 384], F32, s)
                wi = sb("ds_wi", [128, 2, 8], F32, s)
                with ExitStack() as s2:
                    Q = sb("ds_q", [128, 2, 1280], F32, s2)
                    I = sb("ds_i", [128, 2, 640], F32, s2)
                    sna = sb("ds_sna", [128, 2, 16], F32, s2)
                    csa = sb("ds_csa", [128, 2, 16], F32, s2)
                    sni = sb("ds_sni", [128, 2, 8], F32, s2)
                    csi = sb("ds_csi", [128, 2, 8], F32, s2)
                    tmp = sb("ds_tmp", [128, 4, 10, 16], F32, s2)
                    ta = angles(d["positions_2"], const("inva"), 16, sna, csa, s2, "posa")
                    ti = angles(d["positions_2"], const("invi"), 8, sni, csi, s2, "posi")
                    toks = {}

                    def evac(c, w, bs):
                        for t, (b, tok) in enumerate(bs):
                            if c < 2:
                                toks[c, t] = p.act(Q[:, t, c * 512:(c + 1) * 512], b.t[:, :], waits=[tok])
                            elif c == 2:
                                toks[c, t] = p.act(Q[:, t, 1024:1280], b.t[:, 0:256], waits=[tok])
                                toks["v", t] = p.act(V[:, t, :], b.t[:, 256:512], waits=[tok])
                            elif c == 3:
                                toks[c, t] = p.act(I[:, t, 0:512], b.t[:, :], waits=[tok])
                            else:
                                toks["i", t] = p.act(I[:, t, 512:576], b.t[:, 0:64], waits=[tok])
                                toks["w", t] = p.act(wi[:, t, :], b.t[:, 64:72], waits=[tok], scale=float(512.0 ** -0.5))
                            b.free = [p.last["act"]]

                    x_used[0] = linear("c_in", lhs_of(XH, XL, got), evac)
                    flush()
                    ready, dq = {}, {}
                    for t in range(2):
                        it = I[:, t, 0:576].rearrange("p (h n) -> p h n", h=9)
                        c9 = csi[:, t, :].unsqueeze(1).broadcast_to([128, 9, 8])
                        s9 = sni[:, t, :].unsqueeze(1).broadcast_to([128, 9, 8])
                        x1, x2 = it[:, :, 0:8], it[:, :, 8:16]
                        ab = [tmp[:, j, 0:9, 0:8] for j in range(4)]
                        w = [toks[3, t], toks["i", t], ti, p.last["dve"]]
                        y = [p.tt(ab[0], x1, c9, ALU.mult, w), p.tt(ab[1], x2, s9, ALU.mult, w),
                             p.tt(ab[2], x1, s9, ALU.mult, w), p.tt(ab[3], x2, c9, ALU.mult, w)]
                        o1 = p.tt(x1, ab[0], ab[1], ALU.subtract, y)
                        o2 = p.tt(x2, ab[2], ab[3], ALU.add, y)
                        cp = p.copy(I[:, t, 576:640], I[:, t, 512:576], [o1, o2])
                        for g, n in ((0, 4), (4, 1)):
                            b = scratch()
                            for k in range(n):
                                tok = p.tr(b.t[:, k * 128:(k + 1) * 128], I[:, t, (g + k) * 128:(g + k + 1) * 128], ident,
                                           [cp, b.free], k == n - 1)
                            ready[g, t] = p.act(iT[:, g:g + n, t * 128:(t + 1) * 128],
                                                b.t[:, 0:n * 128].rearrange("p (k n) -> p k n", k=n), waits=[tok])
                            b.free = [ready[g, t]]
                    idep = list(ready.values())
                    segs = [(0, 0, 128), (1, 128, 256)]
                    with ExitStack() as s3:
                        R = sb("ds_r", [128, 2, 384], F32, s3)
                        tacc = {0: None, 1: None}
                        racc = {}
                        for h in range(8):
                            b = scratch()
                            r = slice(64 * (h % 2), 64 * (h % 2) + 64)
                            for t, o, n in segs:
                                tok = p.mm(b.t[:, o:o + n], iT[r, h // 2, t * 128:(t + 1) * 128], iT[r, 4, 0:n], True, True,
                                           [idep, b.free], t == 1)
                            a = p.act(R[:, h % 2, :], b.t[:, 0:384], ACT.Relu, [tok, racc.get(h - 2)])
                            b.free = [a]
                            for t, o, n in segs:
                                base = const("causal")[:, o:o + n] if h == 0 else acc[:, o:o + n]
                                if h == 0:
                                    tacc[t] = p.ts(acc[:, o:o + n], R[:, 0, o:o + n], wi[:, t, 0:1], ALU.mult,
                                                   waits=[a, toks["w", t]])
                                else:
                                    tacc[t] = p.stt(acc[:, o:o + n], R[:, h % 2, o:o + n], wi[:, t, h:h + 1], acc[:, o:o + n],
                                                    ALU.mult, ALU.add, [a, tacc[t]])
                            racc[h] = [tacc[0], tacc[1]]
                        a = p.tt(work[:, :], acc[:, :], const("causal"), ALU.add, [tacc[0], tacc[1], t_const])
                        m8 = sb("ds_m8", [128, 2, 8], F32, s3)
                        tops = {0: a, 1: a}
                        for _ in range(8):
                            for t, o, n in segs:
                                x = p.emit("dve", lambda e, t=t, o=o, n=n: e.max(m8[:, t, :], work[:, o:o + n]), [tops[t]])
                                tops[t] = p.emit("dve", lambda e, t=t, o=o, n=n: e.match_replace(
                                    out=work[:, o:o + n], in_to_replace=m8[:, t, :], in_values=work[:, o:o + n], imm_value=GONE), [x])
                        a = p.ts(acc[:, :], work[:, :], -2.0e38, ALU.is_le, 1.0, ALU.subtract, [tops[0], tops[1]])
                        tsel = p.stt(acc[:, :], acc[:, :], -NEG, const("causal"), ALU.mult, ALU.add, [a])
                    for t in range(2):
                        qt = Q[:, t, :].rearrange("p (h n) -> p h n", h=10)
                        c10 = csa[:, t, :].unsqueeze(1).broadcast_to([128, 10, 16])
                        s10 = sna[:, t, :].unsqueeze(1).broadcast_to([128, 10, 16])
                        x1, x2 = qt[:, :, 0:16], qt[:, :, 16:32]
                        ab = [tmp[:, j, :, :] for j in range(4)]
                        w = [[toks[c, t] for c in range(3)], ta, o1, o2, p.last["pool"], p.last["dve"]]
                        y = [p.tt(ab[0], x1, c10, ALU.mult, w, "pool"), p.tt(ab[1], x2, s10, ALU.mult, w, "pool"),
                             p.tt(ab[2], x1, s10, ALU.mult, w, "pool"), p.tt(ab[3], x2, c10, ALU.mult, w, "pool")]
                        q1 = p.tt(x1, ab[0], ab[1], ALU.subtract, y, "pool")
                        q2 = p.tt(x2, ab[2], ab[3], ALU.add, y, "pool")
                        for g in (0, 4, 8):
                            n = min(4, 10 - g)
                            b = scratch()
                            for k in range(n):
                                tok = p.tr(b.t[:, k * 128:(k + 1) * 128], Q[:, t, (g + k) * 128:(g + k + 1) * 128], ident,
                                           [q1, q2, b.free], k == n - 1)
                            dq[g, t] = p.act(qT[:, g:g + n, t * 128:(t + 1) * 128],
                                             b.t[:, 0:n * 128].rearrange("p (k n) -> p k n", k=n), waits=[tok])
                            b.free = [dq[g, t]]
                p.fence()

                def scores(h, i):
                    return [(qT[:, h, i * 128:(i + 1) * 128], qT[:, 8 + h // 4, 0:128 * (i + 1)])]

                dep = attend("ds", 8, 128, segs, scores, lambda h, j: V[:, j, (h // 4) * 128:(h // 4 + 1) * 128],
                             128.0 ** -0.5, acc[:, :], tsel, lambda t, h, n: XN[:, t, h * 128:(h + n) * 128],
                             list(dq.values()), [toks["v", 0], toks["v", 1]])
                got = xn_halves(dep)
                x_used[0] = linear("c_out", lhs_of(XH, XL, got), full_mix)

        def embed(l):
            p.fence()
            with ExitStack() as s:
                sat, _ = small_at()
                a0, b0 = sat[f"pt{l}"]
                PT = sb(f"pl_p{l}", [128, 2, 256], F32, s)
                PH = sb(f"pl_h{l}", [128, 2, 256], F32R, s)
                PL = sb(f"pl_l{l}", [128, 2, 256], F32R, s)
                PJ = sb(f"pl_j{l}", [128, 2, D], F32, s)
                tp = p.dma("sp", f"d_p{l}", PT[:, :, :], d["small"][:, a0:b0].rearrange("p (k n) -> p k n", k=2),
                           [x for x in p.last.values() if x])
                h = p.act(PH[:, :, :], PT[:, :, :], waits=[tp])
                h = p.tt(PL[:, :, :], PT[:, :, :], PH[:, :, :].bitcast(F32), ALU.subtract, [h])
                tj = {}

                def evac_p(c, w, bs):
                    for t, (b, tok) in enumerate(bs):
                        tj[c, t] = p.act(PJ[:, t, c * 512:(c + 1) * 512], b.t[:, :], waits=[tok])
                        b.free = [tj[c, t]]

                linear(f"ple_p{l}", lhs_of(PH, PL, {(k, t): h for k in range(2) for t in range(2)}), evac_p)
                got = x_halves()

                def evac_g(c, w, bs):
                    for t, (b, tok) in enumerate(bs):
                        cols = slice(c * 512, (c + 1) * 512)
                        a = p.act(XN[:, t, cols], b.t[:, :], ACT.Sigmoid, [tok, xn_used[0]])
                        b.free = [a]
                        a = p.tt(XN[:, t, cols], XN[:, t, cols], PJ[:, t, cols], ALU.mult, [a, tj[c, t]])
                        xt[t] = p.tt(X[:, t, cols], X[:, t, cols], XN[:, t, cols], ALU.add, [a, xt[t], x_used[0]])

                x_used[0] = linear(f"ple_g{l}", lhs_of(XH, XL, got), evac_g)

        for l in range(2):
            ffn(f"gu_pre{l}", f"dn_pre{l}", x_norm_halves(), half_add)
            (even_mixer, mla_mixer)[l]()
            mem_attention(l)
            ffn(f"gu_post{l}", f"dn_post{l}", x_norm_halves(), half_add)
        for l in range(2):
            ffn(f"w13_{l}_0", f"w2_{l}_0", x_halves(), half_mix)
            layer_norm()
            (ab_mixer, dsa_mixer)[l]()
            layer_norm()
            ffn(f"w13_{l}_1", f"w2_{l}_1", x_halves(), half_mix)
            layer_norm()
            embed(l)
        t_out = [p.dma("sp", f"d_o{t}", out[t * 128:(t + 1) * 128, :], X[:, t, :], [xt[t]]) for t in range(2)]
        p.wait("sp", t_out)
        assert unit_now[0] == len(stream) and layer_now[0] == len(plan) and gain_now[0] == len(gains)

        block = ctx.enter_context(nc.Block())

        @block.sync
        def _(eng):
            for f in p.queue["sp"]:
                f(eng)

        @block.scalar
        def _(eng):
            for f in p.queue["act"]:
                f(eng)

        @block.vector
        def _(eng):
            for f in p.queue["dve"]:
                f(eng)

        @block.gpsimd
        def _(eng):
            for f in p.queue["pool"]:
                f(eng)

        @block.tensor
        def _(eng):
            for f in p.queue["pe"]:
                f(eng)


def interleave(a, b):
    k, n = a.shape
    return np.stack([a.reshape(k, n // 256, 256), b.reshape(k, n // 256, 256)], 2).reshape(k, 2 * n)


def lay_weights(v):
    m = {}
    for l in range(2):
        for k, n in (("pre", "ffn_pre"), ("post", "ffn_post")):
            gu = v[n + "_w_gu"][l]
            m[f"gu_{k}{l}"] = interleave(gu[:, :FF], gu[:, FF:])
            m[f"dn_{k}{l}"] = v[n + "_w_down"][l]
        m[f"x_kv{l}"], m[f"x_q{l}"], m[f"x_o{l}"] = v["xmem_wkv"][l], v["xmem_wq"][l], v["xmem_wo"][l]
        for j in range(2):
            m[f"w13_{l}_{j}"] = interleave(v["ffn_w1_2"][l, j], v["ffn_w3_2"][l, j])
            m[f"w2_{l}_{j}"] = v["ffn_w2_2"][l, j]
        m[f"ple_p{l}"], m[f"ple_g{l}"] = v["ple_w_proj_2"][l], v["ple_w_gate_2"][l]
    m["sbg_in"], m["sbg_out"] = v["sbg_w_in"][0], v["sbg_w_out"][0]
    m["mla_in"], m["mla_out"] = v["mla_w_in"][0], v["mla_w_out"][0]
    uq = v["mla_w_uq"][0].reshape(512, 16, 96)
    m["mla_uq"] = np.concatenate([uq[:, :, :64].reshape(512, 1024), uq[:, :, 64:].reshape(512, 512)], 1)
    ukv = v["mla_w_ukv"][0].reshape(256, 16, 128)
    m["mla_ukv"] = np.concatenate([ukv[:, :, :64].reshape(256, 1024), ukv[:, :, 64:].reshape(256, 1024)], 1)
    ab = v["ab_w_in_2"][0]
    m["ab_in"] = np.concatenate([ab[:, 1536:2048], ab[:, 0:512], ab[:, 1024:1536], ab[:, 512:1024]], 1)
    m["ab_out"], m["glu"] = v["ab_w_out_2"][0], v["s5_w_glu_2"][0]
    m["c_in"], m["c_out"] = v["c_w_in_2"][0], v["c_w_out_2"][0]
    out = {}
    for name, kts, widths in layers():
        w = m[name].reshape(kts, 128, -1)
        flat = np.empty(w.size, w.dtype)
        o = 0
        for _, k, nk, width, col in units_of(kts, widths):
            n = nk * 128 * width
            flat[o:o + n].reshape(128, nk, width)[...] = w[k:k + nk, :, col:col + width].transpose(1, 0, 2)
            o += n
        out["w_" + name] = flat
    return out


def lay_small(v):
    f = np.float32
    p = {}
    p["sguw"] = v["sgu_w"][0].transpose(2, 0, 1).reshape(128, 1024)
    p["sgub"] = v["sgu_b"][0].T
    p["convw"] = v["conv_w_2"][0].T.reshape(4, 128, 3).transpose(1, 0, 2).reshape(128, 12)
    p["dskip"] = v["s5_d_2"][0].reshape(4, 128).T
    p["bglu"] = v["s5_b_glu_2"][0].reshape(4, 128).T
    p["lre"] = v["s5_lam_re_2"][0].reshape(16, 128).T
    p["lim"] = v["s5_lam_im_2"][0].reshape(16, 128).T
    p["ldt"] = np.repeat(v["s5_log_dt_2"][0], 64).reshape(16, 128).T
    for n in ("re", "im"):
        b = np.zeros((4, 4, 2, 16, 2, 64), f)
        c = np.zeros((2, 64, 16, 2, 16), f)
        src = v[f"s5_b_{n}_2"][0].reshape(4, 4, 2, 64, 16)
        cs = v[f"s5_c_{n}_2"][0].reshape(16, 2, 16, 64)
        for g in range(2):
            b[:, :, g, :, g, :] = src[:, :, g].transpose(0, 1, 3, 2)
            c[g, :, :, g, :] = cs[:, g].transpose(2, 0, 1)
        p["b" + n] = b.reshape(4, 128, 128).transpose(1, 0, 2).reshape(128, 512)
        p["c" + n] = c.reshape(128, 512)
    for l in range(2):
        p[f"pt{l}"] = v["p_2"][l, 0].T.reshape(2, 128, 256).transpose(1, 0, 2).reshape(128, 512)
    return np.concatenate([p[n].astype(f, copy=False) for n, _ in SMALL], 1)


GAINS = ["ffn_pre_norm", "mix_norm", "sgu_ln_gain", "sgu_ln_bias", "mla_q_lora_gain", "mla_kv_lora_gain",
         "mla_q_gain", "mla_k_gain", "xmem_mem_norm", "xmem_k_gain", "xmem_norm", "xmem_q_gain", "ffn_post_norm",
         "ln_g_2", "ln_b_2"]


def kernel(**inputs):
    import concourse.bacc as bacc
    from concourse.bass_utils import run_bass_kernel_spmd

    v = {k: np.asarray(a) for k, a in inputs.items()}
    arrays = lay_weights(v)
    arrays["small"] = lay_small(v)
    arrays["consts"] = consts()[0]
    arrays["x"], arrays["mem"] = v["x"][0], v["mem"][0]
    for n in ("positions", "positions_2"):
        arrays[n] = v[n].reshape(2, 128).T
    for n in GAINS:
        arrays[n] = v[n]
    arrays = {n: np.ascontiguousarray(a) for n, a in arrays.items()}
    nc = bacc.Bacc("TRN2", target_bir_lowering=False, num_devices=1)
    d = {n: nc.dram_tensor("in_" + n, a.shape, mybir.dt.from_np(a.dtype), kind="ExternalInput").ap()
         for n, a in arrays.items()}
    out = nc.dram_tensor("out", (256, D), F32, kind="ExternalOutput").ap()
    build(nc, d, out)
    r = run_bass_kernel_spmd(nc, [{"in_" + n: a for n, a in arrays.items()}], core_ids=[0])
    return r.results[0]["out"].reshape(1, 256, D)
```

```python
from contextlib import ExitStack

import numpy as np

import concourse.bass as bass
from concourse import mybir

F32 = mybir.dt.float32
F32R = mybir.dt.float32r
I32 = mybir.dt.int32
ALU = mybir.AluOpType
ACT = mybir.ActivationFunctionType
AX = mybir.AxisListType

D = 1024
FF = 2816
UNIT = 1024
RAW = 4
SPLIT = 4
AHEAD = 2
RING = 3
NEG = -1.0e30
GONE = -3.0e38
ALPHA = 4.0 ** 0.25
MAGIC = 12582912.0
TWO_PI = (6.28125, 2029.0 / 2 ** 20, 2 * np.pi - 6.28125 - 2029.0 / 2 ** 20)

FFN_GU = [512] * 11
HALVES = [512, 512]


def layers():
    out = []
    for l in range(2):
        out += [(f"gu_pre{l}", 8, FFN_GU), (f"dn_pre{l}", 22, HALVES)]
        if l == 0:
            out += [("sbg_in", 8, [512] * 5), ("sbg_out", 8, HALVES)]
        else:
            out += [("mla_in", 8, [512, 288]), ("mla_uq", 4, [384] * 4), ("mla_ukv", 2, [512] * 4),
                    ("mla_out", 8, HALVES)]
        out += [(f"x_kv{l}", 8, [512] * 4), (f"x_q{l}", 8, HALVES), (f"x_o{l}", 8, HALVES)]
        out += [(f"gu_post{l}", 8, FFN_GU), (f"dn_post{l}", 22, HALVES)]
    for l in range(2):
        out += [(f"w13_{l}_0", 8, FFN_GU), (f"w2_{l}_0", 22, HALVES)]
        if l == 0:
            out += [("ab_in", 8, [512] * 4), ("glu", 4, [512]), ("ab_out", 8, HALVES)]
        else:
            out += [("c_in", 8, [512, 72] + [512] * 3), ("c_out", 8, HALVES)]
        out += [(f"w13_{l}_1", 8, FFN_GU), (f"w2_{l}_1", 22, HALVES)]
        out += [(f"ple_p{l}", 2, HALVES), (f"ple_g{l}", 8, HALVES)]
    return out


def units_of(kts, widths):
    out, col = [], 0
    for c, w in enumerate(widths):
        n = max(1, UNIT // w)
        for k in range(0, kts, n):
            out.append((c, k, min(n, kts - k), w, col))
        col += w
    return out


CONSTS = ["ident", "incl", "ones", "tril", "sbmask", "causal", "inv1", "inva", "invi"]


def consts():
    i = np.arange(128)
    k, q = i[:, None], np.arange(256)[None, :]
    ident = np.eye(128)
    incl = (i[:, None] >= i[None, :]) * 1.0
    tril = (i[:, None] <= i[None, :]) * 1.0
    sbmask = np.concatenate([np.where(k < q, 0.0, NEG), np.where(k < i[None, :], 0.0, NEG)], 1)
    causal = np.concatenate([np.where(i[None, :] <= k, 0.0, NEG), np.where(q <= k + 128, 0.0, NEG)], 1)

    def inv(theta, half):
        e = -np.arange(half, dtype=np.float32) / np.float32(half)
        return np.broadcast_to(np.float32(theta) ** e, (128, half))

    parts = [ident, incl, np.ones((128, 128)), tril, sbmask, causal,
             inv(10000.0, 16), inv(500000.0, 16), inv(500000.0, 8)]
    at, o = {}, 0
    for name, p in zip(CONSTS, parts):
        at[name] = (o, o + p.shape[1])
        o += p.shape[1]
    return np.concatenate([p.astype(np.float32) for p in parts], 1), at


SMALL = [("sguw", 1024), ("sgub", 8), ("convw", 12), ("dskip", 4), ("bglu", 4),
         ("lre", 16), ("lim", 16), ("ldt", 16), ("bre", 512), ("bim", 512), ("cre", 512), ("cim", 512),
         ("pt0", 512), ("pt1", 512)]


def small_at():
    at, o = {}, 0
    for name, w in SMALL:
        at[name] = (o, o + w)
        o += w
    return at, o


class Program:

    def __init__(self, nc, ctx):
        self.nc = nc
        self.ctx = ctx
        self.queue = {e: [] for e in ("pe", "act", "dve", "pool", "sp")}
        self.sem = {e: ctx.enter_context(nc.semaphore("s_" + e)) for e in ("pe", "act", "dve", "pool")}
        self.count = {}
        self.seen = {e: {} for e in self.queue}
        self.last = {e: None for e in ("pe", "act", "dve", "pool")}

    def wait(self, e, waits):
        need = {}

        def gather(x):
            if x is None:
                return
            if isinstance(x, tuple) and len(x) == 2 and isinstance(x[0], str):
                need[x[0]] = max(need.get(x[0], 0), x[1])
            else:
                for y in x:
                    gather(y)

        gather(waits)
        for s, v in need.items():
            if self.seen[e].get(s, 0) < v:
                self.seen[e][s] = v
                self.queue[e].append(lambda eng, s=s, v=v: eng.wait_ge(self.sem[s], v))

    def emit(self, e, fn, waits=(), inc=True):
        self.wait(e, waits)
        if not inc:
            self.queue[e].append(lambda eng: fn(eng))
            return None
        self.count[e] = self.count.get(e, 0) + 1
        self.queue[e].append(lambda eng: fn(eng).then_inc(self.sem[e], 1))
        self.last[e] = (e, self.count[e])
        return self.last[e]

    def dma(self, e, s, out, in_, waits=()):
        if s not in self.sem:
            self.sem[s] = self.ctx.enter_context(self.nc.semaphore(s))
        self.wait(e, waits)
        self.count[s] = self.count.get(s, 0) + 16
        self.queue[e].append(lambda eng: eng.dma_start(out, in_).then_inc(self.sem[s], 16))
        return (s, self.count[s])

    def fence(self):
        done = [t for t in self.last.values() if t]
        for e in ("act", "dve", "pool"):
            self.wait(e, done)

    def act(self, out, in_, func=ACT.Copy, waits=(), bias=0.0, scale=1.0, accum=None):
        if func == ACT.Copy:
            return self.emit("act", lambda e: e.activation(out, in_, func, scale=scale), waits)
        if accum is None:
            return self.emit("act", lambda e: e.activation(out, in_, func, bias=bias, scale=scale), waits)
        return self.emit("act", lambda e: e.activation(out, in_, func, bias=bias, scale=scale, accum_out=accum), waits)

    def tt(self, out, a, b, op, waits=(), e="dve"):
        return self.emit(e, lambda g: g.tensor_tensor(out, a, b, op), waits)

    def ts(self, out, a, s1, op0, s2=None, op1=ALU.bypass, waits=(), e="dve"):
        if s2 is None:
            return self.emit(e, lambda g: g.tensor_scalar(out, a, s1, None, op0), waits)
        return self.emit(e, lambda g: g.tensor_scalar(out, a, s1, s2, op0, op1), waits)

    def stt(self, out, a, s, b, op0, op1, waits=()):
        return self.emit("dve", lambda g: g.scalar_tensor_tensor(out=out, in0=a, scalar=s, in1=b, op0=op0, op1=op1), waits)

    def copy(self, out, a, waits=(), e="dve"):
        return self.emit(e, lambda g: g.tensor_copy(out, a), waits)

    def recip(self, out, a, waits=()):
        return self.emit("dve", lambda g: g.reciprocal(out, a), waits)

    def reduce(self, out, a, op, waits=(), negate=False):
        return self.emit("dve", lambda g: g.tensor_reduce(out, a, AX.X, op, negate=negate), waits)

    def memset(self, out, v, waits=(), e="dve"):
        return self.emit(e, lambda g: g.memset(out, v), waits)

    def mm(self, out, l, r, start, stop, waits=(), inc=False):
        return self.emit("pe", lambda e: e.matmul(out, l, r, start=start, stop=stop), waits, inc)

    def tr(self, out, in_, ident, waits=(), inc=False):
        return self.emit("pe", lambda e: e.transpose(out, in_, ident), waits, inc)


class Bank:
    def __init__(self, t):
        self.t = t
        self.free = []


def build(nc, d, out, order=None):
    shape_of = {name: (kts, widths) for name, kts, widths in layers()}
    taken = []
    ctx = ExitStack()
    with ctx:
        p = Program(nc, ctx)

        def sb(name, shape, dt=F32, where=None):
            return (where or ctx).enter_context(nc.sbuf_tensor(name, shape, dt))

        X = sb("X", [128, 2, D])
        XN = sb("XN", [128, 2, D])
        XH = sb("XH", [128, 8, 256], F32R)
        XL = sb("XL", [128, 8, 256], F32R)
        raw = [sb(f"raw{i}", [128, UNIT]) for i in range(RAW)]
        whi = [sb(f"whi{i}", [128, UNIT], F32R) for i in range(SPLIT)]
        wlo = [sb(f"wlo{i}", [128, UNIT], F32R) for i in range(SPLIT)]
        gain_sb = [sb(f"gain{i}", [128, D]) for i in range(RING)]
        cat, cn = consts()[1], consts()[0].shape[1]
        C = sb("C", [128, cn])
        st = sb("st", [128, 64])
        banks = [Bank(ctx.enter_context(nc.psum_tensor(f"bank{i}", [128, 512], F32))) for i in range(8)]
        turn = [0, 0]
        spare = [4, 5, 6, 7]
        held = [False, False]

        def const(name):
            a, b = cat[name]
            return C[:, a:b]

        tx = [p.dma("sp", f"d_x{t}", X[:, t, :], d["x"][t * 128:(t + 1) * 128, :]) for t in range(2)]
        ident = const("ident")

        def scratch():
            turn[0] += 1
            return banks[spare[turn[0] % len(spare)]]

        def pair():
            turn[1] += 1
            i = turn[1] % 2 if not held[turn[1] % 2] else 1 - turn[1] % 2
            assert not held[i]
            held[i] = True
            return banks[2 * i], banks[2 * i + 1]

        def close(bs):
            held[0 if bs[0] is banks[0] else 1] = False

        stream = []
        for name, i in order or ():
            us = units_of(*shape_of[name])
            stream.append((name, 128 * sum(u[2] * u[3] for u in us[:i]), us[i][2] * us[i][3]))
        t_load, t_split, t_used = {}, {}, {}

        def load(u):
            if u >= len(stream):
                return
            name, off, n = stream[u]
            t_load[u] = p.dma("sp", f"d_raw{u % RAW}", raw[u % RAW][:, 0:n],
                              d["w_" + name][off:off + 128 * n].rearrange("(p w) -> p w", p=128),
                              [t_split[u - RAW]] if u >= RAW else [])

        split_next = [0]

        def split_to(u):
            while split_next[0] <= min(u, len(stream) - 1):
                v = split_next[0]
                n = stream[v][2]
                src, hi, lo = raw[v % RAW][:, 0:n], whi[v % SPLIT][:, 0:n], wlo[v % SPLIT][:, 0:n]
                free = t_used[v - SPLIT] if v >= SPLIT else None
                th = p.act(hi, src, waits=[t_load[v], free])
                t_split[v] = p.tt(lo, src, hi.bitcast(F32), ALU.subtract, [th, t_load[v], free])
                load(v + RAW)
                split_next[0] += 1

        pending = []

        def flush():
            todo, pending[:] = list(pending), []
            for f in todo:
                f()

        def weights(name, i, nk, w):
            u = len(taken)
            taken.append((name, i))
            if order is None:
                t_split[u] = None
            else:
                assert order[u] == (name, i)
                split_to(u + AHEAD)
            hi = whi[u % SPLIT][:, 0:nk * w].rearrange("p (k w) -> p k w", k=nk)
            lo = wlo[u % SPLIT][:, 0:nk * w].rearrange("p (k w) -> p k w", k=nk)
            return u, hi, lo

        def steps(name, lhs, evac):
            kts, widths = shape_of[name]
            us = units_of(kts, widths)
            for c, w in enumerate(widths):
                bs = pair()
                toks = [None, None]
                mine = [(i, x) for i, x in enumerate(us) if x[0] == c]
                for j, (i, (_, k0, nk, _, _)) in enumerate(mine):
                    u, hi, lo = weights(name, i, nk, w)
                    for k in range(nk):
                        kt = k0 + k
                        for t in range(2):
                            xh, xl, dep = lhs(kt, t)
                            o = bs[t].t[:, 0:w]
                            p.mm(o, xh, hi[:, k, :], kt == 0, False, [dep, t_split[u], bs[t].free])
                            p.mm(o, xh, lo[:, k, :], False, False)
                            toks[t] = p.mm(o, xl, hi[:, k, :], False, kt == kts - 1,
                                           inc=kt == kts - 1 or k == nk - 1)
                    t_used[u] = toks[1]
                    if j == min(1, len(mine) - 1):
                        flush()
                    if j < len(mine) - 1:
                        yield
                later = evac(c, w, [(bs[t], toks[t]) for t in range(2)])
                close(bs)
                if later:
                    pending.append(later)
                yield

        def linear(name, lhs, evac, between=None):
            for i, _ in enumerate(steps(name, lhs, evac)):
                if between:
                    between(i)
            return t_used[len(taken) - 1] if not between else p.last["pe"]

        fillers = []

        def fill(chunks):
            while chunks and fillers:
                for _ in range(4):
                    if next(fillers[0], "end") == "end":
                        fillers.pop(0)
                        break
                chunks -= 1

        x_used = [None]

        def to_halves(src, kts, hi, lo, dep, war=None, first=0):
            got = {}
            for t in range(2):
                for g in range(0, kts, 4):
                    n = min(4, kts - g)
                    b = scratch()
                    for k in range(n):
                        tok = p.tr(b.t[:, k * 128:(k + 1) * 128], src(t, g + k), ident,
                                   [dep[t], b.free, t_const], k == n - 1)
                    v = b.t[:, 0:n * 128].rearrange("p (k n) -> p k n", k=n)
                    h = hi[:, first + g:first + g + n, t * 128:(t + 1) * 128]
                    th = p.act(h, v, waits=[tok, war])
                    tl = p.tt(lo[:, first + g:first + g + n, t * 128:(t + 1) * 128], v, h.bitcast(F32),
                              ALU.subtract, [th, war])
                    b.free = [tl]
                    for k in range(n):
                        got[g + k, t] = tl
            return got

        def lhs_of(hi, lo, got, first=0):
            return lambda kt, t: (hi[:, first + kt, t * 128:(t + 1) * 128],
                                  lo[:, first + kt, t * 128:(t + 1) * 128], got[kt, t])

        gains = [d["ffn_pre_norm"][0]]
        for l in range(2):
            gains += [d["xmem_mem_norm"][l], d["mix_norm"][l], d["xmem_norm"][l], d["ffn_post_norm"][l]]
            if l == 0:
                gains += [d["ffn_pre_norm"][1]]
        for l in range(2):
            for j in range(3):
                gains += [d["ln_g_2"][l, j], d["ln_b_2"][l, j]]
        gain_tok, gain_now = {}, [0]

        def gain_load(i, waits=()):
            if i < len(gains):
                n = gains[i].shape[0]
                gain_tok[i] = p.dma("sp", f"d_gain{i % RING}", gain_sb[i % RING][:, 0:n], gains[i].partition_broadcast(128), waits)

        gain_load(0)
        t_const = p.dma("sp", "d_const", C[:, :], d["consts"])
        for u in range(RAW):
            load(u)
        for i in range(1, RING):
            gain_load(i)

        def gain():
            i = gain_now[0]
            gain_now[0] += 1
            return i, gain_sb[i % RING][:, 0:gains[i].shape[0]], gain_tok[i]

        def gain_done(i, tok):
            gain_load(i + RING, [tok])

        def row(name, src, s):
            n = src.shape[0]
            m = sb("row_" + name, [128, n], F32, s)
            return m[:, :], p.dma("sp", "d_row_" + name, m[:, :], src.partition_broadcast(128), [x for x in p.last.values() if x])

        def rstd_of(ss, n, inv_n, eps, waits):
            a = p.ts(ss, ss, inv_n, ALU.mult, eps, ALU.add, waits)
            b = p.act(ss, ss, ACT.Sqrt, [a])
            return p.recip(ss, ss, [b])

        def rms(src, dst, g, gt, col, n, waits, junk, eps=1e-6):
            a = rms_sum(src, col, waits, junk)
            return rms_scale(src, dst, g, gt, col, n, [a], eps)

        def rms_sum(src, col, waits, junk):
            return p.act(junk, src, ACT.Square, waits, accum=st[:, col:col + 1])

        def rms_scale(src, dst, g, gt, col, n, a, eps=1e-6):
            s = st[:, col:col + 1]
            r = rstd_of(s, 1, 1.0 / n, eps, [a])
            return p.stt(dst, src, s, g, ALU.mult, ALU.mult, [r, gt, a])

        xt = tx

        xn_used = [None]
        part = sb("part", [128, 2, 2])
        root = sb("root", [128, 2])
        junk = sb("junk", [128, 2, 512])
        norm = {}
        junk_tok = [None, None]

        def square(i, src, total, waits):
            junk_tok[i] = p.act(junk[:, i, 0:src.shape[1]], src, ACT.Square, [waits, junk_tok[i]], accum=total)
            return junk_tok[i]

        def norm_open():
            norm.clear()
            norm["i"], norm["g"], norm["gt"] = gain()
            norm["got"] = {}
            norm["war"] = x_used[0]

        def norm_piece(c):
            cols = slice(c * 512, (c + 1) * 512)
            toks = []
            for t in range(2):
                toks.append(p.tt(XN[:, t, cols], X[:, t, cols], norm["g"][:, cols], ALU.mult,
                                 [xt[t], norm["gt"], xn_used[0]]))
                norm["s", t, c] = square(t, X[:, t, cols], part[:, c, t:t + 1], [xt[t], norm.get("r")])
            norm["m", c] = toks

            def later():
                norm["got"].update(turn_piece(XN, c, toks, XH, XL, norm["war"]))
                xn_used[0] = p.last["pe"]

            return later

        def norm_close():
            gain_done(norm["i"], norm["m", 1])
            a = p.tt(root[:, :], part[:, 0, :], part[:, 1, :], ALU.add, [norm["s", t, c] for t in range(2) for c in range(2)])
            norm["r"] = rstd_of(root[:, :], 2, 1.0 / D, 1e-6, [a])
            return norm["r"], lhs_of(XH, XL, norm["got"])

        def turn_piece(src, c, toks, hi, lo, war):
            got = {}
            for t in range(2):
                b = scratch()
                for k in range(4):
                    tok = p.tr(b.t[:, k * 128:(k + 1) * 128], src[:, t, c * 512 + k * 128:c * 512 + (k + 1) * 128], ident,
                               [toks[t], b.free, t_const], k == 3)
                v = b.t[:, :].rearrange("p (k n) -> p k n", k=4)
                h = hi[:, 4 * c:4 * c + 4, t * 128:(t + 1) * 128]
                th = p.act(h, v, waits=[tok, war])
                tl = p.tt(lo[:, 4 * c:4 * c + 4, t * 128:(t + 1) * 128], v, h.bitcast(F32), ALU.subtract, [th, war])
                b.free = [tl]
                for k in range(4):
                    got[4 * c + k, t] = tl
            return got

        def xn_halves(dep, hi, lo):
            got = to_halves(lambda t, k: XN[:, t, k * 128:(k + 1) * 128], 8, hi, lo, dep, x_used[0])
            xn_used[0] = p.last["pe"]
            return lhs_of(hi, lo, got)

        def add_x(c, w, bs):
            for t, (b, tok) in enumerate(bs):
                xs = X[:, t, c * 512:c * 512 + w]
                xt[t] = p.tt(xs, b.t[:, 0:w], xs, ALU.add, [tok, xt[t]])
                b.free = [xt[t]]
            return norm_piece(c)

        phase = [0]

        def ffn(gu, dn, lhs, root_tok, post, opens=None, between=None, between_dn=None):
            phase[0] += 1
            n = phase[0]
            p.fence()
            with ExitStack() as s:
                HH = sb(f"HH{n}", [128, 22, 256], F32R, s)
                HL = sb(f"HL{n}", [128, 22, 256], F32R, s)
                sg = sb(f"sg{n}", [128, 2, 2, 256], F32, s)
                hb = sb(f"hb{n}", [128, 2, 2, 256], F32, s)
                ready, turned = {}, {}

                def evac(c, w, bs):
                    toks = []
                    for t, (b, tok) in enumerate(bs):
                        a = p.act(sg[:, c % 2, t, :], b.t[:, 0:256], ACT.Silu, [tok, turned.get(c - 2), root_tok],
                                  scale=root[:, t:t + 1] if root_tok else 1.0)
                        if root_tok:
                            h = p.stt(hb[:, c % 2, t, :], b.t[:, 256:512], root[:, t:t + 1], sg[:, c % 2, t, :],
                                      ALU.mult, ALU.mult, [a, tok, turned.get(c - 2)])
                        else:
                            h = p.tt(hb[:, c % 2, t, :], sg[:, c % 2, t, :], b.t[:, 256:512], ALU.mult,
                                     [a, tok, turned.get(c - 2)])
                        b.free = [h]
                        toks.append(h)

                    def later():
                        b = scratch()
                        for k in range(2):
                            for t in range(2):
                                tok = p.tr(b.t[:, (2 * k + t) * 128:(2 * k + t + 1) * 128],
                                           hb[:, c % 2, t, k * 128:(k + 1) * 128], ident,
                                           [toks[t], b.free], k == 1 and t == 1)
                        turned[c] = tok
                        v = b.t[:, :].rearrange("p (k n) -> p k n", k=2)
                        hh = HH[:, 2 * c:2 * c + 2, :]
                        th = p.act(hh, v, waits=[tok])
                        tl = p.tt(HL[:, 2 * c:2 * c + 2, :], v, hh.bitcast(F32), ALU.subtract, [th])
                        b.free = [tl]
                        ready[2 * c] = ready[2 * c + 1] = tl

                    return later

                x_used[0] = linear(gu, lhs, evac, between)
                if opens:
                    opens()

                def hidden(kt, t):
                    return HH[:, kt, t * 128:(t + 1) * 128], HL[:, kt, t * 128:(t + 1) * 128], ready[kt]

                linear(dn, hidden, post, between_dn)

        def half_add(c, w, bs):
            for t, (b, tok) in enumerate(bs):
                xs = X[:, t, c * 512:c * 512 + w]
                xt[t] = p.stt(xs, b.t[:, 0:w], 0.5, xs, ALU.mult, ALU.add, [tok, xt[t]])
                b.free = [xt[t]]
            return norm_piece(c) if norm else None

        def half_mix(c, w, bs, half=0.5):
            for t, (b, tok) in enumerate(bs):
                xs, tmp = X[:, t, c * 512:c * 512 + w], XN[:, t, c * 512:c * 512 + w]
                a = p.act(tmp, b.t[:, 0:w], waits=[tok, xn_used[0]], scale=half)
                b.free = [a]
                xt[t] = p.stt(xs, xs, ALPHA, tmp, ALU.mult, ALU.add, [a, xt[t], x_used[0]])
                bn_tok[t, c] = p.emit("dve", lambda e, t=t, c=c: e.bn_stats(bn[:, t, c, :], X[:, t, c * 512:(c + 1) * 512]), [xt[t]])

        def full_mix(c, w, bs):
            half_mix(c, w, bs, 1.0)

        bn = sb("bn", [128, 2, 2, 6])
        mv = sb("mv", [128, 2, 2])

        bn_tok = {}

        def layer_norm(hi, lo):
            gi, g, gt = gain()
            bi, bb, bt = gain()
            a, r, got = {}, {}, {}
            for t in range(2):
                a[t] = p.emit("dve", lambda e, t=t: e.bn_aggr(mv[:, t, :], bn[:, t, :, :].rearrange("p c n -> p (c n)")),
                              [bn_tok[t, 0], bn_tok[t, 1]])
            r = rstd_of(mv[:, :, 1], 2, 1.0, 1e-5, [a[0], a[1]])
            for c in range(2):
                cols = slice(c * 512, (c + 1) * 512)
                for t in range(2):
                    m = p.stt(XN[:, t, cols], X[:, t, cols], mv[:, t, 0:1], g[:, cols], ALU.subtract, ALU.mult, [a[t], gt])
                    xt[t] = p.stt(X[:, t, cols], XN[:, t, cols], mv[:, t, 1:2], bb[:, cols], ALU.mult, ALU.add, [r, m, bt])
                    x_piece[c, t] = xt[t]
                got.update(turn_piece(X, c, [x_piece[c, 0], x_piece[c, 1]], hi, lo, x_used[0]))
            xn_used[0] = xt[1]
            gain_done(gi, xt[1])
            gain_done(bi, xt[1])
            return lhs_of(hi, lo, got)

        x_piece = {}

        def sincos(sn, cs, ang, tmp, waits):
            a = p.ts(tmp, ang, float(1 / (2 * np.pi)), ALU.mult, MAGIC, ALU.add, waits)
            a = p.ts(tmp, tmp, MAGIC, ALU.subtract, waits=[a])
            for part in TWO_PI:
                a = p.stt(ang, tmp, -float(part), ang, ALU.mult, ALU.add, [a])
            a = p.ts(ang, ang, 3.1415925, ALU.min, -3.1415925, ALU.max, [a])
            b = p.act(sn, ang, ACT.Sin, [a])
            c = p.act(cs, ang, ACT.Sin, [a], scale=0.5)
            c = p.tt(cs, cs, cs, ALU.mult, [c])
            c = p.ts(cs, cs, -2.0, ALU.mult, 1.0, ALU.add, [c])
            return [b, c]

        def attend(name, heads, dv, segs, scores, values, scale, bias, bt, dst, dep, vdep, during=None):
            nb = 4
            width = sum(s[2] for s in segs)
            hpb = 512 // dv
            blocks = [(t, o + 128 * j, j, n // 128) for t, o, n in segs for j in range(n // 128)]
            with ExitStack() as s:
                S = sb(name + "S", [128, nb, width], F32, s)
                PT = sb(name + "PT", [128, nb, width], F32, s)
                nm = sb(name + "nm", [128, heads, 2], F32, s)
                rs = sb(name + "rs", [128, 2, heads], F32, s)
                t_exp, t_turn, t_pt, t_pv, obanks, outs = {}, {}, {}, {}, {}, {}

                def score(h):
                    b = scratch()
                    for i, (t, o, n) in enumerate(segs):
                        parts = scores(h, i)
                        for j, (l, r) in enumerate(parts):
                            tok = p.mm(b.t[:, o:o + n], l, r, j == 0, j == len(parts) - 1,
                                       [dep, b.free], j == len(parts) - 1 and i == len(segs) - 1)
                    src = b.t[:, 0:width]
                    war = t_turn.get(h - nb)
                    if bias is not None:
                        if callable(scale):
                            a = [p.stt(S[:, h % nb, o:o + n], src[:, o:o + n], scale(h, t), bias[:, o:o + n], ALU.mult, ALU.add,
                                       [tok, bt, war]) for t, o, n in segs]
                        else:
                            a = [p.stt(S[:, h % nb, :], src, scale, bias, ALU.mult, ALU.add, [tok, bt, war])]
                        b.free = a
                        src = S[:, h % nb, :]
                    else:
                        a = tok
                    es, ms = [], []
                    for i, (t, o, n) in enumerate(segs):
                        m = p.reduce(nm[:, h, t:t + 1], src[:, o:o + n], ALU.max, [a], negate=True)
                        if bias is None:
                            m = p.ts(nm[:, h, t:t + 1], nm[:, h, t:t + 1], scale, ALU.mult, waits=[m])
                        ms.append(m)
                    for i, (t, o, n) in enumerate(segs):
                        es.append(p.act(S[:, h % nb, o:o + n], src[:, o:o + n], ACT.Exp, [ms, war],
                                        bias=nm[:, h, t:t + 1], scale=1.0 if bias is not None else scale,
                                        accum=rs[:, t, h:h + 1]))
                    if bias is None:
                        b.free = es
                    t_exp[h] = es

                def turn_p(h):
                    b = scratch()
                    for i, (t, o, j, n) in enumerate(blocks):
                        tok = p.tr(b.t[:, i * 128:(i + 1) * 128], S[:, h % nb, o:o + 128], ident,
                                   [t_exp[h], b.free], i == len(blocks) - 1)
                    t_turn[h] = tok
                    t_pt[h] = p.act(PT[:, h % nb, :], b.t[:, 0:width], waits=[tok, t_pv.get(h - nb)])
                    b.free = [t_pt[h]]

                def pv(h):
                    if h % hpb == 0:
                        obanks[h // hpb] = pair()
                    ob = obanks[h // hpb]
                    for i, (t, o, j, n) in enumerate(blocks):
                        v = values(h, j)
                        tok = p.mm(ob[t].t[:, (h % hpb) * dv:(h % hpb + 1) * dv], PT[:, h % nb, i * 128:(i + 1) * 128], v,
                                   j == 0, j == n - 1, [t_pt[h], vdep, ob[t].free], i == len(blocks) - 1)
                    t_pv[h] = tok
                    if h % hpb == hpb - 1:
                        h0 = h - hpb + 1
                        for t in range(2):
                            r = p.recip(rs[:, t, h0:h + 1], rs[:, t, h0:h + 1], [t_exp[x] for x in range(h0, h + 1)])
                            outs[t] = p.tt(dst(t, h0, hpb).rearrange("p (h d) -> p h d", h=hpb),
                                           ob[t].t[:, 0:hpb * dv].rearrange("p (h d) -> p h d", h=hpb),
                                           rs[:, t, h0:h + 1].unsqueeze(2).broadcast_to([128, hpb, dv]),
                                           ALU.mult, [r, tok, xn_used[0]])
                            ob[t].free = [outs[t]]
                        close(ob)

                for i in range(heads + 2):
                    if during:
                        during(i)
                    if i < heads:
                        score(i)
                    if 1 <= i <= heads:
                        turn_p(i - 1)
                    if i >= 2:
                        pv(i - 2)
            return [outs[0], outs[1]]


        def even_mixer():
            root_tok, lhs = norm_close()
            p.fence()
            with ExitStack() as s:
                sat, _ = small_at()
                W = sb("sguw", [128, 8, 128], F32, s)
                sbias = sb("sgub", [128, 8], F32, s)
                Q = sb("ev_qk", [128, 2, 512], F32, s)
                qT = sb("ev_qT", [128, 4, 256], F32, s)
                kT = sb("ev_kT", [128, 4, 256], F32, s)
                V = sb("ev_v", [128, 2, 512], F32, s)
                U = sb("ev_u", [128, 2, 512], F32, s)
                G = sb("ev_g", [128, 2, 512], F32, s)
                Z = sb("ev_z", [128, 8, 384], F32, s)
                E = sb("ev_e", [128, 4, 384], F32, s)
                SP = sb("ev_sp", [128, 4, 384], F32, s)
                OH = sb("ev_oh", [128, 8, 256], F32R, s)
                OL = sb("ev_ol", [128, 8, 256], F32R, s)
                tw = p.dma("sp", "d_sguw", W[:, :, :], d["small"][:, sat["sguw"][0]:sat["sguw"][1]].rearrange("p (g n) -> p g n", g=8), list(p.last.values()))
                tb = p.dma("sp", "d_sgub", sbias[:, :], d["small"][:, sat["sgub"][0]:sat["sgub"][1]], list(p.last.values()))
                g, gt = row("sgu_g", d["sgu_ln_gain"][0], s)
                bb, bt = row("sgu_b", d["sgu_ln_bias"][0], s)
                twm = p.tt(W[:, :, :], W[:, :, :], const("tril").unsqueeze(1).broadcast_to([128, 8, 128]), ALU.mult,
                           [tw, t_const], "pool")
                turned = [None]
                ready = {}
                held_back = []

                def evac(c, w, bs):
                    if c < 2:
                        toks = []
                        for t, (b, tok) in enumerate(bs):
                            a = p.act(Q[:, t, :], b.t[:, :], waits=[tok, turned[0], root_tok], scale=root[:, t:t + 1])
                            b.free = [a]
                            toks.append(a)

                        def later():
                            dst = (qT, kT)[c]
                            for t in range(2):
                                b = scratch()
                                for k in range(4):
                                    tok = p.tr(b.t[:, k * 128:(k + 1) * 128], Q[:, t, k * 128:(k + 1) * 128], ident,
                                               [toks[t], b.free], k == 3)
                                turned[0] = tok
                                ready[c, t] = p.copy(dst[:, :, t * 128:(t + 1) * 128],
                                                     b.t[:, :].rearrange("p (k n) -> p k n", k=4), [tok])
                                b.free = [ready[c, t]]

                        return later
                    for t, (b, tok) in enumerate(bs):
                        if c == 2:
                            ready["v", t] = p.act(V[:, t, :], b.t[:, :], waits=[tok, root_tok], scale=root[:, t:t + 1])
                        else:
                            held_back.append((c, t, p.act((U, G)[c - 3][:, t, :], b.t[:, :], waits=[tok, root_tok],
                                                          scale=root[:, t:t + 1])))
                        b.free = [p.last["act"]]
                    return None

                tz, tsp, tw_, tcum, tpv = {}, {}, {}, {}, {}

                def logits(h):
                    b = scratch()
                    r = slice(64 * (h % 2), 64 * (h % 2) + 64)
                    p.mm(b.t[:, 0:256], kT[r, h // 2, 0:128], qT[r, h // 2, :], True, True,
                         [[ready[c, t] for c in range(2) for t in range(2)], b.free])
                    tok = p.mm(b.t[:, 256:384], kT[r, h // 2, 128:256], qT[r, h // 2, 128:256], True, True, inc=True)
                    a = p.stt(Z[:, h, :], b.t[:, 0:384], 0.125, const("sbmask"), ALU.mult, ALU.add, [tok, t_const])
                    b.free = [a]
                    x = p.act(E[:, h % 4, :], Z[:, h, :], ACT.Abs, [a, tsp.get(h - 4)])
                    x = p.act(E[:, h % 4, :], E[:, h % 4, :], ACT.Exp, [x], scale=-1.0)
                    x = p.act(E[:, h % 4, :], E[:, h % 4, :], ACT.Ln, [x], bias=1.0)
                    tsp[h] = p.stt(SP[:, h % 4, :], Z[:, h, :], 0.0, E[:, h % 4, :], ALU.max, ALU.add, [x, tcum.get(h - 4)])
                    tz[h] = a

                def rest(h):
                    b = scratch()
                    p.mm(b.t[:, 0:384], const("incl"), SP[:, h % 4, :], True, False, [tsp[h], b.free, t_const])
                    tcum[h] = p.mm(b.t[:, 128:256], const("ones"), SP[:, h % 4, 256:384], False, True, inc=True)
                    a = p.tt(Z[:, h, :], Z[:, h, :], b.t[:, 0:384], ALU.subtract, [tcum[h]])
                    b.free = [a]
                    tw_[h] = p.act(Z[:, h, :], Z[:, h, :], ACT.Exp, [a])

                def weigh(h):
                    c = slice(h * 64, h * 64 + 64)
                    p.mm(ob[0].t[:, c], Z[:, h, 0:128], V[:, 0, c], True, True,
                         [tw_[h], ready["v", 0], ready["v", 1], ob[0].free, ob[1].free])
                    p.mm(ob[1].t[:, c], Z[:, h, 128:256], V[:, 0, c], True, False)
                    tpv[h] = p.mm(ob[1].t[:, c], Z[:, h, 256:384], V[:, 1, c], False, True, inc=True)

                def attention(i):
                    i -= 10
                    if 0 <= i < 8:
                        logits(i)
                    if 2 <= i < 10:
                        rest(i - 2)

                x_used[0] = linear("sbg_in", lhs, evac, attention)
                flush()
                ob = pair()
                for c, t, tok in held_back:
                    m = (U, G)[c - 3][:, t, :]
                    ready["ug"[c - 3], t] = p.act(m, m, ACT.Gelu_apprx_tanh, [tok])
                sgu = []
                for t in range(2):
                    a = p.emit("dve", lambda e, t=t: e.bn_stats(bn[:, t, 0, :], G[:, t, :]), [ready["g", t]])
                    a = p.emit("dve", lambda e, t=t: e.bn_aggr(mv[:, t, :], bn[:, t, 0, :]), [a])
                    r = rstd_of(mv[:, t, 1:2], 1, 1.0, 1e-6, [a])
                    m = p.stt(G[:, t, :], G[:, t, :], mv[:, t, 0:1], g, ALU.subtract, ALU.mult, [a, gt])
                    m = p.stt(G[:, t, :], G[:, t, :], mv[:, t, 1:2], bb, ALU.mult, ALU.add, [r, m, bt])
                    sgu.append(m)
                osg = [None, None]

                def spatial(t):
                    b = scratch()
                    for j in range(8):
                        tok = p.mm(b.t[:, j * 64:(j + 1) * 64], W[:, j, :], G[:, t, j * 64:(j + 1) * 64], True, True,
                                   [sgu[t], twm, b.free], j == 7)
                    for j in range(8):
                        osg[t] = p.stt(XN[:, t, 512 + j * 64:512 + (j + 1) * 64], b.t[:, j * 64:(j + 1) * 64], sbias[:, j:j + 1],
                                       U[:, t, j * 64:(j + 1) * 64], ALU.add, ALU.mult, [tok, tb, ready["u", t], xn_used[0]])
                    b.free = [osg[t]]

                spatial(0)
                spatial(1)
                for h in range(8):
                    weigh(h)
                dep2 = []
                for t in range(2):
                    a = p.copy(XN[:, t, 0:512], ob[t].t[:, :], [tpv[7], xn_used[0]])
                    ob[t].free = [a]
                    dep2.append([a, osg[t]])
                close(ob)
                lhs = xn_halves(dep2, OH, OL)
                norm_open()
                linear("sbg_out", lhs, add_x)

        def mem_norm(l, M):
            gi, g, gt = gain()
            done = [x for x in p.last.values() if x]
            dep = []
            for t in range(2):
                tm = p.dma("sp", f"d_m{l}{t}", M[:, t, :], d["mem"][t * 128:(t + 1) * 128, :], done)
                a = square(0, M[:, t, 0:512], st[:, 2 + t:3 + t], [tm])
                b = square(1, M[:, t, 512:1024], st[:, 4 + t:5 + t], [tm])
                a = p.tt(st[:, 2 + t:3 + t], st[:, 2 + t:3 + t], st[:, 4 + t:5 + t], ALU.add, [a, b])
                r = rstd_of(st[:, 2 + t:3 + t], 1, 1.0 / D, 1e-6, [a])
                for c in range(2):
                    cols = slice(c * 512, (c + 1) * 512)
                    r = p.stt(M[:, t, cols], M[:, t, cols], st[:, 2 + t:3 + t], g[:, cols], ALU.mult, ALU.mult, [r, gt])
                dep.append(r)
            gain_done(gi, dep[1])

            def later():
                got = to_halves(lambda t, k: M[:, t, k * 128:(k + 1) * 128], 8, MH, ML, dep, mem.get("used"))
                mem["lhs"] = lhs_of(MH, ML, got)

            return later

        mem = {}

        def qk_turn(dst, src, k0, toks, got, key):
            b = scratch()
            for k in range(2):
                for t in range(2):
                    tok = p.tr(b.t[:, (2 * k + t) * 128:(2 * k + t + 1) * 128], src[:, t, k * 128:(k + 1) * 128],
                               ident, [toks[t], b.free], k == 1 and t == 1)
            got[key] = p.copy(dst[:, k0:k0 + 2, :], b.t[:, :].rearrange("p (k n) -> p k n", k=2), [tok])
            b.free = [got[key]]
            return tok

        def mem_keys(l, kT, V, q, s):
            kg, kgt = row(f"xk{l}", d["xmem_k_gain"][l], s)
            t_k, turned, vt = {}, {}, {}

            def evac(c, w, bs):
                toks = []
                for t, (b, tok) in enumerate(bs):
                    vt[c, t] = p.act(V[:, t, c * 256:(c + 1) * 256], b.t[:, 256:512], waits=[tok])
                    toks.append(rms(b.t[:, 0:256], q[:, c % 2, t, :], kg, kgt, 6 + t, 256,
                                    [tok, vt[c, t], turned.get(c - 2)], q[:, c % 2, t, :]))
                    b.free = [toks[t], vt[c, t]]
                mem["used"] = p.last["pe"]

                def later():
                    turned[c] = qk_turn(kT, q[:, c % 2, :, :], 2 * c, toks, t_k, c)

                return later

            return steps(f"x_kv{l}", mem["lhs"], evac), t_k, vt, turned

        def mem_attention(l, kT, V, q, t_k, vt, turned):
            root_tok, lhs = norm_close()
            p.fence()
            with ExitStack() as s:
                qT = sb(f"xm_qT{l}", [128, 8, 256], F32, s)
                OH = sb(f"xm_oh{l}", [128, 8, 256], F32R, s)
                OL = sb(f"xm_ol{l}", [128, 8, 256], F32R, s)
                qg, qgt = row(f"xq{l}", d["xmem_q_gain"][l], s)
                t_q = {}

                def evac(c, w, bs):
                    toks = {}
                    for t, (b, tok) in enumerate(bs):
                        sums = [p.act(q[:, j, t, :], b.t[:, j * 256:(j + 1) * 256], ACT.Square,
                                      [tok, turned.get(2), turned.get(3), turned.get(("q", c - 1, j)), root_tok],
                                      scale=root[:, t:t + 1], accum=st[:, 8 + 2 * t + j:9 + 2 * t + j]) for j in range(2)]
                        r = rstd_of(st[:, 8 + 2 * t:10 + 2 * t], 2, 1.0 / 256, 1e-6, sums)
                        r = p.ts(st[:, 8 + 2 * t:10 + 2 * t], st[:, 8 + 2 * t:10 + 2 * t], root[:, t:t + 1], ALU.mult, waits=[r])
                        for j in range(2):
                            toks[j, t] = p.stt(q[:, j, t, :], b.t[:, j * 256:(j + 1) * 256], st[:, 8 + 2 * t + j:9 + 2 * t + j], qg,
                                               ALU.mult, ALU.mult, [r, qgt])
                        b.free = [toks[0, t], toks[1, t]]

                    def later():
                        for j in range(2):
                            turned["q", c, j] = qk_turn(qT, q[:, j, :, :], 4 * c + 2 * j, [toks[j, 0], toks[j, 1]], t_q, 2 * c + j)

                    return later

                x_used[0] = linear(f"x_q{l}", lhs, evac)
                flush()

                def scores(h, i):
                    return [(qT[:, 2 * h + k, i * 128:(i + 1) * 128], kT[:, 2 * h + k, :]) for k in range(2)]

                dep = attend(f"xm{l}", 4, 256, [(0, 0, 256), (1, 256, 256)], scores,
                             lambda h, j: V[:, j, h * 256:(h + 1) * 256], 0.0625, None, None,
                             lambda t, h, n: XN[:, t, h * 256:(h + n) * 256],
                             [list(t_k.values()), list(t_q.values())], list(vt.values()))
                lhs = xn_halves(dep, OH, OL)
                norm_open()
                linear(f"x_o{l}", lhs, add_x)

        def angles(pos, inv, half, sn, cs, s, name):
            pi = sb(name + "pi", [128, 2], I32, s)
            pf = sb(name + "pf", [128, 2], F32, s)
            ang = sb(name + "an", [128, 2, half], F32, s)
            tmp = sb(name + "at", [128, 2, half], F32, s)
            a = p.dma("sp", "d_" + name, pi[:, :], pos, [x for x in p.last.values() if x])
            a = p.copy(pf[:, :], pi[:, :], [a])
            toks = [p.ts(ang[:, t, :], inv, pf[:, t:t + 1], ALU.mult, waits=[a, t_const]) for t in range(2)]
            return sincos(sn[:, :, :], cs[:, :, :], ang[:, :, :], tmp[:, :, :], toks)

        def rope(o1, o2, x1, x2, cs, sn, a, b, waits, e="dve"):
            t1 = p.tt(a, x1, cs, ALU.mult, waits, e)
            t2 = p.tt(b, x2, sn, ALU.mult, waits, e)
            t3 = p.tt(o1, a, b, ALU.subtract, [t1, t2, waits], e)
            t1 = p.tt(a, x1, sn, ALU.mult, [t3, waits], e)
            t2 = p.tt(b, x2, cs, ALU.mult, [t3, waits], e)
            return p.tt(o2, a, b, ALU.add, [t1, t2], e)

        def mla_mixer():
            root_tok, lhs = norm_close()
            p.fence()
            with ExitStack() as s:
                qT = sb("ml_qT", [96, 16, 256], F32, s)
                kT = sb("ml_kT", [96, 16, 256], F32, s)
                V = sb("ml_v", [128, 2, D], F32, s)
                rq = sb("ml_rq", [128, 2, 16], F32, s)
                rk = sb("ml_rk", [128, 2, 16], F32, s)
                with ExitStack() as s2:
                    Q = sb("ml_q", [128, 2, 16, 96], F32, s2)
                    K = sb("ml_k", [128, 2, 16, 96], F32, s2)
                    KR = sb("ml_kr", [128, 2, 32], F32, s2)
                    KE = sb("ml_ke", [128, 2, 32], F32, s2)
                    sn = sb("ml_sn", [128, 2, 16], F32, s2)
                    cs = sb("ml_cs", [128, 2, 16], F32, s2)
                    tmp = XN[:, 0, :].rearrange("p (j h n) -> p j h n", j=4, h=16)
                    t_ang = angles(d["positions"], const("inv1"), 16, sn, cs, s2, "pos1")
                    qg, qgt = row("ql", d["mla_q_lora_gain"][0], s2)
                    kg, kgt = row("kl", d["mla_kv_lora_gain"][0], s2)
                    gq, gqt = row("mq", d["mla_q_gain"][0], s2)
                    gk, gkt = row("mk", d["mla_k_gain"][0], s2)
                    tc = {}

                    def lora(b, t, lo, hi, g, gt, col, n, waits):
                        s_ = st[:, col:col + 1]
                        a = p.act(XN[:, t, lo:hi], b.t[:, 0:n], ACT.Square, [waits, xn_used[0], root_tok],
                                  scale=root[:, t:t + 1], accum=s_)
                        r = rstd_of(s_, 1, 1.0 / n, 1e-6, [a])
                        r = p.tt(s_, s_, root[:, t:t + 1], ALU.mult, [r])
                        return p.stt(XN[:, t, lo:hi], b.t[:, 0:n], s_, g, ALU.mult, ALU.mult, [r, gt, a])

                    def evac(c, w, bs):
                        for t, (b, tok) in enumerate(bs):
                            if c == 0:
                                tc["q", t] = lora(b, t, 0, 512, qg, qgt, 12 + t, 512, [tok])
                                b.free = [tc["q", t]]
                            else:
                                tc["r", t] = p.act(KR[:, t, :], b.t[:, 256:288], waits=[tok, root_tok], scale=root[:, t:t + 1])
                                tc["k", t] = lora(b, t, 512, 768, kg, kgt, 14 + t, 256, [tok, tc["r", t]])
                                b.free = [tc["k", t], tc["r", t]]

                    x_used[0] = linear("mla_in", lhs, evac)
                    fill(1)
                    got = to_halves(lambda t, k: XN[:, t, k * 128:(k + 1) * 128], 6, XH, XL,
                                    [[tc["q", t], tc["k", t]] for t in range(2)], x_used[0])
                    xn_used[0] = p.last["pe"]
                    tq, tk, tv, sq, sk = {}, {}, {}, {}, {}
                    free = {}

                    def sums(b, dst, t, heads, n, tok, key):
                        v = junk[:, t, 0:heads * n]
                        a = p.act(v, b.t[:, 0:heads * n], ACT.Square, [tok, free.get(t), junk_tok[t]])
                        junk_tok[t] = free[t] = p.reduce(dst, v.rearrange("p (h n) -> p h n", h=heads), ALU.add, [a])
                        return free[t]

                    def evac_q(c, w, bs):
                        for t, (b, tok) in enumerate(bs):
                            sq[c, t] = sums(b, rq[:, t, 4 * c:4 * c + 4], t, 4, 96, tok, c)
                            tq[c, t] = p.act(Q[:, t, 4 * c:4 * c + 4, :], b.t[:, 0:384].rearrange("p (h n) -> p h n", h=4),
                                             waits=[tok])
                            b.free = [tq[c, t]]

                    def evac_kv(c, w, bs):
                        for t, (b, tok) in enumerate(bs):
                            if c < 2:
                                sk[c, t] = sums(b, rk[:, t, 8 * c:8 * c + 8], t, 8, 64, tok, c)
                                tk[c, t] = p.act(K[:, t, 8 * c:8 * c + 8, 0:64], b.t[:, :].rearrange("p (h n) -> p h n", h=8),
                                                 waits=[tok])
                                b.free = [tk[c, t]]
                            else:
                                tv[c, t] = p.act(V[:, t, (c - 2) * 512:(c - 1) * 512], b.t[:, :], waits=[tok])
                                b.free = [tv[c, t]]

                    def over_heads(m):
                        return m.unsqueeze(1).broadcast_to([128, 16, m.shape[1]])

                    def over_row(m, n):
                        return m.unsqueeze(2).broadcast_to([128, 16, n])

                    linear("mla_uq", lhs_of(XH, XL, got), evac_q)
                    done = {}
                    for t in range(2):
                        dep = [tq[c, t] for c in range(4)]
                        r = rstd_of(rq[:, t, :], 16, 1.0 / 96, 1e-6, [sq[c, t] for c in range(4)])
                        done["rq", t] = p.ts(rq[:, t, :], rq[:, t, :], float(96.0 ** -0.5), ALU.mult, waits=[r])
                        qr = Q[:, t, :, 64:96]
                        n2 = p.tt(qr, qr, over_heads(gq[:, 64:96]), ALU.mult, [dep, gqt])
                        x1, x2 = qr[:, :, 0:16], qr[:, :, 16:32]
                        c_, s_ = over_heads(cs[:, t, :]), over_heads(sn[:, t, :])
                        w = [n2, t_ang, done.get(("q", t - 1)), xn_used[0]]
                        ab = [p.tt(tmp[:, 0], x1, c_, ALU.mult, w), p.tt(tmp[:, 1], x2, s_, ALU.mult, w),
                              p.tt(tmp[:, 2], x1, s_, ALU.mult, w), p.tt(tmp[:, 3], x2, c_, ALU.mult, w)]
                        done["q", t] = [p.tt(x1, tmp[:, 0], tmp[:, 1], ALU.subtract, ab), p.tt(x2, tmp[:, 2], tmp[:, 3], ALU.add, ab)]
                    gg = gk[:, 0:64]
                    tg = p.tt(gg, gq[:, 0:64], gg, ALU.mult, [gqt, gkt])
                    for t in range(2):
                        rs_ = st[:, 16 + t:17 + t]
                        b = p.act(KE[:, t, :], KR[:, t, :], ACT.Square, [tc["r", t]], accum=rs_)
                        n2 = p.tt(KR[:, t, :], KR[:, t, :], gk[:, 64:96], ALU.mult, [b, gkt])
                        x1, x2, c_, s_ = KR[:, t, 0:16], KR[:, t, 16:32], cs[:, t, :], sn[:, t, :]
                        w = [n2, t_ang, done["q", 1], done.get(("e", t - 1))]
                        ab = [p.tt(tmp[:, 0, 0], x1, c_, ALU.mult, w), p.tt(tmp[:, 1, 0], x2, s_, ALU.mult, w),
                              p.tt(tmp[:, 2, 0], x1, s_, ALU.mult, w), p.tt(tmp[:, 3, 0], x2, c_, ALU.mult, w)]
                        done["e", t] = [p.tt(KE[:, t, 0:16], tmp[:, 0, 0], tmp[:, 1, 0], ALU.subtract, ab),
                                        p.tt(KE[:, t, 16:32], tmp[:, 2, 0], tmp[:, 3, 0], ALU.add, ab), b]
                    x_used[0] = linear("mla_ukv", lhs_of(XH, XL, {(k, t): got[k + 4, t] for k in range(2) for t in range(2)}, 4), evac_kv)
                    for t in range(2):
                        r = rk[:, t, :]
                        a = p.ts(r, r, st[:, 16 + t:17 + t], ALU.add, waits=[sk[0, t], sk[1, t], done["e", t]])
                        a = rstd_of(r, 16, 1.0 / 96, 1e-6, [a])
                        kn = K[:, t, :, 0:64]
                        n1 = p.tt(kn, kn, over_row(r, 64), ALU.mult, [a, tk[0, t], tk[1, t]])
                        n1 = p.tt(kn, kn, over_heads(gg), ALU.mult, [n1, tg])
                        n2 = p.tt(K[:, t, :, 64:96], over_heads(KE[:, t, :]), over_row(r, 32), ALU.mult, [a, done["e", t]])
                        done["k", t] = [n1, n2]
                    turned = []

                    def turn_heads(src, dst, t, tok):
                        for g in range(4):
                            b = scratch()
                            for j in range(4):
                                x = p.tr(b.t[0:96, j * 128:(j + 1) * 128], src[:, t, 4 * g + j, :], ident, [tok, b.free], j == 3)
                            o = dst[:, 4 * g:4 * g + 4, t * 128:(t + 1) * 128]
                            v = b.t[0:96, :].rearrange("p (h n) -> p h n", h=4)
                            turned.append(p.act(o, v, waits=[x]) if g % 2 else p.copy(o, v, [x]))
                            b.free = [turned[-1]]

                    turn_heads(Q, qT, 0, done["q", 0])
                    turn_heads(Q, qT, 1, done["q", 1])
                    fill(1)
                    turn_heads(K, kT, 0, done["k", 0])
                    turn_heads(K, kT, 1, done["k", 1])
                p.fence()
                OH = sb("ml_oh", [128, 8, 256], F32R, s)
                OL = sb("ml_ol", [128, 8, 256], F32R, s)

                xn_used[0] = [xn_used[0], done["e", 1]]

                def scores(h, i):
                    return [(qT[:, h, i * 128:(i + 1) * 128], kT[:, h, 0:128 * (i + 1)])]

                dep = attend("ml", 16, 64, [(0, 0, 128), (1, 128, 256)], scores,
                             lambda h, j: V[:, j, h * 64:(h + 1) * 64], lambda h, t: rq[:, t, h:h + 1], const("causal"),
                             [t_const, done["rq", 0], done["rq", 1]],
                             lambda t, h, n: XN[:, t, h * 64:(h + n) * 64], turned, list(tv.values()),
                             lambda i: fill(1) if i in (3, 11) else None)
                fill(4)
                lhs = xn_halves(dep, OH, OL)
                norm_open()
                linear("mla_out", lhs, add_x)

        def s5_tables(s):
            sat, _ = small_at()
            P = sb("s5_p", [128, 48], F32, s)
            T = sb("s5_T", [128, 2, 16, 256], F32, s)
            names = ["dt", "mag", "th", "tm", "sn", "cs", "abr", "abi", "den", "fre", "fim", "t1"]
            v = {n: sb("s5_" + n, [128, 16], F32, s)[:, :] for n in names}
            tmp = sb("s5_tt", [128, 8, 128], F32, s)
            ts_ = p.dma("sp", "d_s5p", P[:, :], d["small"][:, sat["lre"][0]:sat["ldt"][1]], [x for x in p.last.values() if x])
            lre, lim, ldt = P[:, 0:16], P[:, 16:32], P[:, 32:48]
            got = {"mag": v["mag"], "fre": v["fre"], "fim": v["fim"], "T": T}

            def params():
                a = p.act(v["dt"], ldt, ACT.Exp, [ts_])
                l = p.ts(lre, lre, -1e-4, ALU.min, waits=[ts_])
                m = p.tt(v["mag"], lre, v["dt"], ALU.mult, [a, l])
                m = p.act(v["mag"], v["mag"], ACT.Exp, [m])
                t = p.tt(v["th"], lim, v["dt"], ALU.mult, [a])
                sc = sincos(v["sn"], v["cs"], v["th"], v["tm"], [t])
                r = p.tt(v["abr"], v["mag"], v["cs"], ALU.mult, [m, sc])
                r = p.ts(v["abr"], v["abr"], 1.0, ALU.subtract, waits=[r])
                i = p.tt(v["abi"], v["mag"], v["sn"], ALU.mult, [m, sc])
                e = p.tt(v["den"], lre, lre, ALU.mult, [l])
                f = p.tt(v["t1"], lim, lim, ALU.mult, [ts_])
                e = p.tt(v["den"], v["den"], v["t1"], ALU.add, [e, f])
                e = p.recip(v["den"], v["den"], [e])
                a1 = p.tt(v["fre"], v["abr"], lre, ALU.mult, [r, l])
                a2 = p.tt(v["t1"], v["abi"], lim, ALU.mult, [i, e])
                a1 = p.tt(v["fre"], v["fre"], v["t1"], ALU.add, [a1, a2])
                a1 = p.tt(v["fre"], v["fre"], v["den"], ALU.mult, [a1, e])
                a2 = p.tt(v["fim"], v["abi"], lre, ALU.mult, [i, l])
                a3 = p.tt(v["t1"], v["abr"], lim, ALU.mult, [r, a1])
                a2 = p.tt(v["fim"], v["fim"], v["t1"], ALU.subtract, [a2, a3])
                a2 = p.tt(v["fim"], v["fim"], v["den"], ALU.mult, [a2, e])
                got["tok"] = [m, sc, a1, a2]

            def phases():
                a = p.copy(T[:, 0, :, 0], v["cs"], got["tok"], "pool")
                b = p.copy(T[:, 1, :, 0], v["sn"], got["tok"], "pool")
                for half in range(2):
                    r = slice(8 * half, 8 * half + 8)
                    x = [a, b, p.last["pool"]]
                    for k in range(8):
                        m = 1 << k
                        R, I = T[:, 0, r, 0:m], T[:, 1, r, 0:m]
                        Br = T[:, 0, r, m - 1:m].broadcast_to([128, 8, m])
                        Bi = T[:, 1, r, m - 1:m].broadcast_to([128, 8, m])
                        oR, oI, tm = T[:, 0, r, m:2 * m], T[:, 1, r, m:2 * m], tmp[:, :, 0:m]
                        y1 = p.tt(oR, R, Br, ALU.mult, x, "pool")
                        y2 = p.tt(tm, I, Bi, ALU.mult, x, "pool")
                        y1 = p.tt(oR, oR, tm, ALU.subtract, [y1, y2], "pool")
                        y2 = p.tt(oI, R, Bi, ALU.mult, x, "pool")
                        y3 = p.tt(tm, I, Br, ALU.mult, [x, y1], "pool")
                        y2 = p.tt(oI, oI, tm, ALU.add, [y2, y3], "pool")
                        x = [y1, y2]
                    got["t", half] = x

            return got, lambda i: {6: params, 12: phases}.get(i, lambda: None)()

        def ab_mixer(s5, lhs):
            p.fence()
            with ExitStack() as s:
                sat, _ = small_at()
                at = {"convw": 0, "dskip": 12, "bglu": 16}
                S1 = sb("ab_s1", [128, 20], F32, s)
                S2 = sb("ab_s2", [128, 2048], F32, s)
                done = [x for x in p.last.values() if x]
                ts_ = [p.dma("sp", "d_ab1", S1[:, :], d["small"][:, sat["convw"][0]:sat["bglu"][1]], done),
                       p.dma("sp", "d_ab2", S2[:, :], d["small"][:, sat["bre"][0]:sat["cim"][1]], done)]
                small = {n: S2[:, 512 * i:512 * i + 512] for i, n in enumerate(("bre", "bim", "cre", "cim"))}
                cw, dskip, bglu = S1[:, 0:12].rearrange("p (k j) -> p k j", k=4), S1[:, 12:16], S1[:, 16:20]
                T, mag = s5["T"], s5["mag"]
                uT = sb("ab_uT", [128, 4, 256], F32, s)
                gT = sb("ab_gT", [128, 4, 256], F32, s)
                cT = sb("ab_cT", [128, 4, 258], F32, s)
                Z = sb("ab_z", [128, 4, 256], F32, s)
                H = sb("ab_h", [128, 2, 512], F32, s)
                B = sb("ab_b", [128, 2, 512], F32, s)
                ncr = sb("ab_ncr", [128, 512], F32, s)
                nci = sb("ab_nci", [128, 512], F32, s)
                ct = sb("ab_ct", [128, 512], F32, s)
                nb = 2
                A_ = sb("ab_A", [128, nb, 2, 256], F32, s)
                B_ = sb("ab_B", [128, nb, 2, 256], F32, s)
                C_ = sb("ab_C", [128, nb, 2, 256], F32, s)
                D_ = sb("ab_D", [128, nb, 2, 256], F32, s)
                ZH = sb("ab_zh", [128, 4, 256], F32R, s)
                ZL = sb("ab_zl", [128, 4, 256], F32R, s)
                W_ = B_
                z0 = p.memset(cT[:, :, 0:2], 0.0)
                g = lambda m: m.rearrange("p (i c) -> p i c", i=16)
                fr = s5["fre"].unsqueeze(2).broadcast_to([128, 16, 32])
                fi = s5["fim"].unsqueeze(2).broadcast_to([128, 16, 32])
                cr, ci = small["cre"], small["cim"]
                w = [s5["tok"], ts_]
                x1 = p.tt(g(nci[:, :]), g(cr), fi, ALU.mult, w, "pool")
                x2 = p.tt(g(ct[:, :]), g(ci), fr, ALU.mult, w, "pool")
                x1 = p.stt(nci[:, :], nci[:, :], -1.0, ct[:, :], ALU.mult, ALU.subtract, [x1, x2])
                x3 = p.tt(g(cr), g(cr), fr, ALU.mult, [x1], "pool")
                x4 = p.tt(g(ct[:, :]), g(ci), fi, ALU.mult, [x1, w], "pool")
                x3 = p.tt(cr, cr, ct[:, :], ALU.subtract, [x3, x4], "pool")
                x4 = p.ts(ncr[:, :], cr, -1.0, ALU.mult, waits=[x3])
                cre, ncre, ncim, t_c = cr, ncr[:, :], nci[:, :], [x1, x3, x4]
                ready, turned = {}, {}
                spare[:] = [4, 5]

                def turn_all(src, dst, key, toks, off=0):
                    for t in range(2):
                        b = scratch()
                        for k in range(4):
                            tok = p.tr(b.t[:, k * 128:(k + 1) * 128], src[:, t, k * 128:(k + 1) * 128], ident,
                                       [toks[t], b.free], k == 3)
                        ready[key, t] = p.act(dst[:, :, off + t * 128:off + (t + 1) * 128],
                                              b.t[:, :].rearrange("p (k n) -> p k n", k=4), waits=[tok, z0])
                        b.free = [ready[key, t]]
                    turned[key] = tok

                hold = {}

                def evac(c, w, bs):
                    toks = []
                    for t, (b, tok) in enumerate(bs):
                        if c in (0, 3):
                            toks.append(p.act(B[:, t, :], b.t[:, :], waits=[tok, turned.get("u")]))
                        elif c == 1:
                            toks.append(p.act(H[:, t, :], b.t[:, :], waits=[tok]))
                        else:
                            toks.append(p.tt(H[:, t, :], b.t[:, :], H[:, t, :], ALU.mult, [tok, hold[t]]))
                        hold[t] = toks[t]
                        b.free = [toks[t]]
                    if c == 0:
                        return lambda: turn_all(B, uT, "u", toks)
                    if c == 2:
                        return lambda: turn_all(H, cT, "c", toks, 2)
                    if c == 3:
                        return lambda: turn_all(B, gT, "g", toks)

                t_w, t_y, t_cd, zt = {}, {}, {}, {}
                ya, got = {}, {}

                def state(i):
                    r = slice(32 * (i % 4), 32 * (i % 4) + 32)
                    b = scratch()
                    for j, nm in enumerate(("bre", "bim")):
                        l = small[nm].rearrange("p (k n) -> p k n", k=4)[r, i // 4, :]
                        tok = p.mm(b.t[:, j * 256:(j + 1) * 256], l, uT[r, i // 4, :], True, True,
                                   [ready["u", 0], ready["u", 1], ts_, b.free], j == 1)
                    Tr = T[:, 0, i, :].unsqueeze(1).broadcast_to([128, 2, 256])
                    v = b.t[:, :].rearrange("p (j n) -> p j n", j=2)
                    n = i % nb
                    x = p.tt(A_[:, n, :, :], v, Tr, ALU.mult, [tok, s5["t", i // 8], t_w.get(i - nb)])
                    y1 = p.tt(B_[:, n, 0, :], b.t[:, 256:512], T[:, 1, i, :], ALU.mult, [tok, t_cd.get(i - nb)])
                    y2 = p.tt(B_[:, n, 1, :], b.t[:, 0:256], T[:, 1, i, :], ALU.mult, [tok, t_cd.get(i - nb)])
                    b.free = [x, y1, y2]
                    x1 = p.tt(A_[:, n, 0, :], A_[:, n, 0, :], B_[:, n, 0, :], ALU.add, [x, y1])
                    x2 = p.tt(A_[:, n, 1, :], A_[:, n, 1, :], B_[:, n, 1, :], ALU.subtract, [x, y2])
                    for j, x in ((0, x1), (1, x2)):
                        t_w[i] = p.emit("dve", lambda e, j=j: e.tensor_tensor_scan(
                            W_[:, n, j, :], mag[:, i:i + 1].broadcast_to([128, 256]), A_[:, n, j, :], 0.0, ALU.mult, ALU.add),
                            [x, t_cd.get(i - nb)])
                    Ti = T[:, 1, i, :].unsqueeze(1).broadcast_to([128, 2, 256])
                    p.tt(C_[:, n, :, :], W_[:, n, :, :], Tr, ALU.mult, [t_w[i], t_y.get(i - nb)], "pool")
                    t_cd[i] = p.tt(D_[:, n, :, :], W_[:, n, :, :], Ti, ALU.mult, [t_w[i], t_y.get(i - nb)], "pool")

                def outputs(i):
                    yb = banks[6 + i // 4 % 2]
                    n, cc = i % nb, slice(32 * i, 32 * i + 32)
                    o = yb.t[32 * (i % 4):32 * (i % 4) + 32, 0:256]
                    p.mm(o, cre[:, cc], C_[:, n, 0, :], True, False, [t_cd[i], t_c, yb.free])
                    p.mm(o, ncim[:, cc], C_[:, n, 1, :], False, False)
                    p.mm(o, ncim[:, cc], D_[:, n, 0, :], False, False)
                    t_y[i] = p.mm(o, ncre[:, cc], D_[:, n, 1, :], False, True, inc=True)
                    if i % 4 == 3:
                        k = i // 4
                        zt["y", k] = p.stt(Z[:, k, :], uT[:, k, :], dskip[:, k:k + 1], yb.t[:, 0:256], ALU.mult, ALU.add,
                                           [t_y[i], ts_])
                        yb.free = [zt["y", k]]

                queue = [(f, i) for i in range(18) for f in (outputs, state)]

                def recurrence(n):
                    for f, i in queue[:2 * n]:
                        j = i if f is state else i - 2
                        if 0 <= j < 16:
                            f(j)
                    del queue[:2 * n]

                def convolve():
                    Y = [H[:, 0, 0:256], H[:, 0, 256:512]]
                    cd = [ready["c", 0], ready["c", 1], ts_, turned["c"]]
                    for k in range(4):
                        y = Y[k % 2]
                        a = p.ts(y, cT[:, k, 0:256], cw[:, k, 0:1], ALU.mult, waits=[cd, ya.get(k - 2)])
                        a = p.stt(y, cT[:, k, 1:257], cw[:, k, 1:2], y, ALU.mult, ALU.add, [a])
                        a = p.stt(y, cT[:, k, 2:258], cw[:, k, 2:3], y, ALU.mult, ALU.add, [a])
                        a = p.tt(y, y, gT[:, k, :], ALU.mult, [a, ready["g", 0], ready["g", 1]])
                        h = p.act(XH[:, k, :], y, waits=[a, x_used[0]])
                        ya[k] = p.tt(XL[:, k, :], y, XH[:, k, :].bitcast(F32), ALU.subtract, [h, x_used[0]])
                        got[k, 0] = got[k, 1] = ya[k]

                x_used[0] = linear("ab_in", lhs, evac, lambda i: recurrence(1) if i >= 6 else None)
                flush()
                recurrence(18)
                convolve()
                for k in range(4):
                    zt["z", k] = p.act(Z[:, k, :], Z[:, k, :], ACT.Gelu_apprx_tanh, [zt["y", k]])
                    h = p.copy(ZH[:, k, :], Z[:, k, :], [zt["z", k]])
                    zt[k] = p.tt(ZL[:, k, :], Z[:, k, :], ZH[:, k, :].bitcast(F32), ALU.subtract, [h])
                spare[:] = [4, 5, 6, 7]
                gb = [banks[i] for i in range(4)]
                for i, (c, k0, nk, w, _) in enumerate(units_of(4, [512])):
                    u, wh, wl = weights("glu", i, nk, w)
                    for k in range(nk):
                        kt = k0 + k
                        for m in range(4):
                            ms = slice(m * 128, (m + 1) * 128)
                            o = gb[m].t[:, 0:256]
                            p.mm(o, wh[:, k, ms], ZH[:, kt, :], kt == 0, False, [zt[kt], t_split[u], gb[m].free])
                            p.mm(o, wh[:, k, ms], ZL[:, kt, :], False, False)
                            tok = p.mm(o, wl[:, k, ms], ZH[:, kt, :], False, kt == 3, inc=kt == 3 or k == nk - 1)
                            if kt == 3:
                                t_y["g", m] = tok
                    t_used[u] = tok
                for m in range(4):
                    sgm = W_[:, m % 2, m // 2, :]
                    a = p.act(sgm, gb[m].t[:, 0:256], ACT.Sigmoid, [t_y["g", m], t_cd[15], ts_], bias=bglu[:, m:m + 1])
                    gb[m].free = [a]
                    a = p.tt(sgm, sgm, Z[:, m, :], ALU.mult, [a, zt["z", m]])
                    h = p.act(XH[:, 4 + m, :], sgm, waits=[a, x_used[0]])
                    got[4 + m, 0] = got[4 + m, 1] = p.tt(XL[:, 4 + m, :], sgm, XH[:, 4 + m, :].bitcast(F32), ALU.subtract,
                                                         [h, x_used[0]])
                x_used[0] = linear("ab_out", lhs_of(XH, XL, got), full_mix)

        def dsa_mixer(lhs):
            p.fence()
            with ExitStack() as s:
                qT = sb("ds_qT", [128, 10, 256], F32, s)
                iT = sb("ds_iT", [128, 5, 256], F32, s)
                V = sb("ds_v", [128, 2, 256], F32, s)
                acc = sb("ds_acc", [128, 384], F32, s)
                work = sb("ds_work", [128, 384], F32, s)
                wi = sb("ds_wi", [128, 2, 8], F32, s)
                R = sb("ds_r", [128, 2, 384], F32, s)
                m8 = sb("ds_m8", [128, 2, 8], F32, s)
                Q = sb("ds_q", [128, 2, 1280], F32, s)
                I = sb("ds_i", [128, 2, 640], F32, s)
                sna = sb("ds_sna", [128, 2, 16], F32, s)
                csa = sb("ds_csa", [128, 2, 16], F32, s)
                sni = sb("ds_sni", [128, 2, 8], F32, s)
                csi = sb("ds_csi", [128, 2, 8], F32, s)
                tmi = sb("ds_tmi", [128, 4, 9, 8], F32, s)
                tmq = sb("ds_tmq", [128, 4, 10, 16], F32, s)
                toks, ready, dq, tacc, racc, tops = {}, {}, {}, {}, {}, {}
                segs = [(0, 0, 128), (1, 128, 256)]
                ang = {}

                def evac(c, w, bs):
                    for t, (b, tok) in enumerate(bs):
                        if c == 0:
                            toks["qi", t] = p.act(I[:, t, 0:512], b.t[:, :], waits=[tok])
                        elif c == 1:
                            toks["ki", t] = p.act(I[:, t, 512:576], b.t[:, 0:64], waits=[tok])
                            toks["wi", t] = p.act(wi[:, t, :], b.t[:, 64:72], waits=[tok], scale=float(512.0 ** -0.5))
                        elif c < 4:
                            toks["q", c, t] = p.act(Q[:, t, (c - 2) * 512:(c - 1) * 512], b.t[:, :], waits=[tok])
                        else:
                            toks["k", t] = p.act(Q[:, t, 1024:1280], b.t[:, 0:256], waits=[tok])
                            toks["v", t] = p.act(V[:, t, :], b.t[:, 256:512], waits=[tok])
                        b.free = [p.last["act"]]

                def turns(x, n, half, cs, sn, tmp, waits, e):
                    c_ = cs.unsqueeze(1).broadcast_to([128, n, half])
                    s_ = sn.unsqueeze(1).broadcast_to([128, n, half])
                    x1, x2 = x[:, :, 0:half], x[:, :, half:2 * half]
                    ab = [tmp[:, j, 0:n, :] for j in range(4)]
                    y = [p.tt(ab[0], x1, c_, ALU.mult, waits, e), p.tt(ab[1], x2, s_, ALU.mult, waits, e),
                         p.tt(ab[2], x1, s_, ALU.mult, waits, e), p.tt(ab[3], x2, c_, ALU.mult, waits, e)]
                    return [p.tt(x1, ab[0], ab[1], ALU.subtract, y, e), p.tt(x2, ab[2], ab[3], ALU.add, y, e)]

                def tiles(src, dst, t, g, n, tok, got):
                    b = scratch()
                    for k in range(n):
                        x = p.tr(b.t[:, k * 128:(k + 1) * 128], src[:, t, (g + k) * 128:(g + k + 1) * 128], ident,
                                 [tok, b.free], k == n - 1)
                    got[g, t] = p.act(dst[:, g:g + n, t * 128:(t + 1) * 128],
                                      b.t[:, 0:n * 128].rearrange("p (k n) -> p k n", k=n), waits=[x])
                    b.free = [got[g, t]]

                def index_turn():
                    for t in range(2):
                        it = I[:, t, 0:576].rearrange("p (h n) -> p h n", h=9)
                        o = turns(it, 9, 8, csi[:, t, :], sni[:, t, :], tmi,
                                  [toks["qi", t], toks["ki", t], ang["i"], tacc.get(("o", t - 1))], "dve")
                        tacc["o", t] = o
                        tacc["c", t] = p.copy(I[:, t, 576:640], I[:, t, 512:576], o)

                def index_tiles():
                    for t in range(2):
                        tiles(I, iT, t, 0, 4, tacc["c", t], ready)
                        tiles(I, iT, t, 4, 1, tacc["c", t], ready)

                def index_head(h):
                    b = scratch()
                    r = slice(64 * (h % 2), 64 * (h % 2) + 64)
                    for t, o, n in segs:
                        tok = p.mm(b.t[:, o:o + n], iT[r, h // 2, t * 128:(t + 1) * 128], iT[r, 4, 0:n], True, True,
                                   [list(ready.values()), b.free], t == 1)
                    a = p.act(R[:, h % 2, :], b.t[:, 0:384], ACT.Relu, [tok, racc.get(h - 2)])
                    b.free = [a]
                    for t, o, n in segs:
                        if h == 0:
                            tacc[t] = p.ts(acc[:, o:o + n], R[:, 0, o:o + n], wi[:, t, 0:1], ALU.mult, waits=[a, toks["wi", t]])
                        else:
                            tacc[t] = p.stt(acc[:, o:o + n], R[:, h % 2, o:o + n], wi[:, t, h:h + 1], acc[:, o:o + n],
                                            ALU.mult, ALU.add, [a, tacc[t]])
                    racc[h] = [tacc[0], tacc[1]]
                    if h == 7:
                        tops[0] = tops[1] = p.tt(work[:, :], acc[:, :], const("causal"), ALU.add, [tacc[0], tacc[1], t_const])

                def top(n):
                    for _ in range(n):
                        for t, o, w in segs:
                            x = p.emit("dve", lambda e, t=t, o=o, w=w: e.max(m8[:, t, :], work[:, o:o + w]), [tops[t]])
                            tops[t] = p.emit("dve", lambda e, t=t, o=o, w=w: e.match_replace(
                                out=work[:, o:o + w], in_to_replace=m8[:, t, :], in_values=work[:, o:o + w], imm_value=GONE), [x])

                def q_turn():
                    for t in range(2):
                        q = Q[:, t, 0:1024].rearrange("p (h n) -> p h n", h=8)
                        toks["Q", t] = turns(q, 8, 16, csa[:, t, :], sna[:, t, :], tmq,
                                             [toks["q", 2, t], toks["q", 3, t], ang["a"], toks.get(("Q", t - 1))], "pool")

                def angle_tables():
                    ang["a"] = angles(d["positions_2"], const("inva"), 16, sna, csa, s, "posa")
                    ang["i"] = angles(d["positions_2"], const("invi"), 8, sni, csi, s, "posi")

                def during(i):
                    if i == 4:
                        index_turn()
                    if i == 6:
                        index_tiles()
                    if 8 <= i < 12:
                        index_head(2 * i - 16)
                        index_head(2 * i - 15)
                    if 12 <= i < 16:
                        top(2)
                    if i == 14:
                        q_turn()

                angle_tables()
                x_used[0] = linear("c_in", lhs, evac, during)
                flush()
                for t in range(2):
                    k = Q[:, t, 1024:1280].rearrange("p (h n) -> p h n", h=2)
                    toks["K", t] = turns(k, 2, 16, csa[:, t, :], sna[:, t, :], tmq, [toks["k", t], toks["Q", 1], toks.get(("K", t - 1))], "pool")
                for t in range(2):
                    tiles(Q, qT, t, 0, 4, toks["Q", t], dq)
                    tiles(Q, qT, t, 4, 4, toks["Q", t], dq)
                for t in range(2):
                    tiles(Q, qT, t, 8, 2, toks["K", t], dq)
                a = p.ts(acc[:, :], work[:, :], -2.0e38, ALU.is_le, 1.0, ALU.subtract, [tops[0], tops[1]])
                tsel = p.stt(acc[:, :], acc[:, :], -NEG, const("causal"), ALU.mult, ALU.add, [a])

                def scores(h, i):
                    return [(qT[:, h, i * 128:(i + 1) * 128], qT[:, 8 + h // 4, 0:128 * (i + 1)])]

                dep = attend("ds", 8, 128, segs, scores, lambda h, j: V[:, j, (h // 4) * 128:(h // 4 + 1) * 128],
                             128.0 ** -0.5, acc[:, :], tsel, lambda t, h, n: XN[:, t, h * 128:(h + n) * 128],
                             list(dq.values()), [toks["v", 0], toks["v", 1]])
                lhs = xn_halves(dep, XH, XL)
                x_used[0] = linear("c_out", lhs, full_mix)

        def last_part(l, lhs, name, nxt):
            with ExitStack() as s:
                sat, _ = small_at()
                a0, b0 = sat[f"pt{l}"]
                PT = sb(f"pl_p{l}", [128, 2, 256], F32, s)
                PH = sb(f"pl_h{l}", [128, 2, 256], F32R, s)
                PL = sb(f"pl_l{l}", [128, 2, 256], F32R, s)
                PJ = sb(f"pl_j{l}", [128, 2, D], F32, s)
                EH = sb(f"pl_eh{l}", [128, 8, 256], F32R, s)
                EL = sb(f"pl_el{l}", [128, 8, 256], F32R, s)
                tp = p.dma("sp", f"d_p{l}", PT[:, :, :], d["small"][:, a0:b0].rearrange("p (k n) -> p k n", k=2),
                           [x for x in p.last.values() if x])
                ph = {}

                def halve(i):
                    if i == 12:
                        h = p.act(PH[:, :, :], PT[:, :, :], waits=[tp])
                        h = p.tt(PL[:, :, :], PT[:, :, :], PH[:, :, :].bitcast(F32), ALU.subtract, [h])
                        for k in range(2):
                            ph[k, 0] = ph[k, 1] = h

                ffn(f"w13_{l}_1", f"w2_{l}_1", lhs, None, half_mix, None, halve)
                tj = {}

                def evac_p(c, w, bs):
                    for t, (b, tok) in enumerate(bs):
                        tj[c, t] = p.act(PJ[:, t, c * 512:(c + 1) * 512], b.t[:, :], waits=[tok])
                        b.free = [tj[c, t]]

                linear(f"ple_p{l}", lhs_of(PH, PL, ph), evac_p)
                lhs = layer_norm(EH, EL)

                def evac_g(c, w, bs):
                    cols = slice(c * 512, (c + 1) * 512)
                    toks = []
                    for t, (b, tok) in enumerate(bs):
                        a = p.act(XN[:, t, cols], b.t[:, :], ACT.Sigmoid, [tok, xn_used[0]])
                        b.free = [a]
                        a = p.tt(XN[:, t, cols], XN[:, t, cols], PJ[:, t, cols], ALU.mult, [a, tj[c, t]])
                        xt[t] = p.tt(X[:, t, cols], X[:, t, cols], XN[:, t, cols], ALU.add, [a, xt[t], x_piece[c, t]])
                        toks.append(xt[t])
                    return nxt(c, toks)

                linear(f"ple_g{l}", lhs, evac_g)

        norm_open()
        for c in range(2):
            norm_piece(c)()
        with ExitStack() as block1:
            MH = sb("MH", [128, 8, 256], F32R, block1)
            ML = sb("ML", [128, 8, 256], F32R, block1)
            for l in range(2):
                root_tok, lhs = norm_close()
                with ExitStack() as s:
                    todo = []
                    M = sb(f"xm_m{l}", [128, 2, D], F32, s)

                    def memory(i):
                        if i == 8:
                            todo.append(mem_norm(l, M))
                        if i == 20:
                            todo.pop()()

                    ffn(f"gu_pre{l}", f"dn_pre{l}", lhs, root_tok, half_add, norm_open, memory)
                if l == 0:
                    even_mixer()
                with ExitStack() as s:
                    kT = sb(f"xm_kT{l}", [128, 8, 256], F32, s)
                    V = sb(f"xm_v{l}", [128, 2, D], F32, s)
                    q = sb(f"xm_q{l}", [128, 2, 2, 256], F32, s)
                    p.fence()
                    it, t_k, vt, turned = mem_keys(l, kT, V, q, s)
                    fillers.append(it)
                    if l == 1:
                        mla_mixer()
                    fill(8)
                    mem_attention(l, kT, V, q, t_k, vt, turned)
                root_tok, lhs = norm_close()
                if l == 0:
                    ffn(f"gu_post{l}", f"dn_post{l}", lhs, root_tok, half_add, norm_open)
                else:
                    norm_last = lhs, root_tok
        lhs, root_tok = norm_last
        raw_got = {}

        def raw_piece(c, toks):
            def later():
                raw_got.update(turn_piece(X, c, toks, XH, XL, x_used[0]))

            return later

        def half_add_raw(c, w, bs):
            norm.clear()
            half_add(c, w, bs)
            return raw_piece(c, [xt[0], xt[1]])

        ffn("gu_post1", "dn_post1", lhs, root_tok, half_add_raw)

        t_out = []

        def store(c, toks):
            for t in range(2):
                cols = slice(c * 512, (c + 1) * 512)
                t_out.append(p.dma("sp", f"d_o{c}{t}", out[t * 128:(t + 1) * 128, cols], X[:, t, cols], [toks[t]]))

        for l in range(2):
            with ExitStack() as s:
                s5, tables = s5_tables(s) if l == 0 else (None, None)
                ffn(f"w13_{l}_0", f"w2_{l}_0", lhs_of(XH, XL, raw_got), None, half_mix, None, tables)
                lhs = layer_norm(XH, XL)
                if l == 0:
                    ab_mixer(s5, lhs)
                else:
                    dsa_mixer(lhs)
            lhs = layer_norm(XH, XL)
            raw_got.clear()
            last_part(l, lhs, None, store if l == 1 else raw_piece)
        flush()
        p.wait("sp", t_out)
        assert gain_now[0] == len(gains) and not fillers and not pending
        if order is None:
            return taken
        assert len(taken) == len(stream)

        block = ctx.enter_context(nc.Block())

        @block.sync
        def _(eng):
            for f in p.queue["sp"]:
                f(eng)

        @block.scalar
        def _(eng):
            for f in p.queue["act"]:
                f(eng)

        @block.vector
        def _(eng):
            for f in p.queue["dve"]:
                f(eng)

        @block.gpsimd
        def _(eng):
            for f in p.queue["pool"]:
                f(eng)

        @block.tensor
        def _(eng):
            for f in p.queue["pe"]:
                f(eng)


def interleave(a, b):
    k, n = a.shape
    return np.stack([a.reshape(k, n // 256, 256), b.reshape(k, n // 256, 256)], 2).reshape(k, 2 * n)


def lay_weights(v):
    m = {}
    for l in range(2):
        for k, n in (("pre", "ffn_pre"), ("post", "ffn_post")):
            gu = v[n + "_w_gu"][l]
            m[f"gu_{k}{l}"] = interleave(gu[:, :FF], gu[:, FF:])
            m[f"dn_{k}{l}"] = v[n + "_w_down"][l]
        m[f"x_kv{l}"], m[f"x_q{l}"], m[f"x_o{l}"] = v["xmem_wkv"][l], v["xmem_wq"][l], v["xmem_wo"][l]
        for j in range(2):
            m[f"w13_{l}_{j}"] = interleave(v["ffn_w1_2"][l, j], v["ffn_w3_2"][l, j])
            m[f"w2_{l}_{j}"] = v["ffn_w2_2"][l, j]
        m[f"ple_p{l}"], m[f"ple_g{l}"] = v["ple_w_proj_2"][l], v["ple_w_gate_2"][l]
    m["sbg_in"], m["sbg_out"] = v["sbg_w_in"][0], v["sbg_w_out"][0]
    m["mla_in"], m["mla_out"] = v["mla_w_in"][0], v["mla_w_out"][0]
    m["mla_uq"] = v["mla_w_uq"][0]
    ukv = v["mla_w_ukv"][0].reshape(256, 16, 128)
    m["mla_ukv"] = np.concatenate([ukv[:, :, :64].reshape(256, 1024), ukv[:, :, 64:].reshape(256, 1024)], 1)
    ab = v["ab_w_in_2"][0]
    m["ab_in"] = np.concatenate([ab[:, 1536:2048], ab[:, 0:512], ab[:, 1024:1536], ab[:, 512:1024]], 1)
    m["ab_out"], m["glu"] = v["ab_w_out_2"][0], v["s5_w_glu_2"][0]
    c = v["c_w_in_2"][0]
    m["c_in"], m["c_out"] = np.concatenate([c[:, 1536:2120], c[:, 0:1536]], 1), v["c_w_out_2"][0]
    out = {}
    for name, kts, widths in layers():
        w = m[name].reshape(kts, 128, -1)
        flat = np.empty(w.size, w.dtype)
        o = 0
        for _, k, nk, width, col in units_of(kts, widths):
            n = nk * 128 * width
            flat[o:o + n].reshape(128, nk, width)[...] = w[k:k + nk, :, col:col + width].transpose(1, 0, 2)
            o += n
        out["w_" + name] = flat
    return out


def lay_small(v):
    f = np.float32
    p = {}
    p["sguw"] = v["sgu_w"][0].transpose(2, 0, 1).reshape(128, 1024)
    p["sgub"] = v["sgu_b"][0].T
    p["convw"] = v["conv_w_2"][0].T.reshape(4, 128, 3).transpose(1, 0, 2).reshape(128, 12)
    p["dskip"] = v["s5_d_2"][0].reshape(4, 128).T
    p["bglu"] = v["s5_b_glu_2"][0].reshape(4, 128).T
    p["lre"] = v["s5_lam_re_2"][0].reshape(16, 128).T
    p["lim"] = v["s5_lam_im_2"][0].reshape(16, 128).T
    p["ldt"] = np.repeat(v["s5_log_dt_2"][0], 64).reshape(16, 128).T
    for n in ("re", "im"):
        b = np.zeros((4, 4, 2, 16, 2, 64), f)
        c = np.zeros((2, 64, 16, 2, 16), f)
        src = v[f"s5_b_{n}_2"][0].reshape(4, 4, 2, 64, 16)
        cs = v[f"s5_c_{n}_2"][0].reshape(16, 2, 16, 64)
        for g in range(2):
            b[:, :, g, :, g, :] = src[:, :, g].transpose(0, 1, 3, 2)
            c[g, :, :, g, :] = cs[:, g].transpose(2, 0, 1)
        p["b" + n] = b.reshape(4, 128, 128).transpose(1, 0, 2).reshape(128, 512)
        p["c" + n] = c.reshape(128, 512)
    for l in range(2):
        p[f"pt{l}"] = v["p_2"][l, 0].T.reshape(2, 128, 256).transpose(1, 0, 2).reshape(128, 512)
    return np.concatenate([p[n].astype(f, copy=False) for n, _ in SMALL], 1)


GAINS = ["ffn_pre_norm", "mix_norm", "sgu_ln_gain", "sgu_ln_bias", "mla_q_lora_gain", "mla_kv_lora_gain",
         "mla_q_gain", "mla_k_gain", "xmem_mem_norm", "xmem_k_gain", "xmem_norm", "xmem_q_gain", "ffn_post_norm",
         "ln_g_2", "ln_b_2"]


def kernel(**inputs):
    import concourse.bacc as bacc
    from concourse.bass_utils import run_bass_kernel_spmd

    v = {k: np.asarray(a) for k, a in inputs.items()}
    arrays = lay_weights(v)
    arrays["small"] = lay_small(v)
    arrays["consts"] = consts()[0]
    arrays["x"], arrays["mem"] = v["x"][0], v["mem"][0]
    for n in ("positions", "positions_2"):
        arrays[n] = v[n].reshape(2, 128).T
    for n in GAINS:
        arrays[n] = v[n]
    arrays = {n: np.ascontiguousarray(a) for n, a in arrays.items()}
    nc = bacc.Bacc("TRN2", target_bir_lowering=False, num_devices=1)
    d = {n: nc.dram_tensor("in_" + n, a.shape, mybir.dt.from_np(a.dtype), kind="ExternalInput").ap()
         for n, a in arrays.items()}
    out = nc.dram_tensor("out", (256, D), F32, kind="ExternalOutput").ap()
    order = build(bacc.Bacc("TRN2", target_bir_lowering=False, num_devices=1), d, out)
    build(nc, d, out, order)
    r = run_bass_kernel_spmd(nc, [{"in_" + n: a for n, a in arrays.items()}], core_ids=[0])
    return r.results[0]["out"].reshape(1, 256, D)
```

```python
from contextlib import ExitStack

import numpy as np

import concourse.bass as bass
from concourse import mybir

F32 = mybir.dt.float32
F32R = mybir.dt.float32r
I32 = mybir.dt.int32
ALU = mybir.AluOpType
ACT = mybir.ActivationFunctionType
AX = mybir.AxisListType

D = 1024
FF = 2816
UNIT = 1024
RAW = 4
SPLIT = 4
AHEAD = 3
RING = 3
NEG = -1.0e30
GONE = -3.0e38
ALPHA = 4.0 ** 0.25
MAGIC = 12582912.0
TWO_PI = (6.28125, 2029.0 / 2 ** 20, 2 * np.pi - 6.28125 - 2029.0 / 2 ** 20)

FFN_GU = [512] * 11
HALVES = [512, 512]


def layers():
    out = []
    for l in range(2):
        out += [(f"gu_pre{l}", 8, FFN_GU), (f"dn_pre{l}", 22, HALVES)]
        if l == 0:
            out += [("sbg_in", 8, [512] * 5), ("sbg_out", 8, HALVES)]
        else:
            out += [("mla_in", 8, [512, 288]), ("mla_uq", 4, [384] * 4), ("mla_ukv", 2, [512] * 4),
                    ("mla_out", 8, HALVES)]
        out += [(f"x_kv{l}", 8, [512] * 4), (f"x_q{l}", 8, HALVES), (f"x_o{l}", 8, HALVES)]
        out += [(f"gu_post{l}", 8, FFN_GU), (f"dn_post{l}", 22, HALVES)]
    for l in range(2):
        out += [(f"w13_{l}_0", 8, FFN_GU), (f"w2_{l}_0", 22, HALVES)]
        if l == 0:
            out += [("ab_in", 8, [512] * 4), ("glu", 4, [512]), ("ab_out", 8, HALVES)]
        else:
            out += [("c_in", 8, [512, 72] + [512] * 3), ("c_out", 8, HALVES)]
        out += [(f"w13_{l}_1", 8, FFN_GU), (f"w2_{l}_1", 22, HALVES)]
        out += [(f"ple_p{l}", 2, HALVES), (f"ple_g{l}", 8, HALVES)]
    return out


def units_of(kts, widths):
    out, col = [], 0
    for c, w in enumerate(widths):
        n = max(1, UNIT // w)
        for k in range(0, kts, n):
            out.append((c, k, min(n, kts - k), w, col))
        col += w
    return out


CONSTS = ["ident", "incl", "ones", "tril", "sbmask", "causal", "inv1", "inva", "invi"]


def consts():
    i = np.arange(128)
    k, q = i[:, None], np.arange(256)[None, :]
    ident = np.eye(128)
    incl = (i[:, None] >= i[None, :]) * 1.0
    tril = (i[:, None] <= i[None, :]) * 1.0
    sbmask = np.concatenate([np.where(k < q, 0.0, NEG), np.where(k < i[None, :], 0.0, NEG)], 1)
    causal = np.concatenate([np.where(i[None, :] <= k, 0.0, NEG), np.where(q <= k + 128, 0.0, NEG)], 1)

    def inv(theta, half):
        e = -np.arange(half, dtype=np.float32) / np.float32(half)
        return np.broadcast_to(np.float32(theta) ** e, (128, half))

    parts = [ident, incl, np.ones((128, 128)), tril, sbmask, causal,
             inv(10000.0, 16), inv(500000.0, 16), inv(500000.0, 8)]
    at, o = {}, 0
    for name, p in zip(CONSTS, parts):
        at[name] = (o, o + p.shape[1])
        o += p.shape[1]
    return np.concatenate([p.astype(np.float32) for p in parts], 1), at


SMALL = [("sguw", 1024), ("sgub", 8), ("convw", 12), ("dskip", 4), ("bglu", 4),
         ("lre", 16), ("lim", 16), ("ldt", 16), ("bre", 512), ("bim", 512), ("cre", 512), ("cim", 512),
         ("pt0", 512), ("pt1", 512)]


def small_at():
    at, o = {}, 0
    for name, w in SMALL:
        at[name] = (o, o + w)
        o += w
    return at, o


class Program:

    def __init__(self, nc, ctx):
        self.nc = nc
        self.ctx = ctx
        self.queue = {e: [] for e in ("pe", "act", "dve", "pool", "sp")}
        self.sem = {e: ctx.enter_context(nc.semaphore("s_" + e)) for e in ("pe", "act", "dve", "pool")}
        self.count = {}
        self.seen = {e: {} for e in self.queue}
        self.last = {e: None for e in ("pe", "act", "dve", "pool")}

    def wait(self, e, waits):
        need = {}

        def gather(x):
            if x is None:
                return
            if isinstance(x, tuple) and len(x) == 2 and isinstance(x[0], str):
                need[x[0]] = max(need.get(x[0], 0), x[1])
            else:
                for y in x:
                    gather(y)

        gather(waits)
        for s, v in need.items():
            if self.seen[e].get(s, 0) < v:
                self.seen[e][s] = v
                self.queue[e].append(lambda eng, s=s, v=v: eng.wait_ge(self.sem[s], v))

    def emit(self, e, fn, waits=(), inc=True):
        self.wait(e, waits)
        if not inc:
            self.queue[e].append(lambda eng: fn(eng))
            return None
        self.count[e] = self.count.get(e, 0) + 1
        self.queue[e].append(lambda eng: fn(eng).then_inc(self.sem[e], 1))
        self.last[e] = (e, self.count[e])
        return self.last[e]

    def dma(self, e, s, out, in_, waits=()):
        if s not in self.sem:
            self.sem[s] = self.ctx.enter_context(self.nc.semaphore(s))
        self.wait(e, waits)
        self.count[s] = self.count.get(s, 0) + 16
        self.queue[e].append(lambda eng: eng.dma_start(out, in_).then_inc(self.sem[s], 16))
        return (s, self.count[s])

    def fence(self):
        done = [t for t in self.last.values() if t]
        for e in ("act", "dve", "pool"):
            self.wait(e, done)

    def act(self, out, in_, func=ACT.Copy, waits=(), bias=0.0, scale=1.0, accum=None):
        if func == ACT.Copy:
            return self.emit("act", lambda e: e.activation(out, in_, func, scale=scale), waits)
        if accum is None:
            return self.emit("act", lambda e: e.activation(out, in_, func, bias=bias, scale=scale), waits)
        return self.emit("act", lambda e: e.activation(out, in_, func, bias=bias, scale=scale, accum_out=accum), waits)

    def tt(self, out, a, b, op, waits=(), e="dve"):
        return self.emit(e, lambda g: g.tensor_tensor(out, a, b, op), waits)

    def ts(self, out, a, s1, op0, s2=None, op1=ALU.bypass, waits=(), e="dve"):
        if s2 is None:
            return self.emit(e, lambda g: g.tensor_scalar(out, a, s1, None, op0), waits)
        return self.emit(e, lambda g: g.tensor_scalar(out, a, s1, s2, op0, op1), waits)

    def stt(self, out, a, s, b, op0, op1, waits=()):
        return self.emit("dve", lambda g: g.scalar_tensor_tensor(out=out, in0=a, scalar=s, in1=b, op0=op0, op1=op1), waits)

    def copy(self, out, a, waits=(), e="dve"):
        return self.emit(e, lambda g: g.tensor_copy(out, a), waits)

    def recip(self, out, a, waits=()):
        return self.emit("dve", lambda g: g.reciprocal(out, a), waits)

    def reduce(self, out, a, op, waits=(), negate=False):
        return self.emit("dve", lambda g: g.tensor_reduce(out, a, AX.X, op, negate=negate), waits)

    def memset(self, out, v, waits=(), e="dve"):
        return self.emit(e, lambda g: g.memset(out, v), waits)

    def mm(self, out, l, r, start, stop, waits=(), inc=False):
        return self.emit("pe", lambda e: e.matmul(out, l, r, start=start, stop=stop), waits, inc)

    def tr(self, out, in_, ident, waits=(), inc=False):
        return self.emit("pe", lambda e: e.transpose(out, in_, ident), waits, inc)


class Bank:
    def __init__(self, t):
        self.t = t
        self.free = []


def build(nc, d, out, order=None):
    shape_of = {name: (kts, widths) for name, kts, widths in layers()}
    taken = []
    ctx = ExitStack()
    with ctx:
        p = Program(nc, ctx)

        def sb(name, shape, dt=F32, where=None):
            return (where or ctx).enter_context(nc.sbuf_tensor(name, shape, dt))

        X = sb("X", [128, 2, D])
        XN = sb("XN", [128, 2, D])
        XH = sb("XH", [128, 8, 256], F32R)
        XL = sb("XL", [128, 8, 256], F32R)
        raw = [sb(f"raw{i}", [128, UNIT]) for i in range(RAW)]
        whi = [sb(f"whi{i}", [128, UNIT], F32R) for i in range(SPLIT)]
        wlo = [sb(f"wlo{i}", [128, UNIT], F32R) for i in range(SPLIT)]
        gain_sb = [sb(f"gain{i}", [128, D]) for i in range(RING)]
        cat, cn = consts()[1], consts()[0].shape[1]
        C = sb("C", [128, cn])
        st = sb("st", [128, 64])
        banks = [Bank(ctx.enter_context(nc.psum_tensor(f"bank{i}", [128, 512], F32))) for i in range(8)]
        turn = [0, 0]
        spare = [4, 5, 6, 7]
        held = [False, False]

        def const(name):
            a, b = cat[name]
            return C[:, a:b]

        tx = [p.dma("sp", "d_x0", X[:, 0, :], d["x"][0:128, :]), None]
        ident = const("ident")

        def scratch():
            turn[0] += 1
            return banks[spare[turn[0] % len(spare)]]

        def pair():
            turn[1] += 1
            i = turn[1] % 2 if not held[turn[1] % 2] else 1 - turn[1] % 2
            assert not held[i]
            held[i] = True
            return banks[2 * i], banks[2 * i + 1]

        def close(bs):
            held[0 if bs[0] is banks[0] else 1] = False

        stream = []
        for name, i in order or ():
            us = units_of(*shape_of[name])
            stream.append((name, 128 * sum(u[2] * u[3] for u in us[:i]), us[i][2] * us[i][3]))
        t_load, t_split, t_used = {}, {}, {}

        def load(u):
            if u >= len(stream):
                return
            name, off, n = stream[u]
            t_load[u] = p.dma("sp", f"d_raw{u % RAW}", raw[u % RAW][:, 0:n],
                              d["w_" + name][off:off + 128 * n].rearrange("(p w) -> p w", p=128),
                              [t_split[u - RAW]] if u >= RAW else [])

        split_next = [0]
        lag, highs, lows = [False], [], []

        def split_to(u, e="dve"):
            while split_next[0] <= min(u, len(stream) - 1):
                v = split_next[0]
                n = stream[v][2]
                src, hi, lo = raw[v % RAW][:, 0:n], whi[v % SPLIT][:, 0:n], wlo[v % SPLIT][:, 0:n]
                free = t_used[v - SPLIT] if v >= SPLIT else None

                def low(v, src, hi, lo, free, th):
                    t_split[v] = p.tt(lo, src, hi.bitcast(F32), ALU.subtract, [th, t_load[v], free], e)
                    load(v + RAW)

                def high(v=v, src=src, hi=hi, lo=lo, free=free):
                    th = p.act(hi, src, waits=[t_load[v], free])
                    lows.append(lambda: low(v, src, hi, lo, free, th))

                highs.append(high)
                split_next[0] += 1
                if not lag[0]:
                    settle()

        def settle(high=True, low=True):
            for todo, now in (highs, high), (lows, low):
                while now and todo:
                    todo.pop(0)()

        pending = []

        def flush(*tiles):
            todo = [x for x in pending if not tiles or x[0] in tiles]
            pending[:] = [x for x in pending if x not in todo]
            for _, f in todo:
                f()

        def flush_one(tile):
            x = next((x for x in pending if x[0] == tile), None)
            if x:
                pending.remove(x)
                x[1]()

        def put_off(later):
            if later:
                pending.extend(later if isinstance(later, list) else [(None, later)])

        def weights(name, i, nk, w, ahead=AHEAD):
            u = len(taken)
            taken.append((name, i))
            settle()
            if order is None:
                t_split[u] = None
            else:
                assert order[u] == (name, i)
                split_to(u + ahead)
                if not ahead:
                    settle()
            hi = whi[u % SPLIT][:, 0:nk * w].rearrange("p (k w) -> p k w", k=nk)
            lo = wlo[u % SPLIT][:, 0:nk * w].rearrange("p (k w) -> p k w", k=nk)
            return u, hi, lo

        def unit(b, lhs, kts, w, u, hi, lo, k0, nk, t, mark, toks):
            for k in range(nk):
                kt = k0 + k
                xh, xl, dep = lhs(kt, t)
                o = b.t[:, 0:w]
                p.mm(o, xh, hi[:, k, :], kt == 0, False, [dep, t_split[u], b.free])
                p.mm(o, xh, lo[:, k, :], False, False)
                toks[t] = p.mm(o, xl, hi[:, k, :], False, kt == kts - 1, inc=kt == kts - 1 or mark and k == nk - 1)

        def steps(name, lhs, evac, tail=False, hold=False, late=1):
            kts, widths = shape_of[name]
            us = units_of(kts, widths)
            for c, w in enumerate(widths):
                bs = pair()
                toks = [None, None]
                mine = [(i, x) for i, x in enumerate(us) if x[0] == c]
                first = c == 0 and not hold and len(mine) <= SPLIT
                last = tail and c == len(widths) - 1
                alone = 0 if first else len(mine) - min(SPLIT, len(mine)) if last else len(mine)

                def products(u, hi, lo, k0, nk, t, mark):
                    unit(bs[t], lhs, kts, w, u, hi, lo, k0, nk, t, mark, toks)

                for j, (i, (_, k0, nk, _, _)) in enumerate(mine[:alone]):
                    u, hi, lo = weights(name, i, nk, w)
                    for k in range(nk):
                        for t in range(2):
                            products(u, hi[:, k:k + 1, :], lo[:, k:k + 1, :], k0 + k, 1, t, t == 1 and k == nk - 1)
                    t_used[u] = toks[1]
                    if j == min(late, len(mine) - 1) and not hold:
                        flush()
                    if j < len(mine) - 1:
                        yield
                if alone < len(mine):
                    if first:
                        flush(None, 0)
                    got = [weights(name, i, x[2], w, 0) for i, x in mine[alone:]]
                    for j, (i, x) in enumerate(mine[alone:]):
                        if first and j == len(got) - 1:
                            flush_one(1)
                        products(*got[j], x[1], x[2], 0, False)
                        if not first and j == 1:
                            flush()
                    if last:
                        put_off(evac(c, w, [(0, bs[0], toks[0])]))
                    if first:
                        flush(1)
                    for j, (i, x) in enumerate(mine[alone:]):
                        if last and j == len(got) - 1:
                            flush_one(0)
                        products(*got[j], x[1], x[2], 1, True)
                        t_used[got[j][0]] = toks[1]
                        if order is not None and not (last and j == len(mine) - 1 - alone):
                            split_to(got[j][0] + SPLIT, "pool" if last else "dve")
                        if j < len(mine) - 1 - alone:
                            yield
                    if last:
                        flush(0)
                        if order is not None:
                            split_to(got[-1][0] + SPLIT, "pool")
                        put_off(evac(c, w, [(1, bs[1], toks[1])]))
                if not last:
                    put_off(evac(c, w, [(t, bs[t], toks[t]) for t in range(2)]))
                close(bs)
                yield

        def linear(name, lhs, evac, between=None, tail=False, hold=False):
            for i, _ in enumerate(steps(name, lhs, evac, tail, hold)):
                if between:
                    between(i)
            return t_used[len(taken) - 1] if not between else p.last["pe"]

        fillers = []

        def fill(n, late=False):
            while n and fillers:
                lag[0] = late
                if next(fillers[0], "end") == "end":
                    fillers.pop(0)
                lag[0] = False
                n -= 1

        x_used = [None]

        def to_halves(src, kts, hi, lo, dep, war=None, first=0):
            got = {}
            for t in range(2):
                for g in range(0, kts, 4):
                    n = min(4, kts - g)
                    b = scratch()
                    for k in range(n):
                        tok = p.tr(b.t[:, k * 128:(k + 1) * 128], src(t, g + k), ident,
                                   [dep[t], b.free, t_const], k == n - 1)
                    v = b.t[:, 0:n * 128].rearrange("p (k n) -> p k n", k=n)
                    h = hi[:, first + g:first + g + n, t * 128:(t + 1) * 128]
                    th = p.act(h, v, waits=[tok, war])
                    tl = p.tt(lo[:, first + g:first + g + n, t * 128:(t + 1) * 128], v, h.bitcast(F32),
                              ALU.subtract, [th, war])
                    b.free = [tl]
                    for k in range(n):
                        got[g + k, t] = tl
            return got

        def lhs_of(hi, lo, got, first=0):
            return lambda kt, t: (hi[:, first + kt, t * 128:(t + 1) * 128],
                                  lo[:, first + kt, t * 128:(t + 1) * 128], got[kt, t])

        gains = [d["ffn_pre_norm"][0]]
        for l in range(2):
            gains += [d["xmem_mem_norm"][l], d["mix_norm"][l], d["xmem_norm"][l], d["ffn_post_norm"][l]]
            if l == 0:
                gains += [d["ffn_pre_norm"][1]]
        for l in range(2):
            for j in range(3):
                gains += [d["ln_g_2"][l, j], d["ln_b_2"][l, j]]
        gain_tok, gain_now = {}, [0]

        def gain_load(i, waits=()):
            if i < len(gains):
                n = gains[i].shape[0]
                gain_tok[i] = p.dma("sp", f"d_gain{i % RING}", gain_sb[i % RING][:, 0:n], gains[i].partition_broadcast(128), waits)

        gain_load(0)
        t_ident = p.dma("sp", "d_ident", C[:, 0:128], d["consts"][:, 0:128])
        load(0)
        tx[1] = p.dma("sp", "d_x1", X[:, 1, :], d["x"][128:256, :])
        load(1)
        t_const = [t_ident, p.dma("sp", "d_const", C[:, 128:], d["consts"][:, 128:])]
        for u in range(2, RAW):
            load(u)
        for i in range(1, RING):
            gain_load(i)

        def gain():
            i = gain_now[0]
            gain_now[0] += 1
            return i, gain_sb[i % RING][:, 0:gains[i].shape[0]], gain_tok[i]

        def gain_done(i, tok):
            gain_load(i + RING, [tok])

        def row(name, src, s):
            n = src.shape[0]
            m = sb("row_" + name, [128, n], F32, s)
            return m[:, :], p.dma("sp", "d_row_" + name, m[:, :], src.partition_broadcast(128), [x for x in p.last.values() if x])

        def rstd_of(ss, n, inv_n, eps, waits):
            a = p.ts(ss, ss, inv_n, ALU.mult, eps, ALU.add, waits)
            b = p.act(ss, ss, ACT.Sqrt, [a])
            return p.recip(ss, ss, [b])

        xt = tx
        warm_tok = [None]

        def warm(func):
            warm_tok[0] = p.act(st[:, 60:61], C[:, 0:1], func, [t_ident, warm_tok[0]])

        xn_used = [None]
        part = sb("part", [128, 2, 2])
        root = sb("root", [128, 2])
        junk = sb("junk", [128, 2, 512])
        norm = {}
        junk_tok = [None, None]

        def square(i, src, total, waits):
            junk_tok[i] = p.act(junk[:, i, 0:src.shape[1]], src, ACT.Square, [waits, junk_tok[i]], accum=total)
            return junk_tok[i]

        def norm_open():
            norm.clear()
            norm["i"], norm["g"], norm["gt"] = gain()
            warm(ACT.Sqrt)
            norm["got"] = {}
            norm["war"] = x_used[0]

        def norm_piece(c, t):
            cols = slice(c * 512, (c + 1) * 512)
            tok = p.tt(XN[:, t, cols], X[:, t, cols], norm["g"][:, cols], ALU.mult, [xt[t], norm["gt"], xn_used[0]])
            norm["s", t, c] = square(t, X[:, t, cols], part[:, c, t:t + 1], [xt[t], norm.get("r")])
            norm["m", c, t] = tok

            def later():
                norm["got"].update(turn_piece(XN, c, t, tok, XH, XL, norm["war"]))
                xn_used[0] = p.last["pe"]

            return t, later

        def norm_close():
            gain_done(norm["i"], [norm["m", 1, 0], norm["m", 1, 1]])
            a = p.tt(root[:, :], part[:, 0, :], part[:, 1, :], ALU.add, [norm["s", t, c] for t in range(2) for c in range(2)])
            norm["r"] = rstd_of(root[:, :], 2, 1.0 / D, 1e-6, [a])
            return norm["r"], lhs_of(XH, XL, norm["got"])

        def turn_piece(src, c, t, dep, hi, lo, war):
            b = scratch()
            for k in range(4):
                tok = p.tr(b.t[:, k * 128:(k + 1) * 128], src[:, t, c * 512 + k * 128:c * 512 + (k + 1) * 128], ident,
                           [dep, b.free, t_ident], k == 3)
            v = b.t[:, :].rearrange("p (k n) -> p k n", k=4)
            h = hi[:, 4 * c:4 * c + 4, t * 128:(t + 1) * 128]
            th = p.act(h, v, waits=[tok, war])
            tl = p.tt(lo[:, 4 * c:4 * c + 4, t * 128:(t + 1) * 128], v, h.bitcast(F32), ALU.subtract, [th, war])
            b.free = [tl]
            return {(4 * c + k, t): tl for k in range(4)}

        def add_x(c, w, bs):
            for t, b, tok in bs:
                xs = X[:, t, c * 512:c * 512 + w]
                xt[t] = p.tt(xs, b.t[:, 0:w], xs, ALU.add, [tok, xt[t]])
                b.free = [xt[t]]
            return [norm_piece(c, t) for t, b, tok in bs]

        phase = [0]

        def ffn(gu, dn, lhs, root_tok, post, opens=None, between=None):
            phase[0] += 1
            n = phase[0]
            p.fence()
            with ExitStack() as s:
                HH = sb(f"HH{n}", [128, 22, 256], F32R, s)
                HL = sb(f"HL{n}", [128, 22, 256], F32R, s)
                sg = sb(f"sg{n}", [128, 2, 2, 256], F32, s)
                hb = sb(f"hb{n}", [128, 2, 2, 256], F32, s)
                ready, turned = {}, {}

                def evac(c, w, bs):
                    toks = []
                    for t, b, tok in bs:
                        a = p.act(sg[:, c % 2, t, :], b.t[:, 0:256], ACT.Silu, [tok, turned.get(c - 2), root_tok],
                                  scale=root[:, t:t + 1] if root_tok else 1.0)
                        if root_tok:
                            h = p.stt(hb[:, c % 2, t, :], b.t[:, 256:512], root[:, t:t + 1], sg[:, c % 2, t, :],
                                      ALU.mult, ALU.mult, [a, tok, turned.get(c - 2)])
                        else:
                            h = p.tt(hb[:, c % 2, t, :], sg[:, c % 2, t, :], b.t[:, 256:512], ALU.mult,
                                     [a, tok, turned.get(c - 2)])
                        b.free = [h]
                        toks.append(h)

                    def later():
                        b = scratch()
                        for k in range(2):
                            for t in range(2):
                                tok = p.tr(b.t[:, (2 * k + t) * 128:(2 * k + t + 1) * 128],
                                           hb[:, c % 2, t, k * 128:(k + 1) * 128], ident,
                                           [toks[t], b.free], k == 1 and t == 1)
                        turned[c] = tok
                        v = b.t[:, :].rearrange("p (k n) -> p k n", k=2)
                        hh = HH[:, 2 * c:2 * c + 2, :]
                        th = p.act(hh, v, waits=[tok])
                        tl = p.tt(HL[:, 2 * c:2 * c + 2, :], v, hh.bitcast(F32), ALU.subtract, [th])
                        b.free = [tl]
                        ready[2 * c] = ready[2 * c + 1] = tl

                    return later

                x_used[0] = linear(gu, lhs, evac, between)
                if opens:
                    opens()

                def hidden(kt, t):
                    return HH[:, kt, t * 128:(t + 1) * 128], HL[:, kt, t * 128:(t + 1) * 128], ready[kt]

                linear(dn, hidden, post, tail=True)

        def half_add(c, w, bs):
            for t, b, tok in bs:
                xs = X[:, t, c * 512:c * 512 + w]
                xt[t] = p.stt(xs, b.t[:, 0:w], 0.5, xs, ALU.mult, ALU.add, [tok, xt[t]])
                b.free = [xt[t]]
            return [norm_piece(c, t) for t, b, tok in bs] if norm else None

        bn = sb("bn", [128, 2, 2, 6])
        mv = sb("mv", [128, 2, 2])
        ln = {}

        def ln_open(hi, lo):
            ln.clear()
            ln["gi"], ln["g"], ln["gt"] = gain()
            ln["bi"], ln["b"], ln["bt"] = gain()
            ln["hi"], ln["lo"], ln["got"] = hi, lo, {}
            warm(ACT.Sqrt)

        def half_mix(c, w, bs, factor=0.5):
            out = []
            for t, b, tok in bs:
                xs = X[:, t, c * 512:c * 512 + w]
                xt[t] = p.stt(xs, b.t[:, 0:w], factor / ALPHA, xs, ALU.mult, ALU.add, [tok, xt[t], x_used[0]])
                b.free = [xt[t]]
                ln[t, c] = p.emit("dve", lambda e, t=t, xs=xs: e.bn_stats(bn[:, t, c, :], xs), [xt[t]])
                if c == 1:
                    out.extend(ln_row(t))
            return out

        def full_mix(c, w, bs):
            return half_mix(c, w, bs, 1.0)

        def ln_row(t):
            a = p.emit("dve", lambda e: e.bn_aggr(mv[:, t, :], bn[:, t, :, :].rearrange("p c n -> p (c n)")), [ln[t, 0], ln[t, 1]])
            r = rstd_of(mv[:, t, 1:2], 1, 1.0, 1e-5 / ALPHA ** 2, [a])
            toks = []
            for c in range(2):
                xs = X[:, t, c * 512:(c + 1) * 512]
                m = p.stt(xs, xs, mv[:, t, 0:1], ln["g"][:, c * 512:(c + 1) * 512], ALU.subtract, ALU.mult, [a, ln["gt"]])
                xt[t] = p.stt(xs, xs, mv[:, t, 1:2], ln["b"][:, c * 512:(c + 1) * 512], ALU.mult, ALU.add, [r, m, ln["bt"]])
                toks.append(xt[t])
            ln["done", t] = xt[t]
            mine, war = dict(ln), x_used[0]

            return [(t, lambda c=c: mine["got"].update(turn_piece(X, c, t, toks[c], mine["hi"], mine["lo"], war))) for c in range(2)]

        def ln_close():
            for i in (ln["gi"], ln["bi"]):
                gain_done(i, [ln["done", 0], ln["done", 1]])
            return lhs_of(ln["hi"], ln["lo"], ln["got"])

        def sincos(sn, cs, ang, tmp, waits):
            a = p.ts(tmp, ang, float(1 / (2 * np.pi)), ALU.mult, MAGIC, ALU.add, waits)
            a = p.ts(tmp, tmp, MAGIC, ALU.subtract, waits=[a])
            for part in TWO_PI:
                a = p.stt(ang, tmp, -float(part), ang, ALU.mult, ALU.add, [a])
            a = p.ts(ang, ang, 3.1415925, ALU.min, -3.1415925, ALU.max, [a])
            b = p.act(sn, ang, ACT.Sin, [a])
            c = p.act(cs, ang, ACT.Sin, [a], scale=0.5)
            c = p.tt(cs, cs, cs, ALU.mult, [c])
            c = p.ts(cs, cs, -2.0, ALU.mult, 1.0, ALU.add, [c])
            return [b, c]

        def attend(*args, during=None):
            for i, _ in enumerate(attend_steps(*args)):
                if during:
                    during(i)

        def attend_steps(name, heads, dv, segs, scores, values, scale, bias, bt, dst, dep, vdep, hi, lo, got):
            nb = 4
            width = sum(s[2] for s in segs)
            hpb = 512 // dv
            blocks = [(t, o + 128 * j, j, n // 128) for t, o, n in segs for j in range(n // 128)]
            with ExitStack() as s:
                S = sb(name + "S", [128, nb, width], F32, s)
                PT = sb(name + "PT", [128, nb, width], F32, s)
                nm = sb(name + "nm", [128, heads, 2], F32, s)
                rs = sb(name + "rs", [128, 2, heads], F32, s)
                t_exp, t_turn, t_pt, t_pv, obanks, outs, pieces = {}, {}, {}, {}, {}, {}, []

                def score(h):
                    b = scratch()
                    for i, (t, o, n) in enumerate(segs):
                        parts = scores(h, i)
                        for j, (l, r) in enumerate(parts):
                            tok = p.mm(b.t[:, o:o + n], l, r, j == 0, j == len(parts) - 1,
                                       [dep(h), b.free], j == len(parts) - 1 and i == len(segs) - 1)
                    src = b.t[:, 0:width]
                    war = t_turn.get(h - nb)
                    if bias is not None:
                        if callable(scale):
                            a = [p.stt(S[:, h % nb, o:o + n], src[:, o:o + n], scale(h, t), bias[:, o:o + n], ALU.mult, ALU.add,
                                       [tok, bt, war]) for t, o, n in segs]
                        else:
                            a = [p.stt(S[:, h % nb, :], src, scale, bias, ALU.mult, ALU.add, [tok, bt, war])]
                        b.free = a
                        src = S[:, h % nb, :]
                    else:
                        a = tok
                    es, ms = [], []
                    for i, (t, o, n) in enumerate(segs):
                        m = p.reduce(nm[:, h, t:t + 1], src[:, o:o + n], ALU.max, [a], negate=True)
                        if bias is None:
                            m = p.ts(nm[:, h, t:t + 1], nm[:, h, t:t + 1], scale, ALU.mult, waits=[m])
                        ms.append(m)
                    for i, (t, o, n) in enumerate(segs):
                        es.append(p.act(S[:, h % nb, o:o + n], src[:, o:o + n], ACT.Exp, [ms, war],
                                        bias=nm[:, h, t:t + 1], scale=1.0 if bias is not None else scale,
                                        accum=rs[:, t, h:h + 1]))
                    if bias is None:
                        b.free = es
                    t_exp[h] = es

                def turn_p(h):
                    b = scratch()
                    for i, (t, o, j, n) in enumerate(blocks):
                        tok = p.tr(b.t[:, i * 128:(i + 1) * 128], S[:, h % nb, o:o + 128], ident,
                                   [t_exp[h], b.free], i == len(blocks) - 1)
                    t_turn[h] = tok
                    t_pt[h] = p.act(PT[:, h % nb, :], b.t[:, 0:width], waits=[tok, t_pv.get(h - nb)])
                    b.free = [t_pt[h]]

                def pv(h):
                    if h % hpb == 0:
                        obanks[h // hpb] = pair()
                    ob = obanks[h // hpb]
                    for i, (t, o, j, n) in enumerate(blocks):
                        v = values(h, j)
                        tok = p.mm(ob[t].t[:, (h % hpb) * dv:(h % hpb + 1) * dv], PT[:, h % nb, i * 128:(i + 1) * 128], v,
                                   j == 0, j == n - 1, [t_pt[h], vdep, ob[t].free], i == len(blocks) - 1)
                    t_pv[h] = tok
                    if h % hpb == hpb - 1:
                        h0 = h - hpb + 1
                        for t in range(2):
                            r = p.recip(rs[:, t, h0:h + 1], rs[:, t, h0:h + 1], [t_exp[x] for x in range(h0, h + 1)])
                            outs[t] = p.tt(dst(t, h0, hpb).rearrange("p (h d) -> p h d", h=hpb),
                                           ob[t].t[:, 0:hpb * dv].rearrange("p (h d) -> p h d", h=hpb),
                                           rs[:, t, h0:h + 1].unsqueeze(2).broadcast_to([128, hpb, dv]),
                                           ALU.mult, [r, tok, xn_used[0]])
                            ob[t].free = [outs[t]]
                            pieces.append((t, lambda c=h // hpb, t=t, tok=outs[t]: got.update(turn_piece(XN, c, t, tok, hi, lo, None))))
                        close(ob)

                for i in range(heads + 3):
                    if pieces:
                        for _, f in pieces:
                            f()
                        pieces.clear()
                    if 2 <= i < heads + 2:
                        turn_p(i - 2)
                    settle(low=False)
                    if i < heads:
                        score(i)
                    settle()
                    if i >= 3:
                        pv(i - 3)
                    yield outs
                put_off(list(pieces))


        def even_mixer(others):
            root_tok, lhs = norm_close()
            with ExitStack() as s:
                sat, _ = small_at()
                W = sb("sguw", [128, 8, 128], F32, s)
                sbias = sb("sgub", [128, 8], F32, s)
                qT = sb("ev_qT", [128, 4, 256], F32, s)
                kT = sb("ev_kT", [128, 4, 256], F32, s)
                V = sb("ev_v", [128, 2, 512], F32, s)
                U = sb("ev_u", [128, 2, 512], F32, s)
                G = sb("ev_g", [128, 2, 512], F32, s)
                Z = sb("ev_z", [128, 8, 384], F32, s)
                E = sb("ev_e", [128, 4, 384], F32, s)
                SP = sb("ev_sp", [128, 4, 384], F32, s)
                OH = sb("ev_oh", [128, 8, 256], F32R, s)
                OL = sb("ev_ol", [128, 8, 256], F32R, s)
                Q = E[:, :, :].rearrange("p h n -> p (h n)")[:, 0:1024].rearrange("p (t n) -> p t n", t=2)
                done = [x for x in p.last.values() if x]
                tw = p.dma("sp", "d_sguw", W[:, :, :], d["small"][:, sat["sguw"][0]:sat["sguw"][1]].rearrange("p (g n) -> p g n", g=8), done)
                tb = p.dma("sp", "d_sgub", sbias[:, :], d["small"][:, sat["sgub"][0]:sat["sgub"][1]], done)
                g, gt = row("sgu_g", d["sgu_ln_gain"][0], s)
                bb, bt = row("sgu_b", d["sgu_ln_bias"][0], s)
                twm = p.tt(W[:, :, :], W[:, :, :], const("tril").unsqueeze(1).broadcast_to([128, 8, 128]), ALU.mult,
                           [tw, t_const], "pool")
                turned = [None]
                ready, sgu, osg = {}, [None, None], [None, None]

                def evac(c, w, bs):
                    if c in (2, 3):
                        toks = []
                        for t, b, tok in bs:
                            a = p.act(Q[:, t, :], b.t[:, :], waits=[tok, turned[0], root_tok], scale=root[:, t:t + 1])
                            b.free = [a]
                            toks.append(a)

                        def later():
                            dst = (qT, kT)[c - 2]
                            for t in range(2):
                                b = scratch()
                                for k in range(4):
                                    tok = p.tr(b.t[:, k * 128:(k + 1) * 128], Q[:, t, k * 128:(k + 1) * 128], ident,
                                               [toks[t], b.free], k == 3)
                                turned[0] = tok
                                ready[c, t] = p.copy(dst[:, :, t * 128:(t + 1) * 128],
                                                     b.t[:, :].rearrange("p (k n) -> p k n", k=4), [tok])
                                b.free = [ready[c, t]]

                        return later
                    for t, b, tok in bs:
                        f = ACT.Copy if c == 4 else ACT.Gelu_apprx_tanh
                        dst, key = {0: (U, "u"), 1: (G, "g"), 4: (V, "v")}[c]
                        ready[key, t] = p.act(dst[:, t, :], b.t[:, :], f, [tok, root_tok], scale=root[:, t:t + 1])
                        b.free = [ready[key, t]]

                def sgu_norm():
                    a = []
                    for t in range(2):
                        x = p.emit("dve", lambda e, t=t: e.bn_stats(bn[:, t, 0, :], G[:, t, :]), [ready["g", t]])
                        a.append(p.emit("dve", lambda e, t=t: e.bn_aggr(mv[:, t, :], bn[:, t, 0, :]), [x]))
                    r = rstd_of(mv[:, :, 1], 2, 1.0, 1e-6, a)
                    for t in range(2):
                        m = p.stt(G[:, t, :], G[:, t, :], mv[:, t, 0:1], g, ALU.subtract, ALU.mult, [a[t], gt])
                        sgu[t] = p.stt(G[:, t, :], G[:, t, :], mv[:, t, 1:2], bb, ALU.mult, ALU.add, [r, m, bt])

                def spatial(t):
                    b = scratch()
                    for j in range(8):
                        tok = p.mm(b.t[:, j * 64:(j + 1) * 64], W[:, j, :], G[:, t, j * 64:(j + 1) * 64], True, True,
                                   [sgu[t], twm, b.free], j == 7)
                    for j in range(8):
                        osg[t] = p.stt(XN[:, t, 512 + j * 64:512 + (j + 1) * 64], b.t[:, j * 64:(j + 1) * 64], sbias[:, j:j + 1],
                                       U[:, t, j * 64:(j + 1) * 64], ALU.add, ALU.mult, [tok, tb, ready["u", t], xn_used[0]])
                    b.free = [osg[t]]

                tz, te, tsp, tw_, tcum, tsub = {}, {}, {}, {}, {}, {}

                def logits(h):
                    b = scratch()
                    r = slice(64 * (h % 2), 64 * (h % 2) + 64)
                    p.mm(b.t[:, 0:256], kT[r, h // 2, 0:128], qT[r, h // 2, :], True, True,
                         [[ready[c, t] for c in (2, 3) for t in range(2)], b.free])
                    tok = p.mm(b.t[:, 256:384], kT[r, h // 2, 128:256], qT[r, h // 2, 128:256], True, True, inc=True)
                    tz[h] = p.stt(Z[:, h, :], b.t[:, 0:384], 0.125, const("sbmask"), ALU.mult, ALU.add, [tok, t_const])
                    b.free = [tz[h]]

                def stay(n):
                    z = [tz[h] for h in range(4 * n, 4 * n + 4)]
                    x = p.stt(E[:, :, :].rearrange("p h n -> p (h n)"), Z[:, 4 * n:4 * n + 4, :].rearrange("p h n -> p (h n)"), -1.0,
                              Z[:, 4 * n:4 * n + 4, :].rearrange("p h n -> p (h n)"), ALU.mult, ALU.min, [z, tsp.get(n - 1), turned[0]])
                    x = p.act(E[:, :, :], E[:, :, :], ACT.Exp, [x])
                    te[n] = p.act(E[:, :, :], E[:, :, :], ACT.Ln, [x], bias=1.0)

                def plus(n):
                    tsp[n] = p.stt(SP[:, :, :].rearrange("p h n -> p (h n)"), Z[:, 4 * n:4 * n + 4, :].rearrange("p h n -> p (h n)"), 0.0,
                                   E[:, :, :].rearrange("p h n -> p (h n)"), ALU.max, ALU.add, [te[n], tcum.get(4 * n - 1)])

                def rest(h):
                    b = scratch()
                    p.mm(b.t[:, 0:384], const("incl"), SP[:, h % 4, :], True, False, [tsp[h // 4], b.free, t_const])
                    tcum[h] = p.mm(b.t[:, 128:256], const("ones"), SP[:, h % 4, 256:384], False, True, inc=True)
                    tsub[h] = p.tt(Z[:, h, :], Z[:, h, :], b.t[:, 0:384], ALU.subtract, [tcum[h]])
                    b.free = [tsub[h]]

                def weights_of(n):
                    z = Z[:, 4 * n:4 * n + 4, :]
                    tw_[n] = p.act(z, z, ACT.Exp, [tsub[h] for h in range(4 * n, 4 * n + 4)])

                def weigh():
                    ob = pair()
                    for h in range(8):
                        c = slice(h * 64, h * 64 + 64)
                        p.mm(ob[0].t[:, c], Z[:, h, 0:128], V[:, 0, c], True, True,
                             [tw_[h // 4], ready["v", 0], ready["v", 1], ob[0].free, ob[1].free])
                        p.mm(ob[1].t[:, c], Z[:, h, 128:256], V[:, 0, c], True, False)
                        tok = p.mm(ob[1].t[:, c], Z[:, h, 256:384], V[:, 1, c], False, True, inc=True)
                    for t in range(2):
                        ready["o", t] = p.copy(XN[:, t, 0:512], ob[t].t[:, :], [tok, xn_used[0]])
                        ob[t].free = [ready["o", t]]
                    close(ob)

                def both(f, *hs):
                    return lambda: [f(h) for h in hs]

                got = {}

                def turn_out(c, key):
                    return [(t, lambda t=t: got.update(turn_piece(XN, c, t, key[t] if c else ready["o", t], OH, OL, None)))
                            for t in range(2)]

                parts = [both(logits, 0, 1), both(logits, 2, 3), both(stay, 0), both(logits, 4, 5), both(logits, 6, 7), None,
                         both(plus, 0), both(stay, 1), both(rest, 0, 1), both(rest, 2, 3), None, both(plus, 1),
                         both(weights_of, 0), both(rest, 4, 5), both(rest, 6, 7), both(weights_of, 1), None, weigh]

                def step(i):
                    if i in (10, 13, 15):
                        {10: sgu_norm, 13: lambda: spatial(0), 15: lambda: spatial(1)}[i]()
                    if i >= 18 and parts:
                        f = parts.pop(0)
                        if f:
                            f()

                x_used[0] = linear("sbg_in", lhs, evac, step)
                flush()
                for _ in others:
                    step(18)
                while parts:
                    step(18)
                flush()
                for _, f in turn_out(1, osg):
                    f()
                put_off(turn_out(0, None))
                norm_open()
                linear("sbg_out", lhs_of(OH, OL, got), add_x, tail=True)

        def mem_load(l, M):
            done = [x for x in p.last.values() if x]
            return [p.dma("sp", f"d_m{l}{t}", M[:, t, :], d["mem"][t * 128:(t + 1) * 128, :], done) for t in range(2)]

        def mem_norm(l, M, tm):
            gi, g, gt = gain()
            dep, sums = [], []
            for t in range(2):
                for c in range(2):
                    sums.append(square(c, M[:, t, c * 512:(c + 1) * 512], st[:, 2 + t + 2 * c:3 + t + 2 * c], [tm[t]]))
            a = p.tt(st[:, 2:4], st[:, 2:4], st[:, 4:6], ALU.add, sums)
            r = rstd_of(st[:, 2:4], 2, 1.0 / D, 1e-6, [a])
            for t in range(2):
                for c in range(2):
                    cols = slice(c * 512, (c + 1) * 512)
                    x = p.stt(M[:, t, cols], M[:, t, cols], st[:, 2 + t:3 + t], g[:, cols], ALU.mult, ALU.mult, [r, gt])
                dep.append(x)
            gain_done(gi, dep[1])

            def later():
                got = to_halves(lambda t, k: M[:, t, k * 128:(k + 1) * 128], 8, MH, ML, dep, mem.get("used"))
                mem["lhs"] = lhs_of(MH, ML, got)

            return later

        mem = {}

        def qk_turn(dst, src, k0, toks, got, key):
            b = scratch()
            for k in range(2):
                for t in range(2):
                    tok = p.tr(b.t[:, (2 * k + t) * 128:(2 * k + t + 1) * 128], src[:, t, k * 128:(k + 1) * 128],
                               ident, [toks[t], b.free], k == 1 and t == 1)
            got[key] = p.copy(dst[:, k0:k0 + 2, :], b.t[:, :].rearrange("p (k n) -> p k n", k=2), [tok])
            b.free = [got[key]]
            return tok

        def mem_keys(l, kT, V, q, s):
            kg, kgt = row(f"xk{l}", d["xmem_k_gain"][l], s)
            t_k, turned, vt = {}, {}, {}

            def evac(c, w, bs):
                toks, sums = [], []
                for t, b, tok in bs:
                    vt[c, t] = p.act(V[:, t, c * 256:(c + 1) * 256], b.t[:, 256:512], waits=[tok])
                    sums.append(p.act(q[:, c % 2, t, :], b.t[:, 0:256], ACT.Square, [tok, turned.get(c - 2)],
                                      accum=st[:, 6 + t:7 + t]))
                r = rstd_of(st[:, 6:8], 2, 1.0 / 256, 1e-6, [sums, vt[c, 1]])
                for t, b, tok in bs:
                    toks.append(p.stt(q[:, c % 2, t, :], b.t[:, 0:256], st[:, 6 + t:7 + t], kg, ALU.mult, ALU.mult, [r, kgt]))
                    b.free = [toks[t], vt[c, t]]
                mem["used"] = p.last["pe"]

                def later():
                    turned[c] = qk_turn(kT, q[:, c % 2, :, :], 2 * c, toks, t_k, c)

                return later

            return steps(f"x_kv{l}", mem["lhs"], evac, late=2), t_k, vt, turned

        def mem_attention(l, kT, V, q, t_k, vt, turned):
            root_tok, lhs = norm_close()
            p.fence()
            with ExitStack() as s:
                qT = sb(f"xm_qT{l}", [128, 8, 256], F32, s)
                OH = sb(f"xm_oh{l}", [128, 8, 256], F32R, s)
                OL = sb(f"xm_ol{l}", [128, 8, 256], F32R, s)
                qg, qgt = row(f"xq{l}", d["xmem_q_gain"][l], s)
                t_q = {}

                def evac(c, w, bs):
                    toks = {}
                    for t, b, tok in bs:
                        sums = [p.act(q[:, j, t, :], b.t[:, j * 256:(j + 1) * 256], ACT.Square,
                                      [tok, turned.get(2), turned.get(3), turned.get(("q", c - 1, j)), root_tok],
                                      scale=root[:, t:t + 1], accum=st[:, 8 + 2 * t + j:9 + 2 * t + j]) for j in range(2)]
                        r = rstd_of(st[:, 8 + 2 * t:10 + 2 * t], 2, 1.0 / 256, 1e-6, sums)
                        r = p.ts(st[:, 8 + 2 * t:10 + 2 * t], st[:, 8 + 2 * t:10 + 2 * t], root[:, t:t + 1], ALU.mult, waits=[r])
                        for j in range(2):
                            toks[j, t] = p.stt(q[:, j, t, :], b.t[:, j * 256:(j + 1) * 256], st[:, 8 + 2 * t + j:9 + 2 * t + j], qg,
                                               ALU.mult, ALU.mult, [r, qgt])
                        b.free = [toks[0, t], toks[1, t]]

                    def later():
                        for j in range(2):
                            turned["q", c, j] = qk_turn(qT, q[:, j, :, :], 4 * c + 2 * j, [toks[j, 0], toks[j, 1]], t_q, 2 * c + j)

                    return later

                def scores(h, i):
                    return [(qT[:, 2 * h + k, i * 128:(i + 1) * 128], kT[:, 2 * h + k, :]) for k in range(2)]

                got = {}
                heads = attend_steps(f"xm{l}", 4, 256, [(0, 0, 256), (1, 256, 256)], scores,
                             lambda h, j: V[:, j, h * 256:(h + 1) * 256], 0.0625, None, None,
                             lambda t, h, n: XN[:, t, h * 256:(h + n) * 256],
                             lambda h: [t_k[h], t_q[h]], list(vt.values()), OH, OL, got)
                x_used[0] = linear(f"x_q{l}", lhs, evac, lambda i: next(heads) if i in (6, 7) else None)
                flush()
                for _ in heads:
                    pass
                norm_open()
                linear(f"x_o{l}", lhs_of(OH, OL, got), add_x, tail=True)

        trig_sn = sb("trig_sn", [128, 2, 40])
        trig_cs = sb("trig_cs", [128, 2, 40])

        def trig_tables(s):
            pi = sb("tr_pi", [128, 4], I32, s)
            pf = sb("tr_pf", [128, 4], F32, s)
            ang = sb("tr_an", [128, 2, 40], F32, s)
            tmp = sb("tr_at", [128, 2, 40], F32, s)
            dma = [p.dma("sp", "d_pos1", pi[:, 0:2], d["positions"]), p.dma("sp", "d_pos2", pi[:, 2:4], d["positions_2"])]
            lo, hi = cat["inv1"][0], cat["invi"][1]

            def work():
                a = p.copy(pf[:, :], pi[:, :], dma)
                toks = []
                for t in range(2):
                    toks.append(p.ts(ang[:, t, 0:16], C[:, lo:lo + 16], pf[:, t:t + 1], ALU.mult, waits=[a, t_const]))
                    toks.append(p.ts(ang[:, t, 16:40], C[:, lo + 16:hi], pf[:, 2 + t:3 + t], ALU.mult, waits=[a, t_const]))
                trig_tok[0] = sincos(trig_sn[:, :, :], trig_cs[:, :, :], ang[:, :, :], tmp[:, :, :], toks)

            return work

        trig_tok = [None]

        def mla_mixer():
            root_tok, lhs = norm_close()
            p.fence()
            with ExitStack() as s:
                qT = sb("ml_qT", [96, 16, 256], F32, s)
                kT = sb("ml_kT", [96, 16, 256], F32, s)
                V = sb("ml_v", [128, 2, D], F32, s)
                rq = sb("ml_rq", [128, 2, 16], F32, s)
                rk = sb("ml_rk", [128, 2, 16], F32, s)
                with ExitStack() as s2:
                    Q = sb("ml_q", [128, 2, 16, 96], F32, s2)
                    K = sb("ml_k", [128, 2, 16, 96], F32, s2)
                    KR = sb("ml_kr", [128, 2, 32], F32, s2)
                    KE = sb("ml_ke", [128, 2, 32], F32, s2)
                    sn, cs, t_ang = trig_sn[:, :, 0:16], trig_cs[:, :, 0:16], trig_tok[0]
                    qg, qgt = row("ql", d["mla_q_lora_gain"][0], s2)
                    kg, kgt = row("kl", d["mla_kv_lora_gain"][0], s2)
                    gq, gqt = row("mq", d["mla_q_gain"][0], s2)
                    gk, gkt = row("mk", d["mla_k_gain"][0], s2)
                    tc = {}

                    def lora(b, t, lo, hi, g, gt, col, n, waits):
                        s_ = st[:, col:col + 1]
                        a = p.act(XN[:, t, lo:hi], b.t[:, 0:n], ACT.Square, [waits, xn_used[0], root_tok],
                                  scale=root[:, t:t + 1], accum=s_)
                        r = rstd_of(s_, 1, 1.0 / n, 1e-6, [a])
                        r = p.tt(s_, s_, root[:, t:t + 1], ALU.mult, [r])
                        return p.stt(XN[:, t, lo:hi], b.t[:, 0:n], s_, g, ALU.mult, ALU.mult, [r, gt, a])

                    def evac(c, w, bs):
                        for t, b, tok in bs:
                            if c == 0:
                                tc["q", t] = lora(b, t, 0, 512, qg, qgt, 12 + t, 512, [tok])
                                b.free = [tc["q", t]]
                            else:
                                tc["r", t] = p.act(KR[:, t, :], b.t[:, 256:288], waits=[tok, root_tok], scale=root[:, t:t + 1])
                                tc["k", t] = lora(b, t, 512, 768, kg, kgt, 14 + t, 256, [tok, tc["r", t]])
                                b.free = [tc["k", t], tc["r", t]]

                    def turn_e(t):
                        n2 = p.tt(KR[:, t, :], KR[:, t, :], gk[:, 64:96], ALU.mult, [done["ks"], gkt], "pool")
                        x1, x2, c_, s_ = KR[:, t, 0:16], KR[:, t, 16:32], cs[:, t, :], sn[:, t, :]
                        w = [n2, t_ang, xn_used[0], done.get(("e", t - 1))]
                        tm = [XN[:, 1, 768 + 16 * j:784 + 16 * j] for j in range(4)]
                        ab = [p.tt(tm[0], x1, c_, ALU.mult, w, "pool"), p.tt(tm[1], x2, s_, ALU.mult, w, "pool"),
                              p.tt(tm[2], x1, s_, ALU.mult, w, "pool"), p.tt(tm[3], x2, c_, ALU.mult, w, "pool")]
                        done["e", t] = [p.tt(KE[:, t, 0:16], tm[0], tm[1], ALU.subtract, ab, "pool"),
                                        p.tt(KE[:, t, 16:32], tm[2], tm[3], ALU.add, ab, "pool")]

                    x_used[0] = linear("mla_in", lhs, evac)
                    gg = gk[:, 0:64]
                    done = {"g": p.tt(gg, gq[:, 0:64], gg, ALU.mult, [gqt, gkt])}
                    done["ks"] = [p.act(KE[:, t, :], KR[:, t, :], ACT.Square, [tc["r", t]], accum=st[:, 16 + t:17 + t]) for t in range(2)]
                    for t in range(2):
                        turn_e(t)
                    fill(4)
                    got = to_halves(lambda t, k: XN[:, t, k * 128:(k + 1) * 128], 6, XH, XL,
                                    [[tc["q", t], tc["k", t]] for t in range(2)], x_used[0])
                    xn_used[0] = p.last["pe"]
                    tq, tk, tv, sq, sk = {}, {}, {}, {}, {}
                    free = {}

                    def sums(b, dst, t, heads, n, tok, key):
                        v = junk[:, t, 0:heads * n]
                        a = p.act(v, b.t[:, 0:heads * n], ACT.Square, [tok, free.get(t), junk_tok[t]])
                        junk_tok[t] = free[t] = p.reduce(dst, v.rearrange("p (h n) -> p h n", h=heads), ALU.add, [a])
                        return free[t]

                    def evac_q(c, w, bs):
                        for t, b, tok in bs:
                            sq[c, t] = sums(b, rq[:, t, 4 * c:4 * c + 4], t, 4, 96, tok, c)
                            tq[c, t] = p.act(Q[:, t, 4 * c:4 * c + 4, :], b.t[:, 0:384].rearrange("p (h n) -> p h n", h=4),
                                             waits=[tok])
                            b.free = [tq[c, t]]
                            turn_q(c, t)

                    def turn_q(c, t):
                        e = ("pool", "dve")[t]
                        qr = Q[:, t, 4 * c:4 * c + 4, 64:96]
                        over4 = lambda m: m.unsqueeze(1).broadcast_to([128, 4, m.shape[1]])
                        tm = [XN[:, 0, 256 * t + 64 * j:256 * t + 64 * j + 64].rearrange("p (h n) -> p h n", h=4) for j in range(4)]
                        n2 = p.tt(qr, qr, over4(gq[:, 64:96]), ALU.mult, [tq[c, t], gqt], e)
                        x1, x2, c_, s_ = qr[:, :, 0:16], qr[:, :, 16:32], over4(cs[:, t, :]), over4(sn[:, t, :])
                        w = [n2, t_ang, done.get(("q", c - 1, t)), xn_used[0]]
                        ab = [p.tt(tm[0], x1, c_, ALU.mult, w, e), p.tt(tm[1], x2, s_, ALU.mult, w, e),
                              p.tt(tm[2], x1, s_, ALU.mult, w, e), p.tt(tm[3], x2, c_, ALU.mult, w, e)]
                        done["q", c, t] = [p.tt(x1, tm[0], tm[1], ALU.subtract, ab, e),
                                           p.tt(x2, tm[2], tm[3], ALU.add, ab, e)]

                    def evac_kv(c, w, bs):
                        for t, b, tok in bs:
                            if c < 2:
                                sk[c, t] = sums(b, rk[:, t, 8 * c:8 * c + 8], t, 8, 64, tok, c)
                                tk[c, t] = p.act(K[:, t, 8 * c:8 * c + 8, 0:64], b.t[:, :].rearrange("p (h n) -> p h n", h=8),
                                                 waits=[tok])
                                b.free = [tk[c, t]]
                            else:
                                tv[c, t] = p.act(V[:, t, (c - 2) * 512:(c - 1) * 512], b.t[:, :], waits=[tok])
                                b.free = [tv[c, t]]

                    def over_heads(m):
                        return m.unsqueeze(1).broadcast_to([128, 16, m.shape[1]])

                    linear("mla_uq", lhs_of(XH, XL, got), evac_q)
                    def q_root():
                        r = rstd_of(rq[:, :, :], 32, 1.0 / 96, 1e-6, list(sq.values()))
                        r = p.ts(rq[:, :, :], rq[:, :, :], float(96.0 ** -0.5), ALU.mult, waits=[r])
                        done["rq"] = r

                    def norm_k(c, t, e):
                        h = slice(8 * c, 8 * c + 8)
                        r, kn = rk[:, t, h], K[:, t, h, 0:64]
                        over8 = lambda m: m.unsqueeze(1).broadcast_to([128, 8, m.shape[1]])
                        row8 = lambda n: r.unsqueeze(2).broadcast_to([128, 8, n])
                        n1 = p.tt(kn, kn, row8(64), ALU.mult, [done["rk", c], tk[c, t]], e)
                        n1 = p.tt(kn, kn, over8(gg), ALU.mult, [n1, done["g"]], e)
                        n2 = p.tt(K[:, t, h, 64:96], over8(KE[:, t, :]), row8(32), ALU.mult, [done["rk", c], done["e", t]], e)
                        done["k", c, t] = [n1, n2]

                    def root_k(c):
                        h = slice(8 * c, 8 * c + 8)
                        a = [p.ts(rk[:, t, h], rk[:, t, h], st[:, 16 + t:17 + t], ALU.add, waits=[sk[c, t], done["ks"]]) for t in range(2)]
                        done["rk", c] = rstd_of(rk[:, :, h], 16, 1.0 / 96, 1e-6, a)

                    def keys(i):
                        if i == 0:
                            q_root()
                        if i in (1, 2):
                            root_k(i - 1)
                            norm_k(i - 1, 0, "dve")
                            norm_k(i - 1, 1, "dve")

                    x_used[0] = linear("mla_ukv", lhs_of(XH, XL, {(k, t): got[k + 4, t] for k in range(2) for t in range(2)}, 4), evac_kv, keys)
                    turned = []

                    def turn_heads(src, dst, t, tok):
                        for g in range(4):
                            b = scratch()
                            for j in range(4):
                                x = p.tr(b.t[0:96, j * 128:(j + 1) * 128], src[:, t, 4 * g + j, :], ident, [tok, b.free], j == 3)
                            o = dst[:, 4 * g:4 * g + 4, t * 128:(t + 1) * 128]
                            v = b.t[0:96, :].rearrange("p (h n) -> p h n", h=4)
                            turned.append(p.act(o, v, waits=[x]) if g % 2 or dst is qT else p.copy(o, v, [x]))
                            b.free = [turned[-1]]

                    fill(1)
                    for t in range(2):
                        turn_heads(Q, qT, t, [done["q", c, t] for c in range(4)])
                    for t in range(2):
                        turn_heads(K, kT, t, [done["k", 0, t], done["k", 1, t]])
                p.fence()
                OH = sb("ml_oh", [128, 8, 256], F32R, s)
                OL = sb("ml_ol", [128, 8, 256], F32R, s)

                xn_used[0] = [xn_used[0], done["e", 1]]

                def scores(h, i):
                    return [(qT[:, h, i * 128:(i + 1) * 128], kT[:, h, 0:128 * (i + 1)])]

                got = {}
                attend("ml", 16, 64, [(0, 0, 128), (1, 128, 256)], scores,
                             lambda h, j: V[:, j, h * 64:(h + 1) * 64], lambda h, t: rq[:, t, h:h + 1], const("causal"),
                             [t_const, done["rq"]],
                             lambda t, h, n: XN[:, t, h * 64:(h + n) * 64], lambda h: turned, list(tv.values()), OH, OL, got,
                             during=lambda i: fill(1, True) if i % 2 == 0 else None)
                fill(16)
                norm_open()
                linear("mla_out", lhs_of(OH, OL, got), add_x, tail=True)

        def s5_tables(s):
            sat, _ = small_at()
            P = sb("s5_p", [128, 48], F32, s)
            T = sb("s5_T", [128, 2, 16, 256], F32, s)
            names = ["dt", "mag", "th", "tm", "sn", "cs", "abr", "abi", "den", "fre", "fim", "t1"]
            v = {n: sb("s5_" + n, [128, 16], F32, s)[:, :] for n in names}
            tmp = sb("s5_tt", [128, 8, 128], F32, s)
            ts_ = p.dma("sp", "d_s5p", P[:, :], d["small"][:, sat["lre"][0]:sat["ldt"][1]], [x for x in p.last.values() if x])
            S1 = sb("ab_s1", [128, 20], F32, s)
            S2 = sb("ab_s2", [128, 2048], F32, s)
            ncr = sb("ab_ncr", [128, 512], F32, s)
            nci = sb("ab_nci", [128, 512], F32, s)
            ct = sb("ab_ct", [128, 512], F32, s)
            done = [x for x in p.last.values() if x]
            tc = [p.dma("sp", "d_ab1", S1[:, :], d["small"][:, sat["convw"][0]:sat["bglu"][1]], done),
                  p.dma("sp", "d_ab2", S2[:, :], d["small"][:, sat["bre"][0]:sat["cim"][1]], done)]
            small = {n: S2[:, 512 * i:512 * i + 512] for i, n in enumerate(("bre", "bim", "cre", "cim"))}
            lre, lim, ldt = P[:, 0:16], P[:, 16:32], P[:, 32:48]
            got = {"mag": v["mag"], "T": T, "S1": S1, "small": small, "ts": tc, "ncr": ncr, "nci": nci, "tmp": tmp}

            def params():
                a = p.act(v["dt"], ldt, ACT.Exp, [ts_])
                l = p.ts(lre, lre, -1e-4, ALU.min, waits=[ts_])
                m = p.tt(v["mag"], lre, v["dt"], ALU.mult, [a, l])
                m = p.act(v["mag"], v["mag"], ACT.Exp, [m])
                t = p.tt(v["th"], lim, v["dt"], ALU.mult, [a])
                sc = sincos(v["sn"], v["cs"], v["th"], v["tm"], [t])
                r = p.tt(v["abr"], v["mag"], v["cs"], ALU.mult, [m, sc])
                r = p.ts(v["abr"], v["abr"], 1.0, ALU.subtract, waits=[r])
                i = p.tt(v["abi"], v["mag"], v["sn"], ALU.mult, [m, sc])
                e = p.tt(v["den"], lre, lre, ALU.mult, [l])
                f = p.tt(v["t1"], lim, lim, ALU.mult, [ts_])
                e = p.tt(v["den"], v["den"], v["t1"], ALU.add, [e, f])
                e = p.recip(v["den"], v["den"], [e])
                a1 = p.tt(v["fre"], v["abr"], lre, ALU.mult, [r, l])
                a2 = p.tt(v["t1"], v["abi"], lim, ALU.mult, [i, e])
                a1 = p.tt(v["fre"], v["fre"], v["t1"], ALU.add, [a1, a2])
                a1 = p.tt(v["fre"], v["fre"], v["den"], ALU.mult, [a1, e])
                a2 = p.tt(v["fim"], v["abi"], lre, ALU.mult, [i, l])
                a3 = p.tt(v["t1"], v["abr"], lim, ALU.mult, [r, a1])
                a2 = p.tt(v["fim"], v["fim"], v["t1"], ALU.subtract, [a2, a3])
                a2 = p.tt(v["fim"], v["fim"], v["den"], ALU.mult, [a2, e])
                got["tok"] = [m, sc, a1, a2]

            def phases():
                a = p.copy(T[:, 0, :, 0], v["cs"], got["tok"], "pool")
                b = p.copy(T[:, 1, :, 0], v["sn"], got["tok"], "pool")
                for half in range(2):
                    r = slice(8 * half, 8 * half + 8)
                    x = [a, b, p.last["pool"]]
                    for k in range(8):
                        m = 1 << k
                        R, I = T[:, 0, r, 0:m], T[:, 1, r, 0:m]
                        Br = T[:, 0, r, m - 1:m].broadcast_to([128, 8, m])
                        Bi = T[:, 1, r, m - 1:m].broadcast_to([128, 8, m])
                        oR, oI, tm = T[:, 0, r, m:2 * m], T[:, 1, r, m:2 * m], tmp[:, :, 0:m]
                        y1 = p.tt(oR, R, Br, ALU.mult, x, "pool")
                        y2 = p.tt(tm, I, Bi, ALU.mult, x, "pool")
                        y1 = p.tt(oR, oR, tm, ALU.subtract, [y1, y2], "pool")
                        y2 = p.tt(oI, R, Bi, ALU.mult, x, "pool")
                        y3 = p.tt(tm, I, Br, ALU.mult, [x, y1], "pool")
                        y2 = p.tt(oI, oI, tm, ALU.add, [y2, y3], "pool")
                        x = [y1, y2]
                    got["t", half] = x

            def factors():
                g = lambda m: m.rearrange("p (i c) -> p i c", i=16)
                fr = v["fre"].unsqueeze(2).broadcast_to([128, 16, 32])
                fi = v["fim"].unsqueeze(2).broadcast_to([128, 16, 32])
                cr, ci = small["cre"], small["cim"]
                w = [got["tok"], tc]
                x1 = p.tt(g(nci[:, :]), g(cr), fi, ALU.mult, w, "pool")
                x2 = p.tt(g(ct[:, :]), g(ci), fr, ALU.mult, w, "pool")
                x1 = p.tt(nci[:, :], nci[:, :], ct[:, :], ALU.add, [x1, x2], "pool")
                got["i"] = x1
                x3 = p.tt(g(cr), g(cr), fr, ALU.mult, [x1], "pool")
                x4 = p.tt(g(ct[:, :]), g(ci), fi, ALU.mult, [x1, w], "pool")
                x3 = p.tt(cr, cr, ct[:, :], ALU.subtract, [x3, x4], "pool")
                got["last"] = cr, x3

            def negate():
                cr, x3 = got["last"]
                got["c"] = [x3, p.ts(ncr[:, :], cr, -1.0, ALU.mult, waits=[x3]),
                            p.ts(nci[:, :], nci[:, :], -1.0, ALU.mult, waits=[got["i"]])]

            return got, lambda i: {6: params, 12: factors, 16: negate, 18: phases}.get(i, lambda: None)()

        def ab_mixer(s5, lhs):
            p.fence()
            with ExitStack() as s:
                S1, small, ts_, T, mag = s5["S1"], s5["small"], s5["ts"], s5["T"], s5["mag"]
                cw, dskip, bglu = S1[:, 0:12].rearrange("p (k j) -> p k j", k=4), S1[:, 12:16], S1[:, 16:20]
                uT = sb("ab_uT", [128, 4, 256], F32, s)
                gT = sb("ab_gT", [128, 4, 256], F32, s)
                cT = sb("ab_cT", [128, 4, 258], F32, s)
                Z = s5["tmp"][:, :, :].rearrange("p a b -> p (a b)").rearrange("p (k n) -> p k n", k=4)
                H = sb("ab_h", [128, 2, 512], F32, s)
                B = sb("ab_b", [128, 2, 512], F32, s)
                nb = 3
                A_ = sb("ab_A", [128, nb, 2, 256], F32, s)
                B_ = sb("ab_B", [128, nb, 2, 256], F32, s)
                C_ = sb("ab_C", [128, nb, 2, 256], F32, s)
                D_ = sb("ab_D", [128, nb, 2, 256], F32, s)
                ZH = sb("ab_zh", [128, 4, 256], F32R, s)
                ZL = sb("ab_zl", [128, 4, 256], F32R, s)
                W_ = B_
                z0 = p.memset(cT[:, :, 0:2], 0.0)
                cre, ncre, ncim, t_c = small["cre"], s5["ncr"][:, :], s5["nci"][:, :], s5["c"]
                ready, turned = {}, {}
                spare[:] = [4, 5]

                def turn_all(src, dst, key, toks, off=0):
                    for t in range(2):
                        b = scratch()
                        for k in range(4):
                            tok = p.tr(b.t[:, k * 128:(k + 1) * 128], src[:, t, k * 128:(k + 1) * 128], ident,
                                       [toks[t], b.free], k == 3)
                        ready[key, t] = p.act(dst[:, :, off + t * 128:off + (t + 1) * 128],
                                              b.t[:, :].rearrange("p (k n) -> p k n", k=4), waits=[tok, z0])
                        b.free = [ready[key, t]]
                    turned[key] = tok

                hold = {}

                def evac(c, w, bs):
                    toks = []
                    for t, b, tok in bs:
                        if c in (0, 3):
                            toks.append(p.act(B[:, t, :], b.t[:, :], waits=[tok, turned.get("u")]))
                        elif c == 1:
                            toks.append(p.act(H[:, t, :], b.t[:, :], waits=[tok]))
                        else:
                            toks.append(p.tt(H[:, t, :], b.t[:, :], H[:, t, :], ALU.mult, [tok, hold[t]]))
                        hold[t] = toks[t]
                        b.free = [toks[t]]
                    if c == 0:
                        return lambda: turn_all(B, uT, "u", toks)
                    if c == 2:
                        return lambda: turn_all(H, cT, "c", toks, 2)
                    if c == 3:
                        return lambda: turn_all(B, gT, "g", toks)

                t_w, t_y, t_cd, zt = {}, {}, {}, {}
                ya, got = {}, {}

                def state(i):
                    r = slice(32 * (i % 4), 32 * (i % 4) + 32)
                    b = scratch()
                    for j, nm in enumerate(("bre", "bim")):
                        l = small[nm].rearrange("p (k n) -> p k n", k=4)[r, i // 4, :]
                        tok = p.mm(b.t[:, j * 256:(j + 1) * 256], l, uT[r, i // 4, :], True, True,
                                   [ready["u", 0], ready["u", 1], ts_, b.free], j == 1)
                    Tr = T[:, 0, i, :].unsqueeze(1).broadcast_to([128, 2, 256])
                    v = b.t[:, :].rearrange("p (j n) -> p j n", j=2)
                    n = i % nb
                    x = p.tt(A_[:, n, :, :], v, Tr, ALU.mult, [tok, s5["t", i // 8], t_w.get(i - nb)])
                    y1 = p.tt(B_[:, n, 0, :], b.t[:, 256:512], T[:, 1, i, :], ALU.mult, [tok, t_cd.get(i - nb)])
                    y2 = p.tt(B_[:, n, 1, :], b.t[:, 0:256], T[:, 1, i, :], ALU.mult, [tok, t_cd.get(i - nb)])
                    b.free = [x, y1, y2]
                    x1 = p.tt(A_[:, n, 0, :], A_[:, n, 0, :], B_[:, n, 0, :], ALU.add, [x, y1])
                    x2 = p.tt(A_[:, n, 1, :], A_[:, n, 1, :], B_[:, n, 1, :], ALU.subtract, [x, y2], "pool")
                    for j, x in ((0, x1), (1, x2)):
                        t_w[i] = p.emit("dve", lambda e, j=j: e.tensor_tensor_scan(
                            W_[:, n, j, :], mag[:, i:i + 1].broadcast_to([128, 256]), A_[:, n, j, :], 0.0, ALU.mult, ALU.add),
                            [x, t_cd.get(i - nb)])
                    Ti = T[:, 1, i, :].unsqueeze(1).broadcast_to([128, 2, 256])
                    p.tt(C_[:, n, :, :], W_[:, n, :, :], Tr, ALU.mult, [t_w[i], t_y.get(i - nb)], "pool")
                    t_cd[i] = p.tt(D_[:, n, :, :], W_[:, n, :, :], Ti, ALU.mult, [t_w[i], t_y.get(i - nb)], "pool")

                def outputs(i):
                    yb = banks[6 + i // 4 % 2]
                    n, cc = i % nb, slice(32 * i, 32 * i + 32)
                    o = yb.t[32 * (i % 4):32 * (i % 4) + 32, 0:256]
                    p.mm(o, cre[:, cc], C_[:, n, 0, :], True, False, [t_cd[i], t_c, yb.free])
                    p.mm(o, ncim[:, cc], C_[:, n, 1, :], False, False)
                    p.mm(o, ncim[:, cc], D_[:, n, 0, :], False, False)
                    t_y[i] = p.mm(o, ncre[:, cc], D_[:, n, 1, :], False, True, inc=True)
                    if i % 4 == 3:
                        k = i // 4
                        zt["y", k] = p.stt(Z[:, k, :], uT[:, k, :], dskip[:, k:k + 1], yb.t[:, 0:256], ALU.mult, ALU.add,
                                           [t_y[i], ts_])
                        yb.free = [zt["y", k]]

                queue = [(f, i) for i in range(18) for f in (outputs, state)]

                def recurrence(n):
                    for f, i in queue[:2 * n]:
                        j = i if f is state else i - 2
                        if 0 <= j < 16:
                            f(j)
                    del queue[:2 * n]

                Y = [H[:, 0, 0:256], H[:, 0, 256:512]]

                def convolve(*tiles):
                    cd = [ready["c", 0], ready["c", 1], ts_, turned["c"]]
                    for k in tiles:
                        y = Y[k % 2]
                        a = p.ts(y, cT[:, k, 0:256], cw[:, k, 0:1], ALU.mult, waits=[cd, ya.get(k - 2)])
                        a = p.stt(y, cT[:, k, 1:257], cw[:, k, 1:2], y, ALU.mult, ALU.add, [a])
                        a = p.stt(y, cT[:, k, 2:258], cw[:, k, 2:3], y, ALU.mult, ALU.add, [a])
                        a = p.tt(y, y, gT[:, k, :], ALU.mult, [a, ready["g", 0], ready["g", 1]])
                        h = p.act(XH[:, k, :], y, waits=[a, x_used[0]])
                        ya[k] = p.tt(XL[:, k, :], y, XH[:, k, :].bitcast(F32), ALU.subtract, [h, x_used[0]])
                        got[k, 0] = got[k, 1] = ya[k]

                def gate(k):
                    zt["z", k] = p.act(Z[:, k, :], Z[:, k, :], ACT.Gelu_apprx_tanh, [zt["y", k]])
                    h = p.copy(ZH[:, k, :], Z[:, k, :], [zt["z", k]])
                    zt[k] = p.tt(ZL[:, k, :], Z[:, k, :], ZH[:, k, :].bitcast(F32), ALU.subtract, [h])

                x_used[0] = linear("ab_in", lhs, evac, lambda i: recurrence(1) if i >= 5 else None)
                flush()
                lhs = lhs_of(XH, XL, got)
                us = units_of(*shape_of["ab_out"])
                ob = [pair(), pair()]
                otok = [[None, None], [None, None]]

                def half(i):
                    c, k0, nk, w, _ = us[i]
                    u, hi, lo = weights("ab_out", i, nk, w)
                    for t in range(2):
                        unit(ob[c][t], lhs, 8, w, u, hi, lo, k0, nk, t, True, otok[c])
                    t_used[u] = otok[c][1]

                halves = [0, 1, 4, 5]
                gated = 0
                for k in range(4):
                    recurrence(1)
                    convolve(k)
                while queue:
                    recurrence(1)
                    if halves and len(queue) % 4 == 2:
                        half(halves.pop(0))
                    while ("y", gated) in zt and gated < 4:
                        gate(gated)
                        gated += 1
                while halves:
                    half(halves.pop(0))
                spare[:] = [4, 5]
                gb = [banks[6 + m // 2].t[:, (m % 2) * 256:(m % 2) * 256 + 256] for m in range(4)]
                parts = [(x[1], x[2], weights("glu", i, x[2], 512, 0)) for i, x in enumerate(units_of(4, [512]))]
                for m in range(4):
                    ms = slice(m * 128, (m + 1) * 128)
                    for k0, nk, (u, wh, wl) in parts:
                        for k in range(nk):
                            kt = k0 + k
                            p.mm(gb[m], wh[:, k, ms], ZH[:, kt, :], kt == 0, False,
                                 [zt[kt], t_split[u], banks[6].free, banks[7].free])
                            p.mm(gb[m], wh[:, k, ms], ZL[:, kt, :], False, False)
                            tok = p.mm(gb[m], wl[:, k, ms], ZH[:, kt, :], False, kt == 3, inc=k == nk - 1)
                        t_used[u] = tok
                    t_y["g", m] = tok
                for m in range(4):
                    sgm = W_[:, m % 2, m // 2, :]
                    a = p.act(sgm, gb[m], ACT.Sigmoid, [t_y["g", m], t_y["g", m | 1], t_cd[15], ts_], bias=bglu[:, m:m + 1])
                    banks[6 + m // 2].free = [a]
                    a = p.tt(sgm, sgm, Z[:, m, :], ALU.mult, [a, zt["z", m]])
                    h = p.act(XH[:, 4 + m, :], sgm, waits=[a, x_used[0]])
                    got[4 + m, 0] = got[4 + m, 1] = p.tt(XL[:, 4 + m, :], sgm, XH[:, 4 + m, :].bitcast(F32), ALU.subtract,
                                                         [h, x_used[0]])
                spare[:] = [4, 5, 6, 7]
                x_used[0] = None
                ln_open(XH, XL)
                half(2)
                half(3)
                put_off(full_mix(0, 512, [(t, ob[0][t], otok[0][t]) for t in range(2)]))
                close(ob[0])
                last = [(us[i], weights("ab_out", i, us[i][2], 512, 0)) for i in (6, 7)]
                for t in range(2):
                    for (c, k0, nk, w, _), (u, hi, lo) in last:
                        unit(ob[1][t], lhs, 8, w, u, hi, lo, k0, nk, t, t == 1, otok[1])
                        if t == 1:
                            t_used[u] = otok[1][1]
                            if order is not None:
                                split_to(u + SPLIT, "pool")
                    if t == 1:
                        flush(0)
                    put_off(full_mix(1, 512, [(t, ob[1][t], otok[1][t])]))
                close(ob[1])

        def dsa_mixer(lhs):
            p.fence()
            with ExitStack() as s:
                qT = sb("ds_qT", [128, 10, 256], F32, s)
                iT = sb("ds_iT", [128, 5, 256], F32, s)
                V = sb("ds_v", [128, 2, 256], F32, s)
                acc = sb("ds_acc", [128, 384], F32, s)
                work = sb("ds_work", [128, 384], F32, s)
                wi = sb("ds_wi", [128, 2, 8], F32, s)
                R = sb("ds_r", [128, 2, 384], F32, s)
                m8 = sb("ds_m8", [128, 2, 8], F32, s)
                Q = sb("ds_q", [128, 2, 1280], F32, s)
                I = sb("ds_i", [128, 2, 640], F32, s)
                tmi = sb("ds_tmi", [128, 4, 9, 8], F32, s)
                tmq = sb("ds_tmq", [128, 4, 4, 16], F32, s)
                tmi2 = sb("ds_tmp", [128, 4, 4, 16], F32, s)
                toks, ready, dq, tacc, racc, tops = {}, {}, {}, {}, {}, {}
                segs = [(0, 0, 128), (1, 128, 256)]
                csa, sna, csi, sni = trig_cs[:, :, 16:32], trig_sn[:, :, 16:32], trig_cs[:, :, 32:40], trig_sn[:, :, 32:40]

                def evac(c, w, bs):
                    for t, b, tok in bs:
                        if c == 0:
                            toks["qi", t] = p.act(I[:, t, 0:512], b.t[:, :], waits=[tok])
                        elif c == 1:
                            toks["ki", t] = p.act(I[:, t, 512:576], b.t[:, 0:64], waits=[tok])
                            toks["wi", t] = p.act(wi[:, t, :], b.t[:, 64:72], waits=[tok], scale=float(512.0 ** -0.5))
                        elif c == 2:
                            toks["k", t] = p.act(Q[:, t, 1024:1280], b.t[:, 0:256], waits=[tok])
                            toks["v", t] = p.act(V[:, t, :], b.t[:, 256:512], waits=[tok])
                        else:
                            toks["q", c - 3, t] = p.act(Q[:, t, (c - 3) * 512:(c - 2) * 512], b.t[:, :], waits=[tok])
                        b.free = [p.last["act"]]

                def turns(x, n, half, cs, sn, tmp, waits, e):
                    c_ = cs.unsqueeze(1).broadcast_to([128, n, half])
                    s_ = sn.unsqueeze(1).broadcast_to([128, n, half])
                    x1, x2 = x[:, :, 0:half], x[:, :, half:2 * half]
                    ab = [tmp[:, j, 0:n, :] for j in range(4)]
                    y = [p.tt(ab[0], x1, c_, ALU.mult, waits, e), p.tt(ab[1], x2, s_, ALU.mult, waits, e),
                         p.tt(ab[2], x1, s_, ALU.mult, waits, e), p.tt(ab[3], x2, c_, ALU.mult, waits, e)]
                    return [p.tt(x1, ab[0], ab[1], ALU.subtract, y, e), p.tt(x2, ab[2], ab[3], ALU.add, y, e)]

                def tiles(src, dst, t, g, n, tok, got):
                    b = scratch()
                    for k in range(n):
                        x = p.tr(b.t[:, k * 128:(k + 1) * 128], src[:, t, (g + k) * 128:(g + k + 1) * 128], ident,
                                 [tok, b.free], k == n - 1)
                    got[g, t] = p.act(dst[:, g:g + n, t * 128:(t + 1) * 128],
                                      b.t[:, 0:n * 128].rearrange("p (k n) -> p k n", k=n), waits=[x])
                    b.free = [got[g, t]]

                def index_turn():
                    for t in range(2):
                        it = I[:, t, 0:576].rearrange("p (h n) -> p h n", h=9)
                        o = turns(it, 9, 8, csi[:, t, :], sni[:, t, :], tmi,
                                  [toks["qi", t], toks["ki", t], trig_tok[0], tacc.get(("o", t - 1))], "dve")
                        tacc["o", t] = o
                        tacc["c", t] = p.copy(I[:, t, 576:640], I[:, t, 512:576], o)

                def index_tiles():
                    for t in range(2):
                        tiles(I, iT, t, 0, 4, tacc["c", t], ready)
                        tiles(I, iT, t, 4, 1, tacc["c", t], ready)

                def index_head(h):
                    b = scratch()
                    r = slice(64 * (h % 2), 64 * (h % 2) + 64)
                    for t, o, n in segs:
                        tok = p.mm(b.t[:, o:o + n], iT[r, h // 2, t * 128:(t + 1) * 128], iT[r, 4, 0:n], True, True,
                                   [list(ready.values()), b.free], t == 1)
                    a = p.act(R[:, h % 2, :], b.t[:, 0:384], ACT.Relu, [tok, racc.get(h - 2)])
                    b.free = [a]
                    for t, o, n in segs:
                        if h == 0:
                            tacc[t] = p.ts(acc[:, o:o + n], R[:, 0, o:o + n], wi[:, t, 0:1], ALU.mult, waits=[a, toks["wi", t]])
                        else:
                            tacc[t] = p.stt(acc[:, o:o + n], R[:, h % 2, o:o + n], wi[:, t, h:h + 1], acc[:, o:o + n],
                                            ALU.mult, ALU.add, [a, tacc[t]])
                    racc[h] = [tacc[0], tacc[1]]
                    if h == 7:
                        tops[0] = tops[1] = p.tt(work[:, :], acc[:, :], const("causal"), ALU.add, [tacc[0], tacc[1], t_const])

                def top(n):
                    for _ in range(n):
                        for t, o, w in segs:
                            x = p.emit("dve", lambda e, t=t, o=o, w=w: e.max(m8[:, t, :], work[:, o:o + w]), [tops[t]])
                            tops[t] = p.emit("dve", lambda e, t=t, o=o, w=w: e.match_replace(
                                out=work[:, o:o + w], in_to_replace=m8[:, t, :], in_values=work[:, o:o + w], imm_value=GONE), [x])

                def turn_heads(h0, n, key, dep, e, tmp):
                    for t in range(2):
                        x = Q[:, t, h0 * 128:(h0 + n) * 128].rearrange("p (h n) -> p h n", h=n)
                        toks[key, t] = turns(x, n, 16, csa[:, t, :], sna[:, t, :], tmp,
                                             [dep[t], trig_tok[0], toks.get((key, t - 1)), toks.get(("last", e))], e)
                        toks["last", e] = toks[key, t]

                def during(i):
                    if i == 6:
                        index_turn()
                    if i == 7:
                        index_tiles()
                    if 8 <= i < 12:
                        index_head(2 * i - 16)
                        index_head(2 * i - 15)
                    if i == 10:
                        turn_heads(8, 2, "K", [toks["k", t] for t in range(2)], "pool", tmq)
                    if 12 <= i < 16:
                        top(2)
                    if i == 13:
                        for t in range(2):
                            tiles(Q, qT, t, 8, 2, toks["K", t], dq)
                        turn_heads(0, 4, "Q0", [toks["q", 0, t] for t in range(2)], "pool", tmq)
                    if i == 15:
                        for t in range(2):
                            tiles(Q, qT, t, 0, 4, toks["Q0", t], dq)

                x_used[0] = linear("c_in", lhs, evac, during)
                flush()
                a = p.ts(acc[:, :], work[:, :], -2.0e38, ALU.is_le, 1.0, ALU.subtract, [tops[0], tops[1]])
                tsel = p.stt(acc[:, :], acc[:, :], -NEG, const("causal"), ALU.mult, ALU.add, [a])
                turn_heads(4, 4, "Q1", [toks["q", 1, t] for t in range(2)], "pool", tmi2)

                def scores(h, i):
                    return [(qT[:, h, i * 128:(i + 1) * 128], qT[:, 8 + h // 4, 0:128 * (i + 1)])]

                def second(i):
                    if i == 2:
                        for t in range(2):
                            tiles(Q, qT, t, 4, 4, toks["Q1", t], dq)
                    if i in (0, 1):
                        fill(1, True)

                got = {}
                attend("ds", 8, 128, segs, scores, lambda h, j: V[:, j, (h // 4) * 128:(h // 4 + 1) * 128],
                             128.0 ** -0.5, acc[:, :], tsel, lambda t, h, n: XN[:, t, h * 128:(h + n) * 128],
                             lambda h: [dq[8, 0], dq[8, 1], dq[h // 4 * 4, 0], dq[h // 4 * 4, 1]], [toks["v", 0], toks["v", 1]],
                             XH, XL, got, during=second)
                fill(2)
                ln_open(XH, XL)
                linear("c_out", lhs_of(XH, XL, got), full_mix, tail=True)

        def embedding(l, s):
            a0, b0 = small_at()[0][f"pt{l}"]
            PJ = sb(f"pl_j{l}", [128, 2, D], F32, s)
            PT = sb(f"pl_p{l}", [128, 2, 256], F32, s)
            PH = sb(f"pl_h{l}", [128, 2, 256], F32R, s)
            PL = sb(f"pl_l{l}", [128, 2, 256], F32R, s)
            tp = p.dma("sp", f"d_p{l}", PT[:, :, :], d["small"][:, a0:b0].rearrange("p (k n) -> p k n", k=2),
                       [x for x in p.last.values() if x])
            ph, tj = {}, {}

            def turn():
                h = p.act(PH[:, :, :], PT[:, :, :], waits=[tp])
                h = p.tt(PL[:, :, :], PT[:, :, :], PH[:, :, :].bitcast(F32), ALU.subtract, [h])
                for k in range(2):
                    ph[k, 0] = ph[k, 1] = h

            def evac(c, w, bs):
                for t, b, tok in bs:
                    tj[c, t] = p.act(PJ[:, t, c * 512:(c + 1) * 512], b.t[:, :], waits=[tok])
                    b.free = [tj[c, t]]

            return PJ, tj, turn, lambda: steps(f"ple_p{l}", lhs_of(PH, PL, ph), evac, hold=True)

        def last_part(l, lhs, ple, nxt):
            with ExitStack() as s:
                PJ, tj, turn, product = ple or embedding(l, s)
                EH = sb(f"pl_eh{l}", [128, 8, 256], F32R, s)
                EL = sb(f"pl_el{l}", [128, 8, 256], F32R, s)

                def halve(i):
                    if i == 12 and not ple:
                        turn()

                ffn(f"w13_{l}_1", f"w2_{l}_1", lhs, None, half_mix, lambda: ln_open(EH, EL), halve)
                lhs = ln_close()
                if not ple:
                    for _ in product():
                        pass

                def evac_g(c, w, bs):
                    cols = slice(c * 512, (c + 1) * 512)
                    out = []
                    for t, b, tok in bs:
                        a = p.act(XN[:, t, cols], b.t[:, :], ACT.Sigmoid, [tok, xn_used[0]])
                        b.free = [a]
                        a = p.tt(XN[:, t, cols], XN[:, t, cols], PJ[:, t, cols], ALU.mult, [a, tj[c, t]])
                        xt[t] = p.tt(X[:, t, cols], X[:, t, cols], XN[:, t, cols], ALU.add, [a, xt[t], x_turned[0]])
                        out.append(nxt(c, t, xt[t]))
                    return out if out[0] else None

                x_turned = [None]
                g_steps = steps(f"ple_g{l}", lhs, evac_g, True)
                for i, _ in enumerate(g_steps):
                    if i == 0:
                        x_turned[0] = p.last["pe"]

        norm_open()
        for t in range(2):
            for c in range(2):
                pending.append(norm_piece(c, t))
            flush(0)
            split_to(2 * t)
            split_to(2 * t + 1)
        with ExitStack() as block1:
            MH = sb("MH", [128, 8, 256], F32R, block1)
            ML = sb("ML", [128, 8, 256], F32R, block1)
            for l in range(2):
                root_tok, lhs = norm_close()
                with ExitStack() as s:
                    todo = []
                    M = sb(f"xm_m{l}", [128, 2, D], F32, s)
                    trig = trig_tables(s) if l == 0 else None

                    def memory(i):
                        if i == 2:
                            todo.append(mem_load(l, M))
                        if i == 4 and trig:
                            trig()
                        if i == 12:
                            todo.append(mem_norm(l, M, todo.pop()))
                        if i == 20:
                            todo.pop()()

                    ffn(f"gu_pre{l}", f"dn_pre{l}", lhs, root_tok, half_add, norm_open, memory)
                with ExitStack() as s:
                    kT = sb(f"xm_kT{l}", [128, 8, 256], F32, s)
                    V = sb(f"xm_v{l}", [128, 2, D], F32, s)
                    q = sb(f"xm_q{l}", [128, 2, 2, 256], F32, s)
                    p.fence()
                    it, t_k, vt, turned = mem_keys(l, kT, V, q, s)
                    if l == 0:
                        even_mixer(it)
                    else:
                        fillers.append(it)
                        mla_mixer()
                    mem_attention(l, kT, V, q, t_k, vt, turned)
                root_tok, lhs = norm_close()
                if l == 0:
                    ffn(f"gu_post{l}", f"dn_post{l}", lhs, root_tok, half_add, norm_open)
                else:
                    norm_last = lhs, root_tok
        lhs, root_tok = norm_last
        raw_got = {}

        def raw_piece(c, t, dep):
            def later():
                raw_got.update(turn_piece(X, c, t, dep, XH, XL, x_used[0]))

            return t, later

        def half_add_raw(c, w, bs):
            norm.clear()
            half_add(c, w, bs)
            return [raw_piece(c, t, xt[t]) for t, b, tok in bs]

        ffn("gu_post1", "dn_post1", lhs, root_tok, half_add_raw)

        t_out = []
        end = ctx.enter_context(ExitStack())

        def store(c, t, dep):
            cols = slice(c * 512, (c + 1) * 512)
            t_out.append(p.dma("sp", f"d_o{c}{t}", out[t * 128:(t + 1) * 128, cols], X[:, t, cols], [dep]))

        for l in range(2):
            with ExitStack() as s:
                if l == 0:
                    s5, tables = s5_tables(s)
                else:
                    ple = embedding(l, end)
                    tables = lambda i: ple[2]() if i == 12 else None
                ffn(f"w13_{l}_0", f"w2_{l}_0", lhs_of(XH, XL, raw_got), None, half_mix, lambda: ln_open(XH, XL), tables)
                if l == 0:
                    ab_mixer(s5, ln_close())
                else:
                    lhs = ln_close()
                    fillers.append(ple[3]())
                    dsa_mixer(lhs)
            raw_got = {}
            last_part(l, ln_close(), ple if l else None, store if l == 1 else raw_piece)
        flush()
        p.wait("sp", t_out)
        assert gain_now[0] == len(gains) and not fillers and not pending
        if order is None:
            return taken
        assert len(taken) == len(stream)

        block = ctx.enter_context(nc.Block())

        @block.sync
        def _(eng):
            for f in p.queue["sp"]:
                f(eng)

        @block.scalar
        def _(eng):
            for f in p.queue["act"]:
                f(eng)

        @block.vector
        def _(eng):
            for f in p.queue["dve"]:
                f(eng)

        @block.gpsimd
        def _(eng):
            for f in p.queue["pool"]:
                f(eng)

        @block.tensor
        def _(eng):
            for f in p.queue["pe"]:
                f(eng)


def interleave(a, b):
    k, n = a.shape
    return np.stack([a.reshape(k, n // 256, 256), b.reshape(k, n // 256, 256)], 2).reshape(k, 2 * n)


def lay_weights(v):
    m = {}
    for l in range(2):
        for k, n in (("pre", "ffn_pre"), ("post", "ffn_post")):
            gu = v[n + "_w_gu"][l]
            m[f"gu_{k}{l}"] = interleave(gu[:, :FF], gu[:, FF:])
            m[f"dn_{k}{l}"] = v[n + "_w_down"][l]
        m[f"x_kv{l}"], m[f"x_q{l}"], m[f"x_o{l}"] = v["xmem_wkv"][l], v["xmem_wq"][l], v["xmem_wo"][l]
        for j in range(2):
            m[f"w13_{l}_{j}"] = interleave(v["ffn_w1_2"][l, j], v["ffn_w3_2"][l, j])
            m[f"w2_{l}_{j}"] = v["ffn_w2_2"][l, j]
        m[f"ple_p{l}"], m[f"ple_g{l}"] = v["ple_w_proj_2"][l], v["ple_w_gate_2"][l]
    sbg = v["sbg_w_in"][0]
    m["sbg_in"], m["sbg_out"] = np.concatenate([sbg[:, 1536:2560], sbg[:, 0:1536]], 1), v["sbg_w_out"][0]
    m["mla_in"], m["mla_out"] = v["mla_w_in"][0], v["mla_w_out"][0]
    m["mla_uq"] = v["mla_w_uq"][0]
    ukv = v["mla_w_ukv"][0].reshape(256, 16, 128)
    m["mla_ukv"] = np.concatenate([ukv[:, :, :64].reshape(256, 1024), ukv[:, :, 64:].reshape(256, 1024)], 1)
    ab = v["ab_w_in_2"][0]
    m["ab_in"] = np.concatenate([ab[:, 1536:2048], ab[:, 0:512], ab[:, 1024:1536], ab[:, 512:1024]], 1)
    m["ab_out"], m["glu"] = v["ab_w_out_2"][0], v["s5_w_glu_2"][0]
    c = v["c_w_in_2"][0]
    m["c_in"], m["c_out"] = np.concatenate([c[:, 1536:2120], c[:, 1024:1536], c[:, 0:1024]], 1), v["c_w_out_2"][0]
    out = {}
    for name, kts, widths in layers():
        w = m[name].reshape(kts, 128, -1)
        flat = np.empty(w.size, w.dtype)
        o = 0
        for _, k, nk, width, col in units_of(kts, widths):
            n = nk * 128 * width
            flat[o:o + n].reshape(128, nk, width)[...] = w[k:k + nk, :, col:col + width].transpose(1, 0, 2)
            o += n
        out["w_" + name] = flat
    return out


def lay_small(v):
    f = np.float32
    p = {}
    p["sguw"] = v["sgu_w"][0].transpose(2, 0, 1).reshape(128, 1024)
    p["sgub"] = v["sgu_b"][0].T
    p["convw"] = v["conv_w_2"][0].T.reshape(4, 128, 3).transpose(1, 0, 2).reshape(128, 12)
    p["dskip"] = v["s5_d_2"][0].reshape(4, 128).T
    p["bglu"] = v["s5_b_glu_2"][0].reshape(4, 128).T
    p["lre"] = v["s5_lam_re_2"][0].reshape(16, 128).T
    p["lim"] = v["s5_lam_im_2"][0].reshape(16, 128).T
    p["ldt"] = np.repeat(v["s5_log_dt_2"][0], 64).reshape(16, 128).T
    for n in ("re", "im"):
        b = np.zeros((4, 4, 2, 16, 2, 64), f)
        c = np.zeros((2, 64, 16, 2, 16), f)
        src = v[f"s5_b_{n}_2"][0].reshape(4, 4, 2, 64, 16)
        cs = v[f"s5_c_{n}_2"][0].reshape(16, 2, 16, 64)
        for g in range(2):
            b[:, :, g, :, g, :] = src[:, :, g].transpose(0, 1, 3, 2)
            c[g, :, :, g, :] = cs[:, g].transpose(2, 0, 1)
        p["b" + n] = b.reshape(4, 128, 128).transpose(1, 0, 2).reshape(128, 512)
        p["c" + n] = c.reshape(128, 512)
    for l in range(2):
        p[f"pt{l}"] = v["p_2"][l, 0].T.reshape(2, 128, 256).transpose(1, 0, 2).reshape(128, 512)
    return np.concatenate([p[n].astype(f, copy=False) for n, _ in SMALL], 1)


GAINS = ["ffn_pre_norm", "mix_norm", "sgu_ln_gain", "sgu_ln_bias", "mla_q_lora_gain", "mla_kv_lora_gain",
         "mla_q_gain", "mla_k_gain", "xmem_mem_norm", "xmem_k_gain", "xmem_norm", "xmem_q_gain", "ffn_post_norm",
         "ln_g_2", "ln_b_2"]


def kernel(**inputs):
    import concourse.bacc as bacc
    from concourse.bass_utils import run_bass_kernel_spmd

    v = {k: np.asarray(a) for k, a in inputs.items()}
    arrays = lay_weights(v)
    arrays["small"] = lay_small(v)
    arrays["consts"] = consts()[0]
    arrays["x"], arrays["mem"] = v["x"][0], v["mem"][0]
    for n in ("positions", "positions_2"):
        arrays[n] = v[n].reshape(2, 128).T
    for n in GAINS:
        arrays[n] = v[n]
    arrays = {n: np.ascontiguousarray(a) for n, a in arrays.items()}
    nc = bacc.Bacc("TRN2", target_bir_lowering=False, num_devices=1)
    d = {n: nc.dram_tensor("in_" + n, a.shape, mybir.dt.from_np(a.dtype), kind="ExternalInput").ap()
         for n, a in arrays.items()}
    out = nc.dram_tensor("out", (256, D), F32, kind="ExternalOutput").ap()
    order = build(bacc.Bacc("TRN2", target_bir_lowering=False, num_devices=1), d, out)
    build(nc, d, out, order)
    r = run_bass_kernel_spmd(nc, [{"in_" + n: a for n, a in arrays.items()}], core_ids=[0])
    return r.results[0]["out"].reshape(1, 256, D)
```
